# Optimizing a Trainium2 kernel written in Bass

```python
import jax, jax.numpy as jnp
from jax import lax
import numpy as np

D_MODEL = 1024
BATCH = 1
SEQ = 128
DEPTH = 1
DEC_BATCH = 1
DEC_SEQ = 2048
PAST_LEN = 256

GRID_W = 64
CONV_W = 256
CONV_K = 3
RWKV_HEADS = 8
RWKV_HEAD = 64
RWKV_W = RWKV_HEADS * RWKV_HEAD
LORA_DECAY = 64
LORA_A = 64
LORA_GATE = 128
N_DIR = 2
GN_EPS = 64e-5
SGU_GROUPS = 4
SGU_W = 256
SGU_GROUP_W = SGU_W // SGU_GROUPS
CHUNK = 128
N_BRANCH = 3
IN_SIZES = (CONV_W, CONV_W, CONV_W,
            RWKV_W, RWKV_W, RWKV_W,
            N_DIR * LORA_DECAY, N_DIR * LORA_A, LORA_GATE,
            SGU_W, SGU_W,
            N_BRANCH * D_MODEL)
IN_OFFSETS = tuple(np.cumsum(IN_SIZES)[:-1].tolist())
IN_COLS = sum(IN_SIZES)
N_EXPERTS = 16
N_GROUPS = 4
GROUP_SIZE = N_EXPERTS // N_GROUPS
TOP_K = 2
D_EXPERT = 256
MOE_BLOCK = 128
NORM_EPS = 1e-6
N_MOD = 6

kernel_name = "hybrid_flow_conv_rwkv7_sgu_moe_step"

def _normal(k, shape, scale):
    return scale * jax.random.normal(k, shape, jnp.float32)

def rms_norm(x, g):
    x32 = x.astype(jnp.float32)
    y = x32 * lax.rsqrt(jnp.mean(x32 * x32, axis=-1, keepdims=True) + NORM_EPS)
    return (y * g.astype(jnp.float32)).astype(x.dtype)

def layer_norm(x, g, b):
    x32 = x.astype(jnp.float32)
    mu = jnp.mean(x32, axis=-1, keepdims=True)
    var = jnp.mean(jnp.square(x32 - mu), axis=-1, keepdims=True)
    y = (x32 - mu) * lax.rsqrt(var + NORM_EPS)
    return (y * g.astype(jnp.float32) + b.astype(jnp.float32)).astype(x.dtype)

def short_conv3(x, w, grid):
    rows, cols = grid
    B, T, C = x.shape
    xp = jnp.pad(x.reshape(B, rows, cols, C), ((0, 0), (0, 0), (1, 1), (0, 0)))
    y = w[0] * xp[:, :, :-2] + w[1] * xp[:, :, 1:-1] + w[2] * xp[:, :, 2:]
    return y.reshape(B, T, C)

def rwkv7_bidirectional(r, k, v, w_lo, a_lo, g_lo, s0, w0, w2, a0, a2, g2, k_k, k_a, r_k, lnx_w, lnx_b):
    f32 = jnp.float32
    B, T, C = r.shape
    H, N = RWKV_HEADS, RWKV_HEAD
    r, k, v = r.astype(f32), k.astype(f32), v.astype(f32)
    w_logit = w0.astype(f32) + jnp.einsum('btdr,drc->btdc', jnp.tanh(w_lo.astype(f32)), w2.astype(f32))
    decay = jnp.exp(-jnp.exp(-jax.nn.softplus(-w_logit) - 0.5))
    a = jax.nn.sigmoid(a0.astype(f32) + jnp.einsum('btdr,drc->btdc', a_lo.astype(f32), a2.astype(f32)))
    g = jax.nn.sigmoid(g_lo.astype(f32)) @ g2.astype(f32)
    kk = (k * k_k.astype(f32)).reshape(B, T, H, N)
    kk = (kk / jnp.maximum(jnp.sqrt(jnp.sum(kk * kk, axis=-1, keepdims=True)), 1e-12)).reshape(B, T, C)
    k_dir = k[:, :, None, :] * (1.0 + (a - 1.0) * k_a.astype(f32))
    kka = kk[:, :, None, :] * a

    def to_scan(t):
        fwd, bwd = (t, t) if t.ndim == 3 else (t[:, :, 0], t[:, :, 1])
        st = jnp.stack([fwd, jnp.flip(bwd, axis=1)], axis=2).reshape(B, T, N_DIR, H, N)
        return jnp.moveaxis(st, 1, 0)

    xs = (to_scan(r), to_scan(decay), to_scan(k_dir), to_scan(v), to_scan(kk), to_scan(kka))

    def step(S, inp):
        r_t, w_t, k_t, v_t, kk_t, kka_t = inp
        sa = jnp.einsum('bdhvk,bdhk->bdhv', S, kk_t)
        S = (S * w_t[..., None, :] - sa[..., :, None] * kka_t[..., None, :]
             + v_t[..., :, None] * k_t[..., None, :])
        return S, jnp.einsum('bdhvk,bdhk->bdhv', S, r_t)

    s_final, ys = lax.scan(step, s0.astype(f32), xs)
    ys = jnp.moveaxis(ys, 0, 1)
    y = ys[:, :, 0] + jnp.flip(ys[:, :, 1], axis=1)
    mu = jnp.mean(y, axis=-1, keepdims=True)
    var = jnp.mean(jnp.square(y - mu), axis=-1, keepdims=True)
    yn = ((y - mu) * lax.rsqrt(var + GN_EPS)).reshape(B, T, C) * lnx_w.astype(f32) + lnx_b.astype(f32)
    rk = (r[:, :, None, :] * k_dir * r_k.astype(f32).reshape(C)).reshape(B, T, N_DIR, H, N).sum(-1).sum(2)
    bonus = (rk[..., None] * v.reshape(B, T, H, N)).reshape(B, T, C)
    return (yn + bonus) * g, s_final

def spatial_gating(u, v, ln_g, ln_b, ws, bs):
    B, T, _ = v.shape
    vn = layer_norm(v, ln_g, ln_b).reshape(B, T // CHUNK, CHUNK, SGU_GROUPS, SGU_GROUP_W)
    mixed = jnp.einsum('gpq,bnqgc->bnpgc', ws, vn) + jnp.swapaxes(bs, 0, 1)[:, :, None]
    return u * mixed.reshape(B, T, SGU_W)

def parallel_mixer(h, s0, grid, lp):
    B, T, _ = h.shape
    z = h @ lp['w_in']
    cb, cc, cx, r, k, v, w_lo, a_lo, g_lo, su, sv, gates = jnp.split(z, IN_OFFSETS, axis=-1)
    y_conv = cb * short_conv3(cc * cx, lp['conv_w'], grid)
    y_rwkv, s_final = rwkv7_bidirectional(
        r, k, v, w_lo.reshape(B, T, N_DIR, LORA_DECAY), a_lo.reshape(B, T, N_DIR, LORA_A), g_lo, s0,
        lp['rwkv_w0'], lp['rwkv_w2'], lp['rwkv_a0'], lp['rwkv_a2'], lp['rwkv_g2'],
        lp['rwkv_k_k'], lp['rwkv_k_a'], lp['rwkv_r_k'], lp['rwkv_lnx_w'], lp['rwkv_lnx_b'])
    y_sgu = spatial_gating(su, sv, lp['sgu_ln_g'], lp['sgu_ln_b'], lp['sgu_ws'], lp['sgu_bs'])
    g_conv, g_rwkv, g_sgu = jnp.split(jax.nn.sigmoid(gates.astype(jnp.float32)).astype(h.dtype), N_BRANCH, axis=-1)
    merged = (g_conv * (y_conv @ lp['proj_conv'])
              + g_rwkv * (y_rwkv.astype(h.dtype) @ lp['proj_rwkv'])
              + g_sgu * (y_sgu @ lp['proj_sgu']))
    return merged @ lp['w_out'], s_final

def routed_moe(h, router_w, router_b, w1, w3, w2):
    B, T, D = h.shape
    hf = h.reshape(B * T, D)
    n_tok = B * T
    scores = jax.nn.sigmoid(hf.astype(jnp.float32) @ router_w.astype(jnp.float32))
    biased = (scores + router_b.astype(jnp.float32)).reshape(n_tok, N_GROUPS, GROUP_SIZE)
    group_score = lax.top_k(biased, TOP_K)[0].sum(-1)
    g_sel = jnp.argmax(group_score, axis=-1).astype(jnp.int32)
    in_group = jnp.take_along_axis(biased, g_sel[:, None, None], axis=1)[:, 0]
    local = lax.top_k(in_group, TOP_K)[1].astype(jnp.int32)
    expert_idx = g_sel[:, None] * GROUP_SIZE + local
    gate = jnp.take_along_axis(scores, expert_idx, axis=1)
    gate = (gate / jnp.sum(gate, axis=-1, keepdims=True)).astype(h.dtype)

    nk = n_tok * TOP_K
    flat_e = expert_idx.reshape(nk)
    order = jnp.argsort(flat_e).astype(jnp.int32)
    sorted_e = flat_e[order]
    counts = jnp.bincount(flat_e, length=N_EXPERTS).astype(jnp.int32)
    padded = (counts + MOE_BLOCK - 1) // MOE_BLOCK * MOE_BLOCK
    pad_end = jnp.cumsum(padded)
    pad_start = pad_end - padded
    start = jnp.cumsum(counts) - counts
    dest = (pad_start[sorted_e] + jnp.arange(nk, dtype=jnp.int32) - start[sorted_e]).astype(jnp.int32)
    n_blocks = -(-nk // MOE_BLOCK) + N_EXPERTS
    n_rows = n_blocks * MOE_BLOCK
    src_token = jnp.full((n_rows,), n_tok, jnp.int32).at[dest].set(order // TOP_K)
    block_expert = jnp.minimum(
        jnp.searchsorted(pad_end, jnp.arange(n_blocks, dtype=jnp.int32) * MOE_BLOCK, side='right'),
        N_EXPERTS - 1)
    x_rows = jnp.concatenate([hf, jnp.zeros((1, D), hf.dtype)], axis=0)[src_token]
    x_rows = x_rows.reshape(n_blocks, MOE_BLOCK, D)

    def block_ffn(args):
        xb, e = args
        return (jax.nn.silu(xb @ w1[e]) * (xb @ w3[e])) @ w2[e]

    y_rows = lax.map(block_ffn, (x_rows, block_expert)).reshape(n_rows, D)
    dest_of_assign = jnp.zeros((nk,), jnp.int32).at[order].set(dest)
    y = jnp.sum(y_rows[dest_of_assign].reshape(n_tok, TOP_K, D) * gate[..., None], axis=1)
    return y.reshape(B, T, D)

def trunk_layer(x, mod, s0, grid, lp, router_w, router_b):
    sh1, sc1, ga1, sh2, sc2, ga2 = jnp.split(mod[:, None, :], N_MOD, axis=-1)
    h = rms_norm(x, lp['norm1_g']) * (1 + sc1) + sh1
    mix, s_final = parallel_mixer(h, s0, grid, lp)
    x = x + ga1 * mix
    h = rms_norm(x, lp['norm2_g']) * (1 + sc2) + sh2
    x = x + ga2 * routed_moe(h, router_w, router_b, lp['exp_w1'], lp['exp_w3'], lp['exp_w2'])
    return x, s_final

def setup_inputs(seed: int = 0) -> dict:
    key = jax.random.key(seed)
    ks = iter(jax.random.split(key, 40))
    L, D, H, N = DEPTH, D_MODEL, RWKV_HEADS, RWKV_HEAD
    return {
        'x_prompt': _normal(next(ks), (BATCH, SEQ, D), 1.0),
        'x_sample': _normal(next(ks), (DEC_BATCH, DEC_SEQ, D), 1.0),
        'state_rwkv': _normal(next(ks), (DEC_BATCH, L, N_DIR, H, N, N), 0.5),
        'c': _normal(next(ks), (DEC_BATCH, D), 1.0),
        'c_ctx': _normal(next(ks), (D,), 1.0),
        'norm1_g': 1.0 + _normal(next(ks), (L, D), 0.02),
        'norm2_g': 1.0 + _normal(next(ks), (L, D), 0.02),
        'final_g': 1.0 + _normal(next(ks), (D,), 0.02),
        'ada_w': _normal(next(ks), (L, D, N_MOD * D), 0.5 * D ** -0.5),
        'ada_b': _normal(next(ks), (L, N_MOD * D), 0.02),
        'w_in': _normal(next(ks), (L, D, IN_COLS), D ** -0.5),
        'conv_w': _normal(next(ks), (L, CONV_K, CONV_W), CONV_K ** -0.5),
        'rwkv_w0': _normal(next(ks), (L, N_DIR, RWKV_W), 0.5),
        'rwkv_w2': _normal(next(ks), (L, N_DIR, LORA_DECAY, RWKV_W), 0.5 * LORA_DECAY ** -0.5),
        'rwkv_a0': _normal(next(ks), (L, N_DIR, RWKV_W), 0.1),
        'rwkv_a2': _normal(next(ks), (L, N_DIR, LORA_A, RWKV_W), 0.5 * LORA_A ** -0.5),
        'rwkv_g2': _normal(next(ks), (L, LORA_GATE, RWKV_W), LORA_GATE ** -0.5),
        'rwkv_k_k': 1.0 + _normal(next(ks), (L, RWKV_W), 0.1),
        'rwkv_k_a': 1.0 + _normal(next(ks), (L, RWKV_W), 0.1),
        'rwkv_r_k': _normal(next(ks), (L, H, N), 0.1),
        'rwkv_lnx_w': 1.0 + _normal(next(ks), (L, RWKV_W), 0.02),
        'rwkv_lnx_b': _normal(next(ks), (L, RWKV_W), 0.02),
        'sgu_ln_g': 1.0 + _normal(next(ks), (L, SGU_W), 0.02),
        'sgu_ln_b': _normal(next(ks), (L, SGU_W), 0.02),
        'sgu_ws': _normal(next(ks), (L, SGU_GROUPS, CHUNK, CHUNK), CHUNK ** -0.5),
        'sgu_bs': 1.0 + _normal(next(ks), (L, SGU_GROUPS, CHUNK), 0.1),
        'proj_conv': _normal(next(ks), (L, CONV_W, D), CONV_W ** -0.5),
        'proj_rwkv': _normal(next(ks), (L, RWKV_W, D), RWKV_W ** -0.5),
        'proj_sgu': _normal(next(ks), (L, SGU_W, D), SGU_W ** -0.5),
        'w_out': _normal(next(ks), (L, D, D), D ** -0.5),
        'router_w': _normal(next(ks), (D, N_EXPERTS), D ** -0.5),
        'router_b': _normal(next(ks), (N_EXPERTS,), 0.01),
        'exp_w1': _normal(next(ks), (L, N_EXPERTS, D, D_EXPERT), D ** -0.5),
        'exp_w3': _normal(next(ks), (L, N_EXPERTS, D, D_EXPERT), D ** -0.5),
        'exp_w2': _normal(next(ks), (L, N_EXPERTS, D_EXPERT, D), D_EXPERT ** -0.5),
    }

def reference(x_prompt, x_sample, state_rwkv, c, c_ctx, norm1_g, norm2_g, final_g, ada_w, ada_b, w_in,
              conv_w, rwkv_w0, rwkv_w2, rwkv_a0, rwkv_a2, rwkv_g2, rwkv_k_k, rwkv_k_a, rwkv_r_k,
              rwkv_lnx_w, rwkv_lnx_b, sgu_ln_g, sgu_ln_b, sgu_ws, sgu_bs, proj_conv, proj_rwkv, proj_sgu,
              w_out, router_w, router_b, exp_w1, exp_w3, exp_w2):
    ctx_grid = (1, x_prompt.shape[1])
    rows = x_sample.shape[1] // GRID_W
    lat_grid = (rows, GRID_W)
    x_ctx, x_lat = x_prompt, x_sample
    s_ctx0 = jnp.zeros((x_prompt.shape[0], N_DIR, RWKV_HEADS, RWKV_HEAD, RWKV_HEAD), jnp.float32)
    new_states = []
    for l in range(DEPTH):
        lp = {
            'norm1_g': norm1_g[l], 'norm2_g': norm2_g[l], 'w_in': w_in[l], 'conv_w': conv_w[l],
            'rwkv_w0': rwkv_w0[l], 'rwkv_w2': rwkv_w2[l], 'rwkv_a0': rwkv_a0[l], 'rwkv_a2': rwkv_a2[l],
            'rwkv_g2': rwkv_g2[l], 'rwkv_k_k': rwkv_k_k[l], 'rwkv_k_a': rwkv_k_a[l], 'rwkv_r_k': rwkv_r_k[l],
            'rwkv_lnx_w': rwkv_lnx_w[l], 'rwkv_lnx_b': rwkv_lnx_b[l],
            'sgu_ln_g': sgu_ln_g[l], 'sgu_ln_b': sgu_ln_b[l], 'sgu_ws': sgu_ws[l], 'sgu_bs': sgu_bs[l],
            'proj_conv': proj_conv[l], 'proj_rwkv': proj_rwkv[l], 'proj_sgu': proj_sgu[l], 'w_out': w_out[l],
            'exp_w1': exp_w1[l], 'exp_w3': exp_w3[l], 'exp_w2': exp_w2[l],
        }
        mod_ctx = (jax.nn.silu(c_ctx) @ ada_w[l] + ada_b[l])[None]
        mod_lat = jax.nn.silu(c) @ ada_w[l] + ada_b[l]
        x_ctx, s_ctx = trunk_layer(x_ctx, mod_ctx, s_ctx0, ctx_grid, lp, router_w, router_b)
        x_lat, _ = trunk_layer(x_lat, mod_lat, state_rwkv[:, l], lat_grid, lp, router_w, router_b)
        new_states.append(s_ctx)
    y_prompt = rms_norm(x_ctx, final_g)
    y_sample = rms_norm(x_lat, final_g)
    new_state_rwkv = jnp.stack(new_states, axis=1).astype(x_prompt.dtype)
    return (y_prompt, y_sample, new_state_rwkv)


_drawn_inputs = setup_inputs


def setup_inputs(seed=0):
    import zlib

    import numpy as np

    out = dict(_drawn_inputs(seed))
    spreads = {}
    factors = {'state_rwkv': 8.0,
     'final_g': 8.3,
     'rwkv_k_k': 15.721,
     'rwkv_lnx_w': 32.901,
     'rwkv_lnx_b': 37.729,
     'sgu_ln_g': 21.577,
     'sgu_ln_b': 18.395,
     'norm2_g': 4.069,
     'sgu_bs': 3.933}
    for name, (base, spread) in spreads.items():
        noise = np.random.default_rng([zlib.crc32(name.encode()), seed]).standard_normal(out[name].shape)
        drawn = base * np.exp(spread * noise) if base else spread * noise
        out[name] = __import__('jax').numpy.asarray(drawn.astype(out[name].dtype))
    for name, factor in factors.items():
        out[name] = (out[name] * factor).astype(out[name].dtype)
    return out
```

```python
from contextlib import ExitStack

import numpy as np

import concourse.bass as bass
from concourse import mybir

F32 = mybir.dt.float32
U32, I32 = mybir.dt.uint32, mybir.dt.int32
ALU = mybir.AluOpType
ACT = mybir.ActivationFunctionType
X_AXIS = mybir.AxisListType.X

P = 128
D = 1024
KD = D // P
NT = 17
LAT = 16
H, N = 8, 64
W = H * N
NEXP = 16
FE = 256
EPS = 1e-6
GN_EPS = 64e-5
DECAY = float(np.exp(-0.5))

CB, CC, CX = 0, 256, 512
CR, CK, CV = 768, 1280, 1792
CWLO, CALO, CGLO, CSU, CSV, CGATE = 2304, 2432, 2560, 2688, 2944, 3200

IDENT, LOW, UP, LOWI, UPI = range(5)
CUMI = (5, 6)
CUME = (7, 8)
LEVEL = [[9 + 7 * d + l for l in range(7)] for d in range(2)]
IND = 23
PAIR = 24
NCONST = 25
NB = (NT * P * 2 + NEXP * (P - 1)) // P
ROUTE_COLS = 20 + NT + NB + NEXP * NEXP + NT
ROUTE_OH = 24
WSLOTS = 4


def shape_constants():
    i = np.arange(P)
    r, c = i[:, None], i[None, :]
    m = np.zeros((NCONST, P, P), np.float32)
    m[IDENT] = r == c
    m[LOW], m[UP], m[LOWI], m[UPI] = r > c, r < c, r >= c, r <= c
    half = [(i < 64), (i >= 64)]
    for d in range(2):
        s, t = r, c
        incl = (s <= t) if d == 0 else (s >= t)
        excl = (s < t) if d == 0 else (s > t)
        m[CUMI[d]] = -DECAY * (incl.astype(np.float64) - half[d][:, None])
        m[CUME[d]] = -DECAY * (excl.astype(np.float64) - half[d][:, None])
        for l in range(7):
            b = 1 << l
            low = (r // (2 * b) == c // (2 * b)) & ((r // b) % 2 == 1) & ((c // b) % 2 == 0)
            m[LEVEL[d][l]] = low if d == 0 else low.T
        m[IND][:, 2 * d] = -DECAY * half[d]
        m[IND][:, 2 * d + 1] = -DECAY * ~half[d]
    m[PAIR] = r // 64 == c // 64
    return np.ascontiguousarray(m.transpose(1, 0, 2))


def route_constants():
    m = np.zeros((P, ROUTE_COLS), np.float32)
    e = np.arange(NEXP)
    row = np.concatenate([np.arange(4), e, P * np.arange(NT), np.arange(NB),
                          (e[None, :] <= e[:, None]).astype(np.float32).reshape(-1)])
    m[:, :row.size] = row
    m[:, row.size:] = np.arange(P)[:, None] + P * np.arange(NT)
    return m


def after(e, sem, t, per=1):
    e.wait_ge(sem, t * per + per)


def freed(e, sem, t, per=1):
    if not (isinstance(t, int) and t == 0):
        e.wait_ge(sem, t * per)


def over_tiles(e, step):
    for t in range(2):
        step(t, t, 0, 3)
    with e.Fori(1, LAT // 2 - 1) as j:
        step(j * 2, 0, j, 3)
        step(j * 2 + 1, 1, j, 3)
    for t in range(LAT - 2, NT):
        step(t, t % 2, t // 2, LAT - t)


class Sems:

    def __init__(self, nc, ctx):
        self.nc, self.taken = nc, []
        ctx.callback(self.clear)

    def __call__(self, name):
        self.taken.append(self.nc.alloc_semaphore(name=name))
        return self.taken[-1]

    def clear(self):
        self.nc.clear_and_free_semaphores(self.taken)
        self.nc.all_engine_barrier()


def stage_modulation(nc, io, scr, K):
    with ExitStack() as ctx:
        def sb(name, shape):
            return ctx.enter_context(nc.sbuf_tensor(name, shape, F32))

        sem = Sems(nc, ctx)
        NC = 12
        crow = sb("m_crow", [16, P])
        sig = sb("m_sig", [P, 16])
        sil = sb("m_sil", [P, 16])
        cw = [sb(f"m_w{b}", [P, KD, 512]) for b in range(2)]
        brow = sb("m_brow", [2, 6 * D])
        mrow = sb("m_mrow", [2, 6 * D])
        prow = sb("m_prow", [118, P])
        n2row = sb("m_n2row", [2, D])
        rows = sb("m_rows", [2, 3, D])
        ps = ctx.enter_context(nc.psum_tensor("m_ps", [P, 4, 512], F32))
        const_in, c_in, b_in = sem("m_const_in"), sem("m_c_in"), sem("m_b_in")
        w_in = [sem(f"m_w_in{b}") for b in range(2)]
        cT, sig_ok, sil_ok = sem("m_cT"), sem("m_sig_ok"), sem("m_sil_ok")
        out_ps, out_sb, rows_ok = sem("m_out_ps"), sem("m_out_sb"), sem("m_rows_ok")
        stored, rows_in, rowsT, pt_ok, g_ok = (sem("m_stored"), sem("m_rows_in"), sem("m_rowsT"),
                                               sem("m_pt_ok"), sem("m_g_ok"))
        ada = io["ada_w"].rearrange("(k p) n -> p k n", p=P)

        with nc.Block() as block:
            @block.sync
            def _(sp):
                sp.dma_start(K["ident"][:, :], io["consts"][:, IDENT, :]).then_inc(const_in, 16)
                sp.dma_start(crow[:, :], io["c_all"].rearrange("v (k p) -> (v k) p", p=P)).then_inc(c_in, 16)
                for n in range(NC):
                    if n >= 2:
                        sp.wait_ge(out_ps, n - 1)
                    sp.dma_start(cw[n % 2][:, :, :], ada[:, :, n * 512:(n + 1) * 512]).then_inc(w_in[n % 2], 16)
                sp.wait_ge(out_sb, NC)
                sp.dma_start(scr["mod"], mrow[:, :]).then_inc(stored, 16)
                sp.wait_ge(stored, 16)
                sp.dma_start(prow[0:96, :], scr["mod"].rearrange("v (s k p) -> (v s k) p", k=KD, p=P))\
                    .then_inc(rows_in, 16)
                sp.wait_ge(rows_in, 64)
                sp.wait_ge(rows_ok, 3)
                sp.dma_start(scr["rows"], rows[:, :, :]).then_inc(stored, 16)
                sp.wait_ge(stored, 32)

            @block.scalar
            def _(act):
                act.dma_start(brow[:, :], io["ada_b"].partition_broadcast(2)).then_inc(b_in, 16)
                act.dma_start(n2row[:, :], io["norm2_g"].partition_broadcast(2)).then_inc(b_in, 16)
                act.dma_start(prow[96:104, :], io["norm1_g"].rearrange("(k p) -> k p", p=P)).then_inc(rows_in, 16)
                act.dma_start(prow[104:112, :], io["norm2_g"].rearrange("(k p) -> k p", p=P)).then_inc(rows_in, 16)
                act.dma_start(prow[112:118, :], io["conv_w"].rearrange("c (k p) -> (c k) p", p=P))\
                    .then_inc(rows_in, 16)
                act.wait_ge(cT, 1)
                nc.scalar.activation(sig[:, :], ps[:, 0, 0:16], ACT.Sigmoid).then_inc(sig_ok, 1)

            @block.vector
            def _(dve):
                dve.wait_ge(sig_ok, 1)
                nc.vector.tensor_tensor(sil[:, :], ps[:, 0, 0:16], sig[:, :], ALU.mult).then_inc(sil_ok, 1)
                dve.wait_ge(b_in, 32)
                for n in range(NC):
                    dve.wait_ge(out_ps, n + 1)
                    nc.vector.tensor_tensor(mrow[:, n * 512:(n + 1) * 512], ps[0:2, 1 + n % 2, :],
                                            brow[:, n * 512:(n + 1) * 512], ALU.add).then_inc(out_sb, 1)
                dve.wait_ge(out_sb, NC)
                nc.vector.tensor_copy(rows[:, 0, :], mrow[:, 2 * D:3 * D]).then_inc(rows_ok, 1)
                nc.vector.scalar_tensor_tensor(rows[:, 1, :], mrow[:, 4 * D:5 * D], 1.0, n2row[:, :], ALU.add, ALU.mult)\
                    .then_inc(rows_ok, 1)
                nc.vector.tensor_copy(rows[:, 2, :], mrow[:, 3 * D:4 * D]).then_inc(rows_ok, 1)
                dve.wait_ge(rowsT, 1)
                nc.vector.tensor_copy(K["pt"][:, :], ps[:, 3, 0:118]).then_inc(pt_ok, 1)
                dve.wait_ge(pt_ok, 1)
                for norm, sc_at in ((0, 1), (1, 4)):
                    for v in range(2):
                        at = (v * 6 + sc_at) * KD
                        g = 96 + 8 * norm
                        nc.vector.scalar_tensor_tensor(K["gs"][:, norm, v, :], K["pt"][:, at:at + KD], 1.0,
                                                       K["pt"][:, g:g + KD], ALU.add, ALU.mult).then_inc(g_ok, 1)
                dve.wait_ge(g_ok, 4)

            @block.tensor
            def _(pe):
                pe.wait_ge(const_in, 16)
                pe.wait_ge(c_in, 16)
                nc.tensor.transpose(ps[:, 0, 0:16], crow[:, :], K["ident"][0:16, 0:16]).then_inc(cT, 1)
                pe.wait_ge(sil_ok, 1)
                both = sil[:, :].rearrange("p (v k) -> p k v", v=2)
                for n in range(NC):
                    pe.wait_ge(w_in[n % 2], 16 * (n // 2 + 1))
                    if n >= 2:
                        pe.wait_ge(out_sb, n - 1)
                    for k in range(KD):
                        last = nc.tensor.matmul(ps[0:2, 1 + n % 2, :], both[:, k, :], cw[n % 2][:, k, :],
                                                start=k == 0, stop=k == KD - 1)
                    last.then_inc(out_ps, 1)
                pe.wait_ge(rows_in, 64)
                nc.tensor.transpose(ps[:, 3, 0:118], prow[:, :], K["ident"][0:118, 0:118]).then_inc(rowsT, 1)


def stage_tokens(nc, io, scr, K):
    with ExitStack() as ctx:
        def sb(name, shape):
            return ctx.enter_context(nc.sbuf_tensor(name, shape, F32))

        sem = Sems(nc, ctx)
        ps = ctx.enter_context(nc.psum_tensor("a_ps", [P, 8, 512], F32))
        ident = K["ident"][:, :]
        win = sb("a_win", [P, KD, CGATE])
        lw = sb("a_lora_w", [P, W])
        la = sb("a_lora_a", [P, W])
        lg = sb("a_lora_g", [P, W])
        prm = sb("a_prm", [P, 7, W])
        w0b, a0b, kkb, kab, rkb = [0, 1], [2, 3], 4, 5, 6
        lng = sb("a_lng", [P, 256])
        lnb = sb("a_lnb", [P, 256])
        bsb = sb("a_bsb", [P, 2, P])
        wsT = sb("a_wsT", [P, 4, P])
        X = [sb(f"a_x{b}", [P, D]) for b in range(2)]
        Xn = sb("a_xn", [P, D])
        hT = [sb(f"a_hT{b}", [P, KD, P]) for b in range(2)]
        junk = Xn
        sqi = sb("a_sqi", [P, 10])
        sqs = sb("a_sqs", [P, 10])
        sqm = sb("a_sqm", [P, 10])
        rc = sb("a_rc", [P, 10])
        ssx = sb("a_ssx", [P, 1])
        WLO, ALO, GLO = sb("a_wlo", [P, P]), sb("a_alo", [P, P]), sb("a_glo", [P, P])
        CCs = sb("a_cc", [P, 2, P])
        Pc = sb("a_pc", [P, 2, P])
        Yc = sb("a_yc", [P, 2, P])
        CBSU = sb("a_cbsu", [P, 4, P])
        Ks = sb("a_k", [P, W])
        kk0 = sb("a_kk0", [P, W])
        ksq = sb("a_ksq", [P, W])
        m1 = sb("a_m1", [P, W])
        SV = sb("a_sv", [P, 256])
        st = sb("a_st", [P, 6])
        mv = sb("a_mv", [P, 2])
        gap = sb("a_gap", [P, 1])
        vn = sb("a_vn", [P, 256])
        vg = sb("a_vg", [P, 256])
        vb = sb("a_vb", [P, 256])
        mixs = sb("a_mix", [P, 2, P])
        ag = [sb(f"a_ag{d}", [P, W]) for d in range(2)]
        am = sb("a_am", [P, W])
        rsum = sb("a_rsum", [P, W])
        rk8 = sb("a_rk8", [P, H])
        lxb = sb("a_lxb", [P, W])
        oA = sb("a_oA", [P, 3, W])
        oD = [sb(f"a_oD{d}", [P, 3, W]) for d in range(2)]
        oO = sb("a_oO", [P, 2, W])
        tw = [oD[d][:, 2, :] for d in range(2)]
        ta = ag
        oC = sb("a_oC", [P, 4, P])

        B_T, B_F1, B_F2, B_F3, B5, B6, B7 = 0, 2, 3, 4, 5, 6, 7
        s = {n: sem("a_" + n) for n in (
            "win_in", "prm_in", "ssx_ok", "ms_ok", "xrt_ok", "rc_ok", "xm_ok", "xn_ok", "hT_ps", "hT_ok",
            "F1", "F2", "F3", "lo_ok", "cc_ok", "cbsu_ok", "pc_ok", "yc_ok", "conv_ok",
            "K", "R", "V", "SV", "WL0", "AL0", "WL1", "AL1", "G", "MIX",
            "k_ok", "r_ok", "v_ok", "sv_ok", "kk0_ok", "ksq_ok", "n2_ok", "st_ok", "mv_ok", "var_ok", "sq_ok",
            "sqm_ok", "kk_ok", "vn_ok", "vg_ok", "vb_ok", "m1_ok", "tw0", "ta0", "tw1", "ta1",
            "sg0", "sg1", "ag0", "ag1", "ka0", "ka1", "am0", "am1", "kd0", "kd1",
            "s1", "s2", "s3", "rk_ok", "bm_ok", "bonus_ok", "g_ok", "mix_ok", "sgu_ok",
            "stA", "stD0", "stD1", "stO", "stC")}
        x_in = [sem(f"a_x_in{b}") for b in range(2)]
        st_h = [sem(f"a_st_h{b}") for b in range(2)]

        def tile_of(ap, t):
            return ap[bass.ds(t, 1)].rearrange("a p n -> (a p) n")

        with nc.Block() as block:
            @block.sync
            def _(sp):
                def load_x(t, b):
                    sp.dma_start(X[b][:, :], tile_of(io["x_all"], t)).then_inc(x_in[b], 16)

                load_x(0, 0)
                load_x(1, 1)
                w_v = io["w_in"].rearrange("(k p) n -> p k n", p=P)
                for k in range(KD):
                    sp.dma_start(win[:, k, :], w_v[:, k, 0:CGATE]).then_inc(s["win_in"], 16)

                def step(t, b, n, left):
                    last = left == 0
                    if left >= 2:
                        after(sp, s["xn_ok"], t)
                        load_x(t + 2, b)
                    after(sp, s["hT_ok"], t, 2)
                    sp.dma_start(tile_of(scr["h"], t), hT[b][:, :, :].rearrange("p k n -> p (k n)"))\
                        .then_inc(st_h[b], 16)
                    after(sp, s["conv_ok"], t)
                    after(sp, s["sgu_ok"], t)
                    sp.dma_start(tile_of(scr["cs"], t), oC[:, :, :].rearrange("p k n -> p (k n)")).then_inc(s["stC"], 16)
                    after(sp, s["r_ok"], t)
                    after(sp, s["v_ok"], t)
                    after(sp, s["kk_ok"], t)
                    sp.dma_start(tile_of(scr["A"], t), oA[:, :, :].rearrange("p k n -> p (k n)")).then_inc(s["stA"], 16)
                    for d in range(2):
                        after(sp, s[f"sg{d}"], t)
                        after(sp, s[f"ka{d}"], t)
                        after(sp, s[f"kd{d}"], t)
                        sp.dma_start(tile_of(scr[f"D{d}"], t), oD[d][:, :, :].rearrange("p k n -> p (k n)"))\
                            .then_inc(s[f"stD{d}"], 16)
                    after(sp, s["g_ok"], t)
                    after(sp, s["bonus_ok"], t)
                    sp.dma_start(tile_of(scr["O"], t), oO[:, :, :].rearrange("p k n -> p (k n)")).then_inc(s["stO"], 16)

                over_tiles(sp, step)
                for name in ("stC", "stA", "stD0", "stD1", "stO"):
                    sp.wait_ge(s[name], 16 * NT)
                sp.wait_ge(st_h[0], 16 * 9)
                sp.wait_ge(st_h[1], 16 * 8)

            @block.scalar
            def _(act):
                loads = [(lw[:, :], io["rwkv_w2"]), (la[:, :], io["rwkv_a2"]), (lg[:, :], io["rwkv_g2"]),
                         (prm[:, 0, :], io["rwkv_w0"][0].partition_broadcast(P)),
                         (prm[:, 1, :], io["rwkv_w0"][1].partition_broadcast(P)),
                         (prm[:, 2, :], io["rwkv_a0"][0].partition_broadcast(P)),
                         (prm[:, 3, :], io["rwkv_a0"][1].partition_broadcast(P)),
                         (prm[:, 4, :], io["rwkv_k_k"].partition_broadcast(P)),
                         (prm[:, 5, :], io["rwkv_k_a"].partition_broadcast(P)),
                         (prm[:, 6, :], io["rwkv_r_k"].partition_broadcast(P)),
                         (lng[:, :], io["sgu_ln_g"].partition_broadcast(P)),
                         (lnb[:, :], io["sgu_ln_b"].partition_broadcast(P)),
                         (lxb[:, :], io["rwkv_lnx_b"].partition_broadcast(P)),
                         (wsT[:, :, :], io["sgu_wsT"])]
                for g in range(4):
                    loads.append((bsb[64 * (g % 2):64 * (g % 2) + 64, g // 2, :],
                                  io["sgu_bs"][g].partition_broadcast(64)))
                for dst, src in loads:
                    act.dma_start(dst, src).then_inc(s["prm_in"], 16)

                def sum_squares(t, b, n):
                    after(act, x_in[b], n, 16)
                    freed(act, s["hT_ps"], t)
                    nc.scalar.activation(junk[:, :], X[b][:, :], ACT.Square, accum_out=ssx[:, :])\
                        .then_inc(s["ssx_ok"], 1)

                def evacuate_h(t, b, v):
                    after(act, s["hT_ps"], t)
                    for k in range(4):
                        ins = nc.scalar.activation(hT[b][:, k, :], ps[:, B_T, k * P:(k + 1) * P], ACT.Identity,
                                                   bias=K["pt"][:, v * 48 + k:v * 48 + k + 1],
                                                   scale=K["gs"][:, 0, v, k:k + 1])
                    ins.then_inc(s["hT_ok"], 1)

                sum_squares(0, 0, 0)
                act.wait_ge(s["ms_ok"], 1)
                nc.scalar.activation(sqs[:, 9:10], sqi[:, 9:10], ACT.Sqrt).then_inc(s["xrt_ok"], 1)
                evacuate_h(0, 0, 0)

                def step(t, b, n, left):
                    last = left == 0
                    if not last:
                        sum_squares(t + 1, 1 - b, n + b)
                    after(act, s["F1"], t)
                    nc.scalar.activation(WLO[:, :], ps[:, B_F1, 0:P], ACT.Tanh)
                    nc.scalar.activation(ALO[:, :], ps[:, B_F1, P:2 * P], ACT.Copy)
                    nc.scalar.activation(GLO[:, :], ps[:, B_F1, 2 * P:3 * P], ACT.Sigmoid).then_inc(s["lo_ok"], 1)
                    after(act, s["F2"], t)
                    freed(act, s["pc_ok"], t)
                    nc.scalar.activation(CCs[:, :, :].rearrange("p a n -> p (a n)"), ps[:, B_F2, 0:256], ACT.Copy)\
                        .then_inc(s["cc_ok"], 1)
                    after(act, s["F3"], t)
                    freed(act, s["conv_ok"], t)
                    freed(act, s["sgu_ok"], t)
                    nc.scalar.activation(CBSU[:, :, :].rearrange("p a n -> p (a n)"), ps[:, B_F3, :], ACT.Copy)\
                        .then_inc(s["cbsu_ok"], 1)
                    after(act, s["K"], t)
                    freed(act, s["kd1"], t)
                    nc.scalar.activation(Ks[:, :], ps[:, B5, :], ACT.Copy).then_inc(s["k_ok"], 1)
                    after(act, s["R"], t)
                    freed(act, s["stA"], t, 16)
                    freed(act, s["s2"], t)
                    nc.scalar.activation(oA[:, 0, :], ps[:, B7, :], ACT.Copy).then_inc(s["r_ok"], 1)
                    after(act, s["kk0_ok"], t)
                    freed(act, s["n2_ok"], t)
                    nc.scalar.activation(ksq[:, :], kk0[:, :], ACT.Square).then_inc(s["ksq_ok"], 1)
                    after(act, s["n2_ok"], t)
                    after(act, s["var_ok"], t)
                    if last:
                        nc.scalar.activation(sqs[:, 0:9], sqi[:, 0:9], ACT.Sqrt).then_inc(s["sq_ok"], 1)
                    else:
                        after(act, s["ms_ok"], t + 1)
                        nc.scalar.activation(sqs[:, :], sqi[:, :], ACT.Sqrt).then_inc(s["sq_ok"], 1)
                    if not last:
                        freed(act, s["V"], t)
                        freed(act, st_h[1 - b], n + b, 16)
                        evacuate_h(t + 1, 1 - b, int(left == 1))
                    for d in range(2):
                        after(act, s[f"tw{d}"], t)
                        nc.scalar.activation(oD[d][:, 2, :], tw[d], ACT.Sigmoid).then_inc(s[f"sg{d}"], 1)
                        after(act, s[f"ta{d}"], t)
                        nc.scalar.activation(ag[d][:, :], ta[d][:, :], ACT.Sigmoid).then_inc(s[f"ag{d}"], 1)
                    after(act, s["G"], t)
                    freed(act, s["stO"], t, 16)
                    nc.scalar.activation(oO[:, 1, :], ps[:, B7, :], ACT.Copy).then_inc(s["g_ok"], 1)

                over_tiles(act, step)

            @block.vector
            def _(dve):
                def mean_square(t):
                    after(dve, s["ssx_ok"], t)
                    nc.vector.tensor_scalar(sqi[:, 9:10], ssx[:, :], 1.0 / D, EPS, ALU.mult, ALU.add)\
                        .then_inc(s["ms_ok"], 1)

                def evacuate_h(t, b, v):
                    after(dve, s["hT_ps"], t)
                    for k in range(4, KD):
                        ins = nc.vector.tensor_scalar(hT[b][:, k, :], ps[:, B_T + 1, (k - 4) * P:(k - 3) * P],
                                                      K["gs"][:, 0, v, k:k + 1],
                                                      K["pt"][:, v * 48 + k:v * 48 + k + 1], ALU.mult, ALU.add)
                    ins.then_inc(s["hT_ok"], 1)

                dve.wait_ge(s["prm_in"], 16 * 18)
                mean_square(0)
                dve.wait_ge(s["xrt_ok"], 1)
                nc.vector.reciprocal(rc[:, 9:10], sqs[:, 9:10]).then_inc(s["xm_ok"], 1)
                dve.wait_ge(s["xm_ok"], 1)
                nc.vector.tensor_scalar(Xn[:, :], X[0][:, :], rc[:, 9:10], None, ALU.mult).then_inc(s["xn_ok"], 1)
                evacuate_h(0, 0, 0)

                def step(t, b, n, left):
                    last = left == 0
                    if not last:
                        mean_square(t + 1)
                    after(dve, s["cc_ok"], t)
                    freed(dve, s["conv_ok"], t)
                    nc.vector.tensor_tensor(Pc[:, :, :].rearrange("p a n -> p (a n)"),
                                            CCs[:, :, :].rearrange("p a n -> p (a n)"), ps[:, B_F2, 256:512],
                                            ALU.mult).then_inc(s["pc_ok"], 1)
                    after(dve, s["pc_ok"], t)
                    rows, cols = (1, P) if last else (2, 64)
                    for m in range(2):
                        nc.vector.tensor_scalar(Yc[:, m, :], Pc[:, m, :], K["pt"][:, 114 + m:115 + m], None, ALU.mult)\
                            .then_inc(s["yc_ok"], 1)
                    for m in range(2):
                        pv = Pc[:, m, :].rearrange("p (r c) -> p r c", r=rows)
                        yv = Yc[:, m, :].rearrange("p (r c) -> p r c", r=rows)
                        dve.wait_ge(s["yc_ok"], t * 6 + 1 + m)
                        nc.vector.scalar_tensor_tensor(yv[:, :, 1:cols], pv[:, :, 0:cols - 1], K["pt"][:, 112 + m:113 + m],
                                                       yv[:, :, 1:cols], ALU.mult, ALU.add).then_inc(s["yc_ok"], 1)
                    for m in range(2):
                        pv = Pc[:, m, :].rearrange("p (r c) -> p r c", r=rows)
                        yv = Yc[:, m, :].rearrange("p (r c) -> p r c", r=rows)
                        dve.wait_ge(s["yc_ok"], t * 6 + 3 + m)
                        nc.vector.scalar_tensor_tensor(yv[:, :, 0:cols - 1], pv[:, :, 1:cols], K["pt"][:, 116 + m:117 + m],
                                                       yv[:, :, 0:cols - 1], ALU.mult, ALU.add).then_inc(s["yc_ok"], 1)
                    after(dve, s["SV"], t)
                    freed(dve, s["vn_ok"], t)
                    nc.vector.tensor_copy(SV[:, :], ps[:, B6, 0:256]).then_inc(s["sv_ok"], 1)
                    after(dve, s["sv_ok"], t)
                    nc.vector.bn_stats(st[:, :], SV[:, :]).then_inc(s["st_ok"], 1)
                    after(dve, s["st_ok"], t)
                    nc.vector.memset(gap[:, :], 0.0)
                    nc.vector.bn_aggr(mv[:, :], st[:, :]).then_inc(s["mv_ok"], 1)
                    after(dve, s["mv_ok"], t)
                    nc.vector.tensor_scalar(sqi[:, 8:9], mv[:, 1:2], EPS, None, ALU.add).then_inc(s["var_ok"], 1)
                    after(dve, s["ksq_ok"], t)
                    nc.vector.reduce_sum(sqi[:, 0:8], ksq[:, :].rearrange("p (h n) -> p h n", h=H), axis=X_AXIS)\
                        .then_inc(s["n2_ok"], 1)
                    after(dve, s["V"], t)
                    freed(dve, s["stA"], t, 16)
                    freed(dve, s["bonus_ok"], t)
                    nc.vector.tensor_copy(oA[:, 1, :], ps[:, B5, :]).then_inc(s["v_ok"], 1)
                    after(dve, s["sq_ok"], t)
                    cols = 9 if last else 10
                    nc.vector.tensor_scalar(sqm[:, 0:cols], sqs[:, 0:cols], 1e-12, None, ALU.max).then_inc(s["sqm_ok"], 1)
                    after(dve, s["sqm_ok"], t)
                    nc.vector.reciprocal(rc[:, 0:cols], sqm[:, 0:cols]).then_inc(s["rc_ok"], 1)
                    after(dve, s["rc_ok"], t)
                    if not last:
                        nc.vector.tensor_scalar(Xn[:, :], X[1 - b][:, :], rc[:, 9:10], None, ALU.mult)\
                            .then_inc(s["xn_ok"], 1)
                    freed(dve, s["vg_ok"], t)
                    nc.vector.tensor_scalar(vn[:, :], SV[:, :], mv[:, 0:1], rc[:, 8:9], ALU.subtract, ALU.mult)\
                        .then_inc(s["vn_ok"], 1)
                    freed(dve, s["ka1"], t)
                    nc.vector.tensor_tensor(oA[:, 2, :].rearrange("p (h n) -> p h n", h=H),
                                            kk0[:, :].rearrange("p (h n) -> p h n", h=H),
                                            rc[:, 0:8].unsqueeze(2).broadcast_to([P, H, N]), ALU.mult)\
                        .then_inc(s["kk_ok"], 1)
                    if not last:
                        freed(dve, s["V"], t)
                        freed(dve, st_h[1 - b], n + b, 16)
                        evacuate_h(t + 1, 1 - b, int(left == 1))
                    for d, bw, ba in ((0, B6, B7), (1, B5, B6)):
                        after(dve, s[f"WL{d}"], t)
                        freed(dve, s[f"stD{d}"], t, 16)
                        nc.vector.tensor_tensor(tw[d], ps[:, bw, :], prm[:, w0b[d], :], ALU.add)\
                            .then_inc(s[f"tw{d}"], 1)
                        after(dve, s[f"AL{d}"], t)
                        freed(dve, s[f"ka{d}"], t)
                        nc.vector.tensor_tensor(ta[d][:, :], ps[:, ba, :], prm[:, a0b[d], :], ALU.add)\
                            .then_inc(s[f"ta{d}"], 1)
                    for d in range(2):
                        after(dve, s[f"ag{d}"], t)
                        after(dve, s["m1_ok"], t)
                        if d == 0:
                            freed(dve, s["kd1"], t)
                        else:
                            after(dve, s["kd0"], t)
                        nc.vector.scalar_tensor_tensor(am[:, :], ag[d][:, :], -1.0, m1[:, :], ALU.add, ALU.mult)\
                            .then_inc(s[f"am{d}"], 1)
                    after(dve, s["s3"], t)
                    nc.vector.reduce_sum(rk8[:, :], rsum[:, :].rearrange("p (h n) -> p h n", h=H), axis=X_AXIS)\
                        .then_inc(s["rk_ok"], 1)
                    after(dve, s["MIX"], t)
                    freed(dve, s["sgu_ok"], t)
                    nc.vector.tensor_tensor(mixs[:, :, :].rearrange("p a n -> p (a n)"), ps[:, B5, 0:256],
                                            bsb[:, :, :].rearrange("p a n -> p (a n)"), ALU.add).then_inc(s["mix_ok"], 1)

                over_tiles(dve, step)

            @block.gpsimd
            def _(pool):
                pool.wait_ge(s["prm_in"], 16 * 18)

                def step(t, b, n, left):
                    last = left == 0
                    g = nc.gpsimd
                    after(pool, s["k_ok"], t)
                    freed(pool, s["kk_ok"], t)
                    g.tensor_tensor(kk0[:, :], Ks[:, :], prm[:, kkb, :], ALU.mult).then_inc(s["kk0_ok"], 1)
                    freed(pool, s["am1"], t)
                    g.tensor_tensor(m1[:, :], Ks[:, :], prm[:, kab, :], ALU.mult).then_inc(s["m1_ok"], 1)
                    after(pool, s["cbsu_ok"], t)
                    pool.wait_ge(s["yc_ok"], t * 6 + 6)
                    freed(pool, s["stC"], t, 16)
                    g.tensor_tensor(oC[:, 0:2, :], CBSU[:, 0:2, :], Yc[:, :, :], ALU.mult).then_inc(s["conv_ok"], 1)
                    after(pool, s["vn_ok"], t)
                    g.tensor_tensor(vg[:, :], vn[:, :], lng[:, :], ALU.mult).then_inc(s["vg_ok"], 1)
                    after(pool, s["vg_ok"], t)
                    freed(pool, s["MIX"], t)
                    g.tensor_tensor(vb[:, :], vg[:, :], lnb[:, :], ALU.add).then_inc(s["vb_ok"], 1)
                    after(pool, s["kk_ok"], t)
                    for d in range(2):
                        after(pool, s[f"ag{d}"], t)
                        freed(pool, s[f"stD{d}"], t, 16)
                        g.tensor_tensor(oD[d][:, 1, :], oA[:, 2, :], ag[d][:, :], ALU.mult).then_inc(s[f"ka{d}"], 1)
                        after(pool, s[f"am{d}"], t)
                        g.tensor_tensor(oD[d][:, 0, :], am[:, :], Ks[:, :], ALU.add).then_inc(s[f"kd{d}"], 1)
                    after(pool, s["kd1"], t)
                    freed(pool, s["rk_ok"], t)
                    g.tensor_tensor(rsum[:, :], oD[0][:, 0, :], oD[1][:, 0, :], ALU.add).then_inc(s["s1"], 1)
                    after(pool, s["s1"], t)
                    after(pool, s["r_ok"], t)
                    g.tensor_tensor(rsum[:, :], rsum[:, :], oA[:, 0, :], ALU.mult).then_inc(s["s2"], 1)
                    after(pool, s["s2"], t)
                    g.tensor_tensor(rsum[:, :], rsum[:, :], prm[:, rkb, :], ALU.mult).then_inc(s["s3"], 1)
                    after(pool, s["rk_ok"], t)
                    after(pool, s["v_ok"], t)
                    freed(pool, s["stO"], t, 16)
                    g.tensor_tensor(oO[:, 0, :].rearrange("p (h n) -> p h n", h=H),
                                    oA[:, 1, :].rearrange("p (h n) -> p h n", h=H),
                                    rk8[:, :].unsqueeze(2).broadcast_to([P, H, N]), ALU.mult).then_inc(s["bm_ok"], 1)
                    after(pool, s["bm_ok"], t)
                    g.tensor_tensor(oO[:, 0, :], oO[:, 0, :], lxb[:, :], ALU.add).then_inc(s["bonus_ok"], 1)
                    after(pool, s["mix_ok"], t)
                    g.tensor_tensor(oC[:, 2:4, :], CBSU[:, 2:4, :], mixs[:, :, :], ALU.mult).then_inc(s["sgu_ok"], 1)

                over_tiles(pool, step)

            @block.tensor
            def _(pe):
                def transposes(t):
                    after(pe, s["xn_ok"], t)
                    freed(pe, s["hT_ok"], t, 2)
                    for k in range(KD):
                        ins = nc.tensor.transpose(ps[:, B_T + k // 4, (k % 4) * P:(k % 4 + 1) * P],
                                                  Xn[:, k * P:(k + 1) * P], ident)
                    ins.then_inc(s["hT_ps"], 1)

                def by_feature(bank, cols, b):
                    for j, c in enumerate(cols):
                        for k in range(KD):
                            ins = nc.tensor.matmul(ps[:, bank, j * P:(j + 1) * P], win[:, k, c:c + P], hT[b][:, k, :],
                                                   start=k == 0, stop=k == KD - 1)
                    return ins

                def by_token(bank, c, width, b):
                    for k in range(KD):
                        ins = nc.tensor.matmul(ps[:, bank, 0:width], hT[b][:, k, :], win[:, k, c:c + width],
                                               start=k == 0, stop=k == KD - 1)
                    return ins

                transposes(0)
                pe.wait_ge(s["win_in"], 16 * KD)
                pe.wait_ge(s["prm_in"], 16 * 18)

                def step(t, b, n, left):
                    last = left == 0
                    after(pe, s["hT_ok"], t, 2)
                    freed(pe, s["lo_ok"], t)
                    by_feature(B_F1, (CWLO, CALO, CGLO), b).then_inc(s["F1"], 1)
                    freed(pe, s["mix_ok"], t)
                    by_token(B5, CK, W, b).then_inc(s["K"], 1)
                    freed(pe, s["ta1"], t)
                    by_token(B6, CSV, 256, b).then_inc(s["SV"], 1)
                    freed(pe, s["pc_ok"], t)
                    by_feature(B_F2, (CC, CC + P, CX, CX + P), b).then_inc(s["F2"], 1)
                    freed(pe, s["cbsu_ok"], t)
                    by_feature(B_F3, (CB, CB + P, CSU, CSU + P), b).then_inc(s["F3"], 1)
                    freed(pe, s["g_ok"], t)
                    by_token(B7, CR, W, b).then_inc(s["R"], 1)
                    after(pe, s["k_ok"], t)
                    by_token(B5, CV, W, b).then_inc(s["V"], 1)
                    if not last:
                        transposes(t + 1)
                    after(pe, s["lo_ok"], t)
                    after(pe, s["sv_ok"], t)
                    nc.tensor.matmul(ps[:, B6, :], WLO[0:64, :], lw[0:64, :], start=True, stop=True).then_inc(s["WL0"], 1)
                    after(pe, s["r_ok"], t)
                    nc.tensor.matmul(ps[:, B7, :], ALO[0:64, :], la[0:64, :], start=True, stop=True).then_inc(s["AL0"], 1)
                    after(pe, s["v_ok"], t)
                    nc.tensor.matmul(ps[:, B5, :], WLO[64:128, :], lw[64:128, :], start=True, stop=True)\
                        .then_inc(s["WL1"], 1)
                    after(pe, s["tw0"], t)
                    nc.tensor.matmul(ps[:, B6, :], ALO[64:128, :], la[64:128, :], start=True, stop=True)\
                        .then_inc(s["AL1"], 1)
                    after(pe, s["ta0"], t)
                    nc.tensor.matmul(ps[:, B7, :], GLO[:, :], lg[:, :], start=True, stop=True).then_inc(s["G"], 1)
                    after(pe, s["vb_ok"], t)
                    after(pe, s["tw1"], t)
                    for g in range(4):
                        q = 64 * (g % 2)
                        ins = nc.tensor.matmul(ps[q:q + 64, B5, (g // 2) * P:(g // 2 + 1) * P],
                                               vb[:, g * 64:(g + 1) * 64], wsT[:, g, :], start=True, stop=True)
                    ins.then_inc(s["MIX"], 1)

                over_tiles(pe, step)


def stage_scan(nc, io, scr, K):
    with ExitStack() as ctx:
        def sb(name, shape):
            return ctx.enter_context(nc.sbuf_tensor(name, shape, F32))

        def each(name, shape):
            return [sb(f"b_{name}{d}", shape) for d in range(2)]

        sem = Sems(nc, ctx)
        ps = ctx.enter_context(nc.psum_tensor("b_ps", [P, 8, 512], F32))
        const = sb("b_const", [P, NCONST, P])
        ident = K["ident"][:, :]
        inA = [[sb(f"b_inA{d}{b}", [P, 3, W]) for b in range(2)] for d in range(2)]
        inD = [[sb(f"b_inD{d}{b}", [P, 3, W]) for b in range(2)] for d in range(2)]
        EI, EN, EX = each("ei", [P, W]), each("en", [P, W]), each("ex", [P, W])
        PM = each("pm", [P, 4, 2])
        QH = each("qh", [P, 2, W])
        Rt, Bt, Kt = each("r", [P, W]), each("b", [P, W]), each("k", [P, W])
        QT, RT, BT, KT = each("qT", [P, 4, P]), each("rT", [P, 4, P]), each("bT", [P, 4, P]), each("kT", [P, 4, P])
        Am, ArbT, AqkT, ArkT = (each(n, [P, H, P]) for n in ("am", "arbT", "aqkT", "arkT"))
        TI, TIT, U, AL = (each(n, [P, H, P]) for n in ("ti", "tiT", "u", "al"))
        GH = each("gh", [P, H, 2, N])
        ET = QT
        MN = each("mn", [P, 4, N])
        MT, Shd = each("mt", [P, 4, P]), each("shd", [P, 4, P])
        S, Sh, SN = each("s", [P, 4, N]), each("sh", [P, 4, N]), each("sn", [P, 4, N])
        Yo = EI
        LV = 6

        def per_dir(name):
            return [sem(f"b_{name}{d}") for d in range(2)]

        def per_group(name):
            return [[sem(f"b_{name}{d}{g}") for g in range(2)] for d in range(2)]

        const_in = sem("b_const_in")
        s0_in, s_out = sem("b_s0_in"), sem("b_s_out")
        a_in = [[sem(f"b_a_in{d}{b}") for b in range(2)] for d in range(2)]
        cum_ps, pm_ps, e_ok, pm_ok = per_dir("cum_ps"), per_dir("pm_ps"), per_dir("e_ok"), per_dir("pm_ok")
        q_ok, r_ok, b_ok, k_ok = per_dir("q_ok"), per_dir("r_ok"), per_dir("b_ok"), per_dir("k_ok")
        qT_ps, rT_ps, bT_ps, kT_ps = per_dir("qT_ps"), per_dir("rT_ps"), per_dir("bT_ps"), per_dir("kT_ps")
        qT_ok, rT_ok, bT_ok, kT_ok = per_dir("qT_ok"), per_dir("rT_ok"), per_dir("bT_ok"), per_dir("kT_ok")
        prod_ps, prod_ok = per_group("prod_ps"), per_group("prod_ok")
        h0_ps, h0_ok = per_dir("h0_ps"), per_dir("h0_ok")
        a0_ok, t0_ok, t0_ps, r0_ok = per_group("a0_ok"), per_group("t0_ok"), per_group("t0_ps"), per_group("r0_ok")
        al_ok, u_ps, u_ok, w_ps, tr_ok = (per_group(n) for n in ("al_ok", "u_ps", "u_ok", "w_ps", "tr_ok"))
        t_ps, t_ok, gh_ps, gh_ok = (per_group(n) for n in ("t_ps", "t_ok", "gh_ps", "gh_ok"))
        et_ps, et_ok, mn_ps, mn_ok = per_dir("et_ps"), per_dir("et_ok"), per_dir("mn_ps"), per_dir("mn_ok")
        sh_ok, sn_ok, st_ps, sp_ok, s_ok = (per_dir(n) for n in ("sh_ok", "sn_ok", "st_ps", "sp_ok", "s_ok"))
        y_ps, y_ok, y_st = per_dir("y_ps"), per_dir("y_ok"), per_dir("y_st")
        zero_ok, shd_ok, clear_ok = per_dir("zero_ok"), per_dir("shd_ok"), sem("b_clear_ok")
        GROUPS = [(d, g) for g in range(2) for d in range(2)]

        def tile_of(ap, t):
            return ap[bass.ds(t, 1)].rearrange("a p n -> (a p) n")

        def tile_at(d, q):
            if isinstance(q, int) and q == LAT:
                return LAT
            return q if d == 0 else 15 - q

        def heads(g):
            return slice(4 * g, 4 * g + 4)

        def over_group(c):
            return const[:, c, :].unsqueeze(1).broadcast_to([P, 4, P])

        with nc.Block() as block:
            @block.sync
            def _(sp):
                sp.dma_start(const[:, :, :], io["consts"]).then_inc(const_in, 16)
                for d in range(2):
                    sp.dma_start(S[d][:, :, :], io["state_T"][d]).then_inc(s0_in, 16)

                def load(t, b, d):
                    sp.dma_start(inA[d][b][:, :, :].rearrange("p k n -> p (k n)"), tile_of(scr["A"], t))\
                        .then_inc(a_in[d][b], 16)
                    sp.dma_start(inD[d][b][:, :, :].rearrange("p k n -> p (k n)"), tile_of(scr[f"D{d}"], t))\
                        .then_inc(a_in[d][b], 16)

                for b in range(2):
                    for d in range(2):
                        load(tile_at(d, b), b, d)

                def step(q, b, n, left):
                    now = [tile_at(d, q) for d in range(2)]
                    nxt = [tile_at(d, q + 2 if left > 2 else LAT) for d in range(2)]
                    if left > 2:
                        now, nxt = [sp.snap(t) for t in now], [sp.snap(t) for t in nxt]
                    for d in range(2):
                        sp.wait_ge(const_in, 16)
                        after(sp, y_ps[d], q)
                        if left >= 2:
                            after(sp, a_in[d][b], n, 32)
                            load(nxt[d], b, d)
                        sp.wait_ge(const_in, 16)
                        after(sp, y_ok[d], q)
                        sp.dma_start(tile_of(scr[f"Y{d}"], now[d]), Yo[d][:, :]).then_inc(y_st[d], 16)

                over_tiles(sp, step)
                for d in range(2):
                    sp.wait_ge(s_ok[d], NT)
                    sp.dma_start(io["state_new"][d], S[d][:, :, :]).then_inc(s_out, 16)
                    sp.wait_ge(y_st[d], 16 * NT)
                sp.wait_ge(s_out, 32)

            @block.scalar
            def _(act):
                def flat(ap):
                    return ap.rearrange("p a n -> p (a n)")

                act.wait_ge(clear_ok, 2)

                def step(q, b, n, left):
                    a = nc.scalar.activation
                    for d in range(2):
                        after(act, cum_ps[d], q)
                        freed(act, y_st[d], q, 16)
                        a(EI[d][:, :], ps[:, 4 * d, :], ACT.Exp)
                        a(EN[d][:, :], ps[:, 4 * d, :], ACT.Exp, scale=-1.0)
                        a(EX[d][:, :], ps[:, 4 * d + 1, :], ACT.Exp).then_inc(e_ok[d], 1)
                        after(act, pm_ps[d], q)
                        freed(act, s_ok[d], q)
                        a(flat(PM[d][:, :, :]), ps[:, 4 * d + 2, 0:8], ACT.Exp).then_inc(pm_ok[d], 1)
                    for d in range(2):
                        after(act, qT_ps[d], q)
                        a(flat(QT[d][:, :, :]), ps[:, 4 * d, :], ACT.Copy).then_inc(qT_ok[d], 1)
                        after(act, bT_ps[d], q)
                        a(flat(BT[d][:, :, :]), ps[:, 4 * d + 2, :], ACT.Copy).then_inc(bT_ok[d], 1)
                    for d, g in GROUPS:
                        after(act, t0_ps[d][g], q)
                        a(flat(TIT[d][:, heads(g), :]), ps[:, 4 * d + 2 * g, :], ACT.Copy).then_inc(r0_ok[d][g], 1)
                    for l in range(LV):
                        for d, g in GROUPS:
                            after(act, u_ps[d][g], q * LV + l)
                            a(flat(U[d][:, heads(g), :]), ps[:, 4 * d + 2 * g, :], ACT.Copy).then_inc(u_ok[d][g], 1)
                        if l < LV - 1:
                            for d, g in GROUPS:
                                after(act, t_ps[d][g], q * (LV - 1) + l)
                                a(flat(TI[d][:, heads(g), :]), ps[:, 4 * d + 2 * g, :], ACT.Copy)\
                                    .then_inc(t_ok[d][g], 1)
                    for d, g in GROUPS:
                        after(act, gh_ps[d][g], q)
                        a(GH[d][:, heads(g), :, :].rearrange("p h a n -> p (h a n)"), ps[:, 4 * d + 2 * g, :], ACT.Copy)\
                            .then_inc(gh_ok[d][g], 1)
                    for d in range(2):
                        after(act, mn_ps[d], q)
                        both = ps[:, 4 * d + 3, :].rearrange("p (j n) -> p j n", j=4)
                        a(MN[d][:, :, :], both[:, :, N:P], ACT.Copy)
                        for u in range(2):
                            ins = a(MT[d][64 * u:64 * u + 64, :, 64 * u:64 * u + 64],
                                    both[64 * u:64 * u + 64, :, 0:N], ACT.Copy)
                        ins.then_inc(mn_ok[d], 1)
                    for d in range(2):
                        after(act, y_ps[d], q)
                        a(Yo[d][:, :], ps[:, 4 * d + 2, :], ACT.Copy).then_inc(y_ok[d], 1)

                over_tiles(act, step)

            @block.gpsimd
            def _(pool):
                pool.wait_ge(const_in, 16)
                g_ = nc.gpsimd
                for d in range(2):
                    g_.memset(MT[d][:, :, :], 0.0).then_inc(clear_ok, 1)

                def step(q, b, n, left):
                    for d in range(2):
                        after(pool, e_ok[d], q)
                        after(pool, a_in[d][b], n, 32)
                        freed(pool, y_ps[d], q)
                        g_.tensor_tensor(Rt[d][:, :], inA[d][b][:, 0, :], EI[d][:, :], ALU.mult).then_inc(r_ok[d], 1)
                        g_.tensor_tensor(Kt[d][:, :], inD[d][b][:, 0, :], EN[d][:, :], ALU.mult).then_inc(k_ok[d], 1)
                    for d in range(2):
                        after(pool, sh_ok[d], q)
                        pair = const[:, PAIR, :].rearrange("p (u n) -> p u n", u=2).unsqueeze(1)
                        g_.tensor_tensor(Shd[d][:, :, :].rearrange("p j (u n) -> p j u n", u=2),
                                         Sh[d][:, :, :].unsqueeze(2).broadcast_to([P, 4, 2, N]),
                                         pair.broadcast_to([P, 4, 2, N]), ALU.mult).then_inc(shd_ok[d], 1)
                    for d, g in GROUPS:
                        hs = heads(g)
                        after(pool, prod_ok[d][g], q)
                        freed(pool, u_ps[d][g], q, LV)
                        freed(pool, gh_ps[d][g], q)
                        g_.tensor_tensor(AL[d][:, hs, :], Am[d][:, hs, :], over_group(LEVEL[d][0]), ALU.mult)\
                            .then_inc(a0_ok[d][g], 1)
                        after(pool, a0_ok[d][g], q)
                        g_.tensor_tensor(TI[d][:, hs, :], AL[d][:, hs, :], over_group(IDENT), ALU.add)\
                            .then_inc(t0_ok[d][g], 1)
                        after(pool, t0_ok[d][g], q)
                        g_.tensor_tensor(AL[d][:, hs, :], Am[d][:, hs, :], over_group(LEVEL[d][1]), ALU.mult)\
                            .then_inc(al_ok[d][g], 1)
                    for l in range(1, LV):
                        for d, g in GROUPS:
                            hs = heads(g)
                            after(pool, u_ps[d][g], q * LV + l - 1)
                            g_.tensor_tensor(AL[d][:, hs, :], Am[d][:, hs, :], over_group(LEVEL[d][l + 1]), ALU.mult)\
                                .then_inc(al_ok[d][g], 1)

                over_tiles(pool, step)

            @block.vector
            def _(dve):
                dve.wait_ge(const_in, 16)
                dve.wait_ge(s0_in, 32)
                v_ = nc.vector

                def bank(d, i):
                    return ps[:, 4 * d + i, :].rearrange("p (h n) -> p h n", h=4)

                def step(q, b, n, left):
                    for d in range(2):
                        after(dve, e_ok[d], q)
                        after(dve, a_in[d][b], n, 32)
                        freed(dve, y_ps[d], q)
                        v_.tensor_tensor(QH[d][:, 0, :], inA[d][b][:, 2, :], EX[d][:, :], ALU.mult).then_inc(q_ok[d], 1)
                        v_.scalar_tensor_tensor(Bt[d][:, :], inD[d][b][:, 1, :], -1.0, EN[d][:, :], ALU.mult, ALU.mult)\
                            .then_inc(b_ok[d], 1)
                        after(dve, pm_ok[d], q)
                        if left == 0:
                            v_.memset(S[d][:, :, :], 0.0).then_inc(zero_ok[d], 1)
                            dve.wait_ge(zero_ok[d], 1)
                        else:
                            freed(dve, s_ok[d], q)
                        v_.tensor_tensor(Sh[d][:, :, :], S[d][:, :, :], PM[d][:, :, 0:1].broadcast_to([P, 4, N]),
                                         ALU.mult).then_inc(sh_ok[d], 1)
                    for d in range(2):
                        after(dve, rT_ps[d], q)
                        v_.tensor_copy(RT[d][:, :, :], bank(d, 1)).then_inc(rT_ok[d], 1)
                        after(dve, kT_ps[d], q)
                        v_.tensor_copy(KT[d][:, :, :], bank(d, 3)).then_inc(kT_ok[d], 1)
                    for d, g in GROUPS:
                        hs = heads(g)
                        strict, strictT, inclT = (LOW, UP, UPI) if d == 0 else (UP, LOW, LOWI)
                        after(dve, prod_ps[d][g], q)
                        v_.tensor_tensor(Am[d][:, hs, :], bank(d, 0), over_group(strict), ALU.mult)
                        v_.tensor_tensor(ArbT[d][:, hs, :], bank(d, 1), over_group(inclT), ALU.mult)
                        v_.tensor_tensor(AqkT[d][:, hs, :], bank(d, 2), over_group(strictT), ALU.mult)
                        v_.tensor_tensor(ArkT[d][:, hs, :], bank(d, 3), over_group(inclT), ALU.mult)\
                            .then_inc(prod_ok[d][g], 1)
                    for d in range(2):
                        after(dve, h0_ps[d], q)
                        v_.tensor_copy(QH[d][:, 1, :], ps[:, 4 * d, :])\
                            .then_inc(h0_ok[d], 1)
                    for l in range(LV):
                        for d, g in GROUPS:
                            after(dve, w_ps[d][g], q * LV + l)
                            v_.tensor_tensor(TIT[d][:, heads(g), :], TIT[d][:, heads(g), :], bank(d, 2 * g + 1), ALU.add)\
                                .then_inc(tr_ok[d][g], 1)
                    for d in range(2):
                        after(dve, et_ps[d], q)
                        v_.tensor_tensor(ET[d][:, :, :], RT[d][:, :, :], bank(d, 1), ALU.add).then_inc(et_ok[d], 1)
                    for d in range(2):
                        after(dve, mn_ok[d], q)
                        after(dve, sh_ok[d], q)
                        v_.tensor_tensor(SN[d][:, :, :], Sh[d][:, :, :], MN[d][:, :, :], ALU.add).then_inc(sn_ok[d], 1)
                        after(dve, st_ps[d], q)
                        after(dve, sn_ok[d], q)
                        v_.tensor_tensor(SN[d][:, :, :], SN[d][:, :, :],
                                         ps[:, 4 * d, 0:4 * N].rearrange("p (h n) -> p h n", h=4), ALU.add)\
                            .then_inc(sp_ok[d], 1)
                        after(dve, sp_ok[d], q)
                        v_.tensor_tensor(S[d][:, :, :], SN[d][:, :, :], PM[d][:, :, 1:2].broadcast_to([P, 4, N]),
                                         ALU.mult).then_inc(s_ok[d], 1)

                over_tiles(dve, step)

            @block.tensor
            def _(pe):
                pe.wait_ge(const_in, 16)

                def mm(out, lhsT, rhs, start=True, stop=True):
                    return nc.tensor.matmul(out, lhsT, rhs, start=start, stop=stop)

                def head(h):
                    return h // 2, 64 * (h % 2)

                def slot(h):
                    return 4 * (h % 2) + h // 2

                def step(q, b, n, left):
                    for d in range(2):
                        sg = inD[d][b][:, 2, :]
                        after(pe, a_in[d][b], n, 32)
                        freed(pe, sp_ok[d], q)
                        freed(pe, et_ok[d], q)
                        mm(ps[:, 4 * d, :], const[:, CUMI[d], :], sg)
                        mm(ps[:, 4 * d + 1, :], const[:, CUME[d], :], sg).then_inc(cum_ps[d], 1)
                        freed(pe, y_ok[d], q)
                        for j in range(4):
                            ins = mm(ps[:, 4 * d + 2, 2 * j:2 * j + 2], inD[d][b][:, 2, j * P:(j + 1) * P],
                                     const[:, IND, 2 * d:2 * d + 2])
                        ins.then_inc(pm_ps[d], 1)
                    for d in range(2):
                        after(pe, e_ok[d], q)
                        after(pe, q_ok[d], q)
                        for j in range(4):
                            ins = nc.tensor.transpose(ps[:, 4 * d, j * P:(j + 1) * P],
                                                      QH[d][:, 0, j * P:(j + 1) * P], ident)
                        ins.then_inc(qT_ps[d], 1)
                        after(pe, b_ok[d], q)
                        after(pe, pm_ok[d], q)
                        for j in range(4):
                            ins = nc.tensor.transpose(ps[:, 4 * d + 2, j * P:(j + 1) * P], Bt[d][:, j * P:(j + 1) * P], ident)
                        ins.then_inc(bT_ps[d], 1)
                        after(pe, r_ok[d], q)
                        for j in range(4):
                            ins = nc.tensor.transpose(ps[:, 4 * d + 1, j * P:(j + 1) * P], Rt[d][:, j * P:(j + 1) * P], ident)
                        ins.then_inc(rT_ps[d], 1)
                        after(pe, k_ok[d], q)
                        freed(pe, mn_ok[d], q)
                        for j in range(4):
                            ins = nc.tensor.transpose(ps[:, 4 * d + 3, j * P:(j + 1) * P], Kt[d][:, j * P:(j + 1) * P], ident)
                        ins.then_inc(kT_ps[d], 1)
                    for d, g in GROUPS:
                        if g == 0:
                            for ok in (qT_ok, bT_ok, rT_ok, kT_ok):
                                after(pe, ok[d], q)
                        else:
                            after(pe, prod_ok[d][0], q)
                        for j in range(4):
                            u = 64 * g
                            for bk, left_, right in ((0, QT, BT), (1, BT, RT), (2, KT, QT), (3, KT, RT)):
                                ins = mm(ps[:, 4 * d + bk, j * P:(j + 1) * P], left_[d][u:u + 64, j, :],
                                         right[d][u:u + 64, j, :])
                        ins.then_inc(prod_ps[d][g], 1)
                    for d in range(2):
                        after(pe, prod_ok[d][1], q)
                        for h in range(H):
                            ins = mm(ps[:, 4 * d, h * N:(h + 1) * N], AqkT[d][:, slot(h), :], inA[d][b][:, 1, h * N:(h + 1) * N])
                        ins.then_inc(h0_ps[d], 1)
                    for d, g in GROUPS:
                        after(pe, t0_ok[d][g], q)
                        after(pe, h0_ok[d], q)
                        for i in range(4):
                            ins = nc.tensor.transpose(ps[:, 4 * d + 2 * g, i * P:(i + 1) * P], TI[d][:, 4 * g + i, :], ident)
                        ins.then_inc(t0_ps[d][g], 1)
                    for l in range(LV):
                        for d, g in GROUPS:
                            after(pe, al_ok[d][g], q * LV + l)
                            if l == 0:
                                after(pe, r0_ok[d][g], q)
                            else:
                                after(pe, t_ok[d][g], q * (LV - 1) + l - 1)
                            for i in range(4):
                                k = 4 * g + i
                                ins = mm(ps[:, 4 * d + 2 * g, i * P:(i + 1) * P], AL[d][:, k, :], TIT[d][:, k, :])
                            ins.then_inc(u_ps[d][g], 1)
                        for d, g in GROUPS:
                            after(pe, u_ok[d][g], q * LV + l)
                            for i in range(4):
                                k = 4 * g + i
                                ins = mm(ps[:, 4 * d + 2 * g + 1, i * P:(i + 1) * P], TI[d][:, k, :], U[d][:, k, :])
                            ins.then_inc(w_ps[d][g], 1)
                        if l < LV - 1:
                            for d, g in GROUPS:
                                after(pe, tr_ok[d][g], q * LV + l)
                                for i in range(4):
                                    ins = nc.tensor.transpose(ps[:, 4 * d + 2 * g, i * P:(i + 1) * P],
                                                              TIT[d][:, 4 * g + i, :], ident)
                                ins.then_inc(t_ps[d][g], 1)
                    for d, g in GROUPS:
                        after(pe, tr_ok[d][g], q * LV + LV - 1)
                        for i in range(4):
                            h = 2 * i + g
                            ins = mm(ps[:, 4 * d + 2 * g, i * P:(i + 1) * P], TIT[d][:, slot(h), :],
                                     QH[d][:, :, h * N:(h + 1) * N])
                        ins.then_inc(gh_ps[d][g], 1)
                    for d in range(2):
                        after(pe, gh_ok[d][0], q)
                        after(pe, gh_ok[d][1], q)
                        for h in range(H):
                            j, u = head(h)
                            mm(ps[u:u + 64, 4 * d + 3, j * P:j * P + N], GH[d][:, slot(h), 0, :], Bt[d][:, h * N:(h + 1) * N])
                            new = ps[u:u + 64, 4 * d + 3, j * P + N:(j + 1) * P]
                            mm(new, Kt[d][:, h * N:(h + 1) * N], inA[d][b][:, 1, h * N:(h + 1) * N], stop=False)
                            ins = mm(new, Bt[d][:, h * N:(h + 1) * N], GH[d][:, slot(h), 1, :], start=False)
                        ins.then_inc(mn_ps[d], 1)
                    for d in range(2):
                        for h in range(H):
                            j, u = head(h)
                            ins = mm(ps[u:u + 64, 4 * d + 1, j * P:(j + 1) * P], GH[d][:, slot(h), 0, :], ArbT[d][:, slot(h), :])
                        ins.then_inc(et_ps[d], 1)
                    for d in range(2):
                        after(pe, mn_ok[d], q)
                        after(pe, sh_ok[d], q)
                        for j in range(4):
                            ins = mm(ps[:, 4 * d, j * N:(j + 1) * N], MT[d][:, j, :], Sh[d][:, j, :])
                        ins.then_inc(st_ps[d], 1)
                        after(pe, et_ok[d], q)
                        after(pe, shd_ok[d], q)
                        for j in range(4):
                            mm(ps[:, 4 * d + 2, j * P:(j + 1) * P], ET[d][:, j, :], Shd[d][:, j, :], stop=False)
                            for h in (2 * j, 2 * j + 1):
                                out = ps[:, 4 * d + 2, h * N:(h + 1) * N]
                                mm(out, ArkT[d][:, slot(h), :], inA[d][b][:, 1, h * N:(h + 1) * N],
                                   start=False, stop=False)
                                ins = mm(out, ArbT[d][:, slot(h), :], GH[d][:, slot(h), 1, :], start=False,
                                         stop=h % 2 == 1)
                        ins.then_inc(y_ps[d], 1)

                over_tiles(pe, step)


def stage_merge(nc, io, scr, K):
    with ExitStack() as ctx:
        def sb(name, shape):
            return ctx.enter_context(nc.sbuf_tensor(name, shape, F32))

        sem = Sems(nc, ctx)
        ps = ctx.enter_context(nc.psum_tensor("c_ps", [P, 8, 512], F32))
        ident = K["ident"][:, :]
        wg = sb("c_wg", [P, KD, 3 * D])
        wp = sb("c_wp", [P, KD, D])
        wo = sb("c_wo", [P, KD, D])
        rw = sb("c_rw", [P, KD, NEXP])
        rowp = sb("c_rowp", [P, 3, D])
        ga1, g2, sh2 = (rowp[:, i, :] for i in range(3))
        lnx = sb("c_lnx", [P, W])
        hT = sb("c_hT", [P, KD, P])
        cs = sb("c_cs", [P, 4, P])
        ya, yb = sb("c_ya", [P, W]), sb("c_yb", [P, W])
        ob = sb("c_ob", [P, 2, W])
        s8 = [sb(f"c_s8{i}", [P, H]) for i in range(6)]
        yT = sb("c_yT", [P, 4, P])
        Gs = [sb(f"c_gs{b}", [P, 3 * P]) for b in range(2)]
        Ms = Gs
        mT = sb("c_mT", [P, KD, P])
        h2T = mT
        xx = sb("c_xx", [P, D])
        h2 = sb("c_h2", [P, D])
        s1 = [K["pt"][:, i:i + 1] for i in range(4)]
        GB, PB, WB, TB = (0, 1, 2), (3, 4), (5, 6), 7

        s = {n: sem("c_" + n) for n in (
            "w_in", "rp_in", "h_in", "cs_in", "y_in", "x_in", "ysum", "m_ok", "mean_ok", "yc_ok", "sq_ok",
            "v_ok", "ve_ok", "sd_ok", "rs_ok", "yn_ok", "yw_ok", "yo_ok", "yf_ok", "yT_ps", "yT_ok",
            "G_ps", "G_ok", "P_ps", "M_ok", "mg_ok", "W_ps", "mix_ok", "x2_ok", "ss_ok", "ms_ok", "sx_ok", "rx_ok",
            "hm_ok", "h2_ok", "hT_ps", "hT_ok", "lg_ps", "lg_ok", "st_x", "st_h")}

        def tile_of(ap, t):
            return ap[bass.ds(t, 1)].rearrange("a p n -> (a p) n")

        def tiles(e, step):
            step(0, 0, 0, 3)
            with e.Fori(0, LAT // 2 - 1) as j:
                step(j * 2 + 1, 1, j, 3)
                step(j * 2 + 2, 0, j + 1, 3)
            step(LAT - 1, 1, LAT // 2 - 1, 1)
            step(LAT, 0, LAT // 2, 0)

        def first(t):
            return isinstance(t, int) and t == 0

        with nc.Block() as block:
            @block.sync
            def _(sp):
                def load_h(t):
                    sp.dma_start(hT[:, :, :].rearrange("p k n -> p (k n)"), tile_of(scr["h"], t)).then_inc(s["h_in"], 16)

                def load_y(t):
                    sp.dma_start(ya[:, :], tile_of(scr["Y0"], t)).then_inc(s["y_in"], 16)
                    sp.dma_start(yb[:, :], tile_of(scr["Y1"], t)).then_inc(s["y_in"], 16)
                    sp.dma_start(ob[:, :, :].rearrange("p k n -> p (k n)"), tile_of(scr["O"], t)).then_inc(s["y_in"], 16)

                def load_rows(v):
                    sp.dma_start(ga1, scr["rows"][v, 0].partition_broadcast(P)).then_inc(s["rp_in"], 16)
                    sp.dma_start(g2, scr["rows"][v, 1].partition_broadcast(P)).then_inc(s["rp_in"], 16)
                    sp.dma_start(sh2, scr["rows"][v, 2].partition_broadcast(P)).then_inc(s["rp_in"], 16)

                load_y(0)
                load_h(0)
                w_v = io["w_in"].rearrange("(k p) n -> p k n", p=P)
                for k in range(KD):
                    sp.dma_start(wg[:, k, :], w_v[:, k, CGATE:CGATE + 3 * D]).then_inc(s["w_in"], 16)
                sp.dma_start(wp[:, 0:2, :], io["proj_conv"].rearrange("(k p) n -> p k n", p=P)).then_inc(s["w_in"], 16)
                sp.dma_start(wp[:, 2:6, :], io["proj_rwkv"].rearrange("(k p) n -> p k n", p=P)).then_inc(s["w_in"], 16)
                sp.dma_start(wp[:, 6:8, :], io["proj_sgu"].rearrange("(k p) n -> p k n", p=P)).then_inc(s["w_in"], 16)
                sp.dma_start(wo[:, :, :], io["w_out"].rearrange("(k p) n -> p k n", p=P)).then_inc(s["w_in"], 16)
                sp.dma_start(rw[:, :, :], io["router_w"].rearrange("(k p) n -> p k n", p=P)).then_inc(s["w_in"], 16)
                sp.dma_start(lnx[:, :], io["rwkv_lnx_w"].partition_broadcast(P)).then_inc(s["w_in"], 16)
                load_rows(0)

                def step(t, b, n, left):
                    freed(sp, s["P_ps"], t, KD)
                    sp.dma_start(cs[:, :, :].rearrange("p k n -> p (k n)"), tile_of(scr["cs"], t)).then_inc(s["cs_in"], 16)
                    sp.wait_ge(s["w_in"], 16 * (KD + 6))
                    freed(sp, s["st_x"], t, 16)
                    sp.wait_ge(s["w_in"], 16 * (KD + 6))
                    freed(sp, s["h2_ok"], t)
                    if left == 0:
                        load_rows(1)
                    sp.dma_start(xx[:, :], tile_of(io["x_all"], t)).then_inc(s["x_in"], 16)
                    if left > 0:
                        sp.wait_ge(s["w_in"], 16 * (KD + 6))
                        after(sp, s["yT_ps"], t)
                        load_y(t + 1)
                        sp.wait_ge(s["w_in"], 16 * (KD + 6))
                        after(sp, s["G_ps"], t, KD)
                        load_h(t + 1)
                    after(sp, s["x2_ok"], t)
                    sp.dma_start(tile_of(scr["x2"], t), xx[:, :]).then_inc(s["st_x"], 16)
                    sp.wait_ge(s["w_in"], 16 * (KD + 6))
                    after(sp, s["h2_ok"], t)
                    sp.dma_start(tile_of(scr["h2"], t), h2[:, :]).then_inc(s["st_h"], 16)

                tiles(sp, step)
                sp.wait_ge(s["st_x"], 16 * NT)
                sp.wait_ge(s["st_h"], 16 * NT)

            @block.scalar
            def _(act):
                a = nc.scalar.activation

                def scan_norm(t, part):
                    if part == 0:
                        after(act, s["yc_ok"], t)
                        a(ya[:, :], yb[:, :], ACT.Square).then_inc(s["sq_ok"], 1)
                    else:
                        after(act, s["ve_ok"], t)
                        a(s8[3][:, :], s8[2][:, :], ACT.Sqrt).then_inc(s["sd_ok"], 1)

                scan_norm(0, 0)
                scan_norm(0, 1)

                def step(t, b, n, left):
                    for j in range(KD):
                        if j == 2:
                            after(act, s["yT_ps"], t)
                            freed(act, s["P_ps"], t, KD)
                            a(yT[:, :, :].rearrange("p k n -> p (k n)"), ps[:, TB, :], ACT.Copy).then_inc(s["yT_ok"], 1)
                        after(act, s["G_ps"], t * KD + j)
                        if j >= 2:
                            act.wait_ge(s["mg_ok"], t * KD + j - 1)
                        else:
                            freed(act, s["mg_ok"], t, KD)
                        a(Gs[j % 2][:, :], ps[:, GB[j % 3], 0:3 * P], ACT.Sigmoid).then_inc(s["G_ok"], 1)
                        if left > 0 and j == 4:
                            scan_norm(t + 1, 0)
                    if left > 0:
                        scan_norm(t + 1, 1)
                    after(act, s["x2_ok"], t)
                    after(act, s["mix_ok"], t, 2)
                    a(h2[:, :], xx[:, :], ACT.Square, accum_out=s1[0]).then_inc(s["ss_ok"], 1)
                    after(act, s["ms_ok"], t)
                    a(s1[2], s1[1], ACT.Sqrt).then_inc(s["sx_ok"], 1)

                tiles(act, step)

            @block.gpsimd
            def _(pool):
                g = nc.gpsimd
                pool.wait_ge(s["w_in"], 16 * (KD + 6))

                def scan_sum(t):
                    after(pool, s["y_in"], t, 48)
                    g.tensor_tensor(ya[:, :], ya[:, :], yb[:, :], ALU.add).then_inc(s["ysum"], 1)

                def scan_out(t):
                    after(pool, s["yn_ok"], t)
                    g.tensor_tensor(yb[:, :], yb[:, :], lnx[:, :], ALU.mult).then_inc(s["yw_ok"], 1)
                    after(pool, s["yw_ok"], t)
                    g.tensor_tensor(yb[:, :], yb[:, :], ob[:, 0, :], ALU.add).then_inc(s["yo_ok"], 1)
                    after(pool, s["yo_ok"], t)
                    g.tensor_tensor(ya[:, :], yb[:, :], ob[:, 1, :], ALU.mult).then_inc(s["yf_ok"], 1)

                scan_sum(0)
                scan_out(0)

                def step(t, b, n, left):
                    if left > 0:
                        scan_sum(t + 1)
                        scan_out(t + 1)
                    after(pool, s["x_in"], t, 16)
                    after(pool, s["mix_ok"], t, 2)
                    g.tensor_tensor(xx[:, :], xx[:, :], h2[:, :], ALU.add).then_inc(s["x2_ok"], 1)
                    after(pool, s["hm_ok"], t)
                    g.tensor_tensor(h2[:, :], h2[:, :], sh2, ALU.add).then_inc(s["h2_ok"], 1)

                tiles(pool, step)

            @block.vector
            def _(dve):
                v = nc.vector
                dve.wait_ge(s["w_in"], 16 * (KD + 6))

                def by_head(ap):
                    return ap.rearrange("p (h n) -> p h n", h=H)

                def wide(ap):
                    return ap.unsqueeze(2).broadcast_to([P, H, N])

                def scan_center(t):
                    after(dve, s["ysum"], t)
                    v.reduce_sum(s8[0][:, :], by_head(ya[:, :]), axis=X_AXIS).then_inc(s["m_ok"], 1)
                    after(dve, s["m_ok"], t)
                    v.tensor_scalar(s8[5][:, :], s8[0][:, :], 1.0 / N, None, ALU.mult).then_inc(s["mean_ok"], 1)
                    after(dve, s["mean_ok"], t)
                    v.tensor_tensor(by_head(yb[:, :]), by_head(ya[:, :]), wide(s8[5][:, :]), ALU.subtract)\
                        .then_inc(s["yc_ok"], 1)

                def scan_variance(t):
                    after(dve, s["sq_ok"], t)
                    v.reduce_sum(s8[1][:, :], by_head(ya[:, :]), axis=X_AXIS).then_inc(s["v_ok"], 1)
                    after(dve, s["v_ok"], t)
                    v.tensor_scalar(s8[2][:, :], s8[1][:, :], 1.0 / N, GN_EPS, ALU.mult, ALU.add).then_inc(s["ve_ok"], 1)

                def scan_scale(t):
                    after(dve, s["sd_ok"], t)
                    v.reciprocal(s8[4][:, :], s8[3][:, :]).then_inc(s["rs_ok"], 1)
                    after(dve, s["rs_ok"], t)
                    v.tensor_tensor(by_head(yb[:, :]), by_head(yb[:, :]), wide(s8[4][:, :]), ALU.mult)\
                        .then_inc(s["yn_ok"], 1)

                def tail(t):
                    for half in range(2):
                        after(dve, s["hT_ps"], t * 2 + half)
                        v.tensor_copy(h2T[:, 4 * half:4 * half + 4, :].rearrange("p k n -> p (k n)"), ps[:, TB, :])\
                            .then_inc(s["hT_ok"], 1)
                    after(dve, s["lg_ps"], t)
                    v.tensor_copy(K["logits"][:, bass.ds(t * NEXP, NEXP)], ps[:, TB, 0:NEXP]).then_inc(s["lg_ok"], 1)

                scan_center(0)
                scan_variance(0)
                scan_scale(0)

                def step(t, b, n, left):
                    if not first(t):
                        tail(t - 1)
                    for j in range(KD):
                        after(dve, s["P_ps"], t * KD + j)
                        after(dve, s["G_ok"], t * KD + j)
                        v.tensor_tensor(Ms[j % 2][:, :], Gs[j % 2][:, :], ps[:, PB[j % 2], 0:3 * P], ALU.mult)\
                            .then_inc(s["M_ok"], 1)
                        after(dve, s["M_ok"], t * KD + j)
                        v.reduce_sum(mT[:, j, :], Ms[j % 2][:, :].rearrange("p (b n) -> p n b", b=3), axis=X_AXIS)\
                            .then_inc(s["mg_ok"], 1)
                        if left > 0 and j in (3, 5):
                            (scan_center if j == 3 else scan_variance)(t + 1)
                    if left > 0:
                        scan_scale(t + 1)
                    freed(dve, s["st_h"], t, 16)
                    dve.wait_ge(s["rp_in"], 96 if left == 0 else 48)
                    for i in range(2):
                        after(dve, s["W_ps"], t * 2 + i)
                        if not first(t) and i == 0:
                            freed(dve, s["hT_ps"], t, 2)
                        v.tensor_tensor(h2[:, i * 512:(i + 1) * 512], ga1[:, i * 512:(i + 1) * 512], ps[:, WB[i], :],
                                        ALU.mult).then_inc(s["mix_ok"], 1)
                    after(dve, s["ss_ok"], t)
                    v.tensor_scalar(s1[1], s1[0], 1.0 / D, EPS, ALU.mult, ALU.add).then_inc(s["ms_ok"], 1)
                    after(dve, s["sx_ok"], t)
                    v.reciprocal(s1[3], s1[2]).then_inc(s["rx_ok"], 1)
                    after(dve, s["rx_ok"], t)
                    after(dve, s["x2_ok"], t)
                    v.scalar_tensor_tensor(h2[:, :], xx[:, :], s1[3], g2, ALU.mult, ALU.mult)\
                        .then_inc(s["hm_ok"], 1)
                    if left == 0:
                        tail(t)

                tiles(dve, step)
                dve.wait_ge(s["lg_ok"], NT)

            @block.tensor
            def _(pe):
                def mm(out, lhsT, rhs, start, stop):
                    return nc.tensor.matmul(out, lhsT, rhs, start=start, stop=stop)

                pe.wait_ge(s["w_in"], 16 * (KD + 6))

                def tail(t):
                    for half in range(2):
                        after(pe, s["h2_ok"], t)
                        if half == 0:
                            after(pe, s["yT_ok"], t)
                            freed(pe, s["lg_ok"], t)
                            after(pe, s["W_ps"], t * 2 + 1)
                        else:
                            after(pe, s["hT_ok"], t * 2)
                        for k in range(4):
                            c = (4 * half + k) * P
                            ins = nc.tensor.transpose(ps[:, TB, k * P:(k + 1) * P], h2[:, c:c + P], ident)
                        ins.then_inc(s["hT_ps"], 1)
                    after(pe, s["hT_ok"], t, 2)
                    for k in range(KD):
                        ins = mm(ps[:, TB, 0:NEXP], h2T[:, k, :], rw[:, k, :], k == 0, k == KD - 1)
                    ins.then_inc(s["lg_ps"], 1)

                def step(t, b, n, left):
                    def gates(j):
                        if j >= 3:
                            pe.wait_ge(s["G_ok"], t * KD + j - 2)
                        else:
                            freed(pe, s["G_ok"], t, KD)
                        for br in range(3):
                            c = br * D + j * P
                            for k in range(KD):
                                ins = mm(ps[:, GB[j % 3], br * P:(br + 1) * P], wg[:, k, c:c + P], hT[:, k, :],
                                         k == 0, k == KD - 1)
                        ins.then_inc(s["G_ps"], 1)

                    def project(j):
                        if j >= 2:
                            pe.wait_ge(s["M_ok"], t * KD + j - 1)
                        else:
                            freed(pe, s["M_ok"], t, KD)
                        parts = [(0, [(0, cs[:, 0, :]), (1, cs[:, 1, :])]),
                                 (1, [(2 + i, yT[:, i, :]) for i in range(4)]),
                                 (2, [(6, cs[:, 2, :]), (7, cs[:, 3, :])])]
                        for br, terms in parts:
                            for i, (k, rhs) in enumerate(terms):
                                ins = mm(ps[:, PB[j % 2], br * P:(br + 1) * P], wp[:, k, j * P:(j + 1) * P], rhs,
                                         i == 0, i == len(terms) - 1)
                        ins.then_inc(s["P_ps"], 1)

                    after(pe, s["h_in"], t, 16)
                    gates(0)
                    gates(1)
                    if not first(t):
                        tail(t - 1)
                        freed(pe, s["lg_ok"], t)
                    after(pe, s["yf_ok"], t)
                    for k in range(4):
                        ins = nc.tensor.transpose(ps[:, TB, k * P:(k + 1) * P], ya[:, k * P:(k + 1) * P], ident)
                    ins.then_inc(s["yT_ps"], 1)
                    gates(2)
                    after(pe, s["yT_ok"], t)
                    after(pe, s["cs_in"], t, 16)
                    for j in range(KD):
                        project(j)
                        if j + 3 < KD:
                            gates(j + 3)
                    after(pe, s["mg_ok"], t, KD)
                    for i in range(2):
                        freed(pe, s["mix_ok"], t, 2)
                        for k in range(KD):
                            ins = mm(ps[:, WB[i], :], mT[:, k, :], wo[:, k, i * 512:(i + 1) * 512], k == 0, k == KD - 1)
                        ins.then_inc(s["W_ps"], 1)
                    if left == 0:
                        tail(t)

                tiles(pe, step)


def stage_route(nc, io, scr, K):
    with ExitStack() as ctx:
        def sb(name, shape, dt=F32):
            return ctx.enter_context(nc.sbuf_tensor(name, shape, dt))

        sem = Sems(nc, ctx)
        ps = ctx.enter_context(nc.psum_tensor("r_ps", [P, 3, 512], F32))
        BIG = 1e30
        E, G, M = NEXP, 4, 4
        rc = sb("r_const", [P, ROUTE_COLS])
        cmask = sb("r_up", [P, P])
        ones = sb("r_ones", [P, P])
        zero = sb("r_zero", [NB, P])
        rb = sb("r_rb", [P, E])
        sc, bi, mb, mb2, key, eq, oh, tmp, base = (sb("r_" + n, [P, NT, E]) for n in (
            "sc", "bi", "mb", "mb2", "key", "eq", "oh", "tmp", "base"))
        ohk = [sb(f"r_oh{k}", [P, NT, E]) for k in range(2)]
        pr = sb("r_pr", [P, NT * G, 6])
        gs, gk, gq = (sb("r_" + n, [P, NT, G]) for n in ("gs", "gk", "gq"))
        mx = sb("r_mx", [P, NT])
        g12 = sb("r_g12", [P, 2, NT])
        gsum, grec = sb("r_gsum", [P, NT]), sb("r_grec", [P, NT])
        carry = sb("r_carry", [P, NT + 1, E])
        cmp_ = sb("r_cmp", [P, E, NT])
        nb, ends, pst = sb("r_nb", [P, E]), sb("r_ends", [P, E]), sb("r_pst", [P, E])
        tri = sb("r_tri", [P, E, E])
        bc = sb("r_bc", [1, NB, E])
        be = sb("r_be", [1, NB])
        dst = sb("r_dst", [P, 2, NT])
        srow = sb("r_srow", [NB, P])
        iota4, iota16 = rc[:, 0:4], rc[:, 4:20]
        j128, iotab = rc[:, 20:20 + NT], rc[:, 20 + NT:20 + NT + NB]
        incl = rc[:, 20 + NT + NB:20 + NT + NB + E * E]
        tok = rc[:, 20 + NT + NB + E * E:ROUTE_COLS]

        c_in, sig_ok, step_ok, cnt_ps, ones_ok, zeroed = (sem("r_" + n) for n in (
            "c_in", "sig_ok", "step_ok", "cnt_ps", "ones_ok", "zeroed"))
        scat, s_in, sT, plan_ok, zstored = (sem("r_" + n) for n in ("scat", "s_in", "sT", "plan_ok", "zstored"))

        def wide(ap, n):
            return ap.unsqueeze(2).broadcast_to([P, ap.shape[1], n])

        def over(ap, m):
            return ap.unsqueeze(1).broadcast_to([P, m, ap.shape[1]])

        with nc.Block() as block:
            @block.sync
            def _(sp):
                sp.dma_start(rc[:, :], io["route_consts"]).then_inc(c_in, 16)
                sp.dma_start(cmask[:, :], io["consts"][:, UP, :]).then_inc(c_in, 16)
                sp.dma_start(rb[:, :], io["router_b"].partition_broadcast(P)).then_inc(c_in, 16)
                sp.wait_ge(zeroed, 1)
                sp.dma_start(scr["src"].rearrange("(b p) a -> b (p a)", p=P), zero[:, :]).then_inc(zstored, 16)
                sp.wait_ge(scat, 16 * 2 * NT)
                sp.dma_start(srow[:, :], scr["src"].rearrange("(b p) a -> b (p a)", p=P)).then_inc(s_in, 16)
                sp.wait_ge(s_in, 16)

            @block.scalar
            def _(act):
                nc.scalar.activation(sc[:, :, :].rearrange("p t e -> p (t e)"), K["logits"][:, :], ACT.Sigmoid)\
                    .then_inc(sig_ok, 1)

            @block.gpsimd
            def _(pool):
                nc.gpsimd.memset(zero[:, :], 0.0).then_inc(zeroed, 1)
                nc.gpsimd.memset(ones[:, :], 1.0).then_inc(ones_ok, 1)
                pool.wait_ge(zstored, 16)
                pool.wait_ge(plan_ok, 1)
                for t in range(NT):
                    for k in range(2):
                        pool.indirect_dma_start(scr["src"], bass.IndirectOffsetOnAxis(K["dest"][:, k, t:t + 1], 0),
                                                tok[:, t:t + 1], None).then_inc(scat, 16)
                pool.wait_ge(scat, 16 * 2 * NT)

            @block.tensor
            def _(pe):
                pe.wait_ge(step_ok, ROUTE_OH)
                pe.wait_ge(ones_ok, 1)
                pe.wait_ge(c_in, 48)
                ohv = oh[:, :, :].rearrange("p t e -> p (t e)")
                nc.tensor.matmul(ps[:, 0, 0:NT * E], cmask[:, :], ohv, start=True, stop=True)
                nc.tensor.matmul(ps[:, 1, 0:NT * E], ones[:, :], ohv, start=True, stop=True).then_inc(cnt_ps, 1)
                pe.wait_ge(s_in, 16)
                nc.tensor.transpose(ps[:, 2, 0:NB], srow[:, :], K["ident"][0:NB, 0:NB]).then_inc(sT, 1)

            @block.vector
            def _(dve):
                v = nc.vector
                count = [0]

                def then(ins):
                    count[0] += 1
                    ins.then_inc(step_ok, 1)
                    dve.wait_ge(step_ok, count[0])

                dve.wait_ge(c_in, 48)
                dve.wait_ge(sig_ok, 1)
                then(v.tensor_tensor(bi[:, :, :], sc[:, :, :], over(rb[:, :], NT), ALU.add))
                b4 = bi[:, :, :].rearrange("p t (g m) -> p (t g) m", m=M)
                then(v.tensor_tensor(pr[:, :, 0:3], b4[:, :, 0:3], b4[:, :, 1:4], ALU.add))
                then(v.tensor_tensor(pr[:, :, 3:5], b4[:, :, 0:2], b4[:, :, 2:4], ALU.add))
                then(v.tensor_tensor(pr[:, :, 5:6], b4[:, :, 0:1], b4[:, :, 3:4], ALU.add))
                then(v.reduce_max(gs[:, :, :].rearrange("p t g -> p (t g)"), pr[:, :, :], axis=X_AXIS))

                def first_max(values, iota, scale, eq_, key_, out):
                    n = values.shape[2]
                    then(v.reduce_max(mx[:, :], values, axis=X_AXIS))
                    then(v.tensor_tensor(eq_, values, wide(mx[:, :], n), ALU.is_equal))
                    then(v.scalar_tensor_tensor(key_, eq_, scale, over(iota, NT), ALU.mult, ALU.subtract))
                    then(v.reduce_max(mx[:, :], key_, axis=X_AXIS))
                    then(v.tensor_tensor(out, key_, wide(mx[:, :], n), ALU.is_equal))

                first_max(gs[:, :, :], iota4, 8.0, gq[:, :, :], gk[:, :, :], gs[:, :, :])
                then(v.tensor_scalar(gq[:, :, :], gs[:, :, :], BIG, -BIG, ALU.mult, ALU.add))
                then(v.tensor_tensor(mb[:, :, :].rearrange("p t (g m) -> p (t g) m", m=M), b4,
                                     wide(gq[:, :, :].rearrange("p t g -> p (t g)"), M), ALU.add))
                first_max(mb[:, :, :], iota16, 32.0, eq[:, :, :], key[:, :, :], ohk[0][:, :, :])
                then(v.scalar_tensor_tensor(mb2[:, :, :], ohk[0][:, :, :], -2 * BIG, mb[:, :, :], ALU.mult, ALU.add))
                first_max(mb2[:, :, :], iota16, 32.0, eq[:, :, :], key[:, :, :], ohk[1][:, :, :])
                then(v.tensor_tensor(oh[:, :, :], ohk[0][:, :, :], ohk[1][:, :, :], ALU.add))
                assert count[0] == ROUTE_OH
                for k in range(2):
                    then(v.tensor_tensor(tmp[:, :, :], sc[:, :, :], ohk[k][:, :, :], ALU.mult))
                    then(v.reduce_sum(g12[:, k, :], tmp[:, :, :], axis=X_AXIS))
                then(v.tensor_tensor(gsum[:, :], g12[:, 0, :], g12[:, 1, :], ALU.add))
                then(v.reciprocal(grec[:, :], gsum[:, :]))
                then(v.tensor_tensor(K["gate"][:, :, :], g12[:, :, :], over(grec[:, :], 2), ALU.mult))
                then(v.memset(carry[:, 0, :], 0.0))
                dve.wait_ge(cnt_ps, 1)
                for t in range(NT):
                    then(v.tensor_tensor(carry[:, t + 1, :], carry[:, t, :], ps[:, 1, t * E:(t + 1) * E], ALU.add))
                then(v.tensor_tensor(cmp_[:, :, :], wide(carry[:, NT, :], NT), over(j128, E), ALU.is_gt))
                then(v.reduce_sum(nb[:, :], cmp_[:, :, :], axis=X_AXIS))
                then(v.tensor_tensor(tri[:, :, :], over(nb[:, :], E), incl.rearrange("p (a b) -> p a b", a=E), ALU.mult))
                then(v.reduce_sum(ends[:, :], tri[:, :, :], axis=X_AXIS))
                then(v.tensor_tensor(pst[:, :], ends[:, :], nb[:, :], ALU.subtract))
                then(v.tensor_scalar(pst[:, :], pst[:, :], float(P), None, ALU.mult))
                then(v.tensor_tensor(bc[:, :, :], iotab[0:1, :].unsqueeze(2).broadcast_to([1, NB, E]),
                                     ends[0:1, :].unsqueeze(1).broadcast_to([1, NB, E]), ALU.is_ge))
                then(v.reduce_sum(be[:, :], bc[:, :, :], axis=X_AXIS))
                then(v.tensor_scalar(be[:, :], be[:, :], float(E - 1), None, ALU.min))
                then(v.tensor_scalar(K["plan"][:, 0, 0:NB], be[:, :], 1.0, None, ALU.add))
                then(v.tensor_scalar(bc[:, :, 0], be[:, :], float(E // 4), None, ALU.is_ge))
                for i in (2, 3):
                    then(v.tensor_scalar(bc[:, :, 1], be[:, :], float(i * E // 4), None, ALU.is_ge))
                    then(v.tensor_tensor(bc[:, :, 0], bc[:, :, 0], bc[:, :, 1], ALU.add))
                then(v.scalar_tensor_tensor(K["plan"][:, 1, 0:NB], bc[:, :, 0], -float(WSLOTS), be[:, :], ALU.mult, ALU.add))
                then(v.tensor_scalar(K["plan"][:, 2, 0:E], ends[0:1, :], 1.0, None, ALU.add))
                then(v.tensor_tensor(base[:, :, :], carry[:, 0:NT, :],
                                     ps[:, 0, 0:NT * E].rearrange("p (t e) -> p t e", t=NT), ALU.add))
                then(v.tensor_tensor(base[:, :, :], base[:, :, :], over(pst[:, :], NT), ALU.add))
                for k in range(2):
                    then(v.tensor_tensor(tmp[:, :, :], base[:, :, :], ohk[k][:, :, :], ALU.mult))
                    then(v.reduce_sum(dst[:, k, :], tmp[:, :, :], axis=X_AXIS))
                v.tensor_copy(K["dest"][:, :, :], dst[:, :, :]).then_inc(plan_ok, 1)
                dve.wait_ge(sT, 1)
                v.tensor_copy(K["src"][:, :], ps[:, 2, 0:NB]).then_inc(plan_ok, 1)
                dve.wait_ge(plan_ok, 2)


def stage_experts(nc, io, scr, K):
    with ExitStack() as ctx:
        def sb(name, shape):
            return ctx.enter_context(nc.sbuf_tensor(name, shape, F32))

        sem = Sems(nc, ctx)
        ps = ctx.enter_context(nc.psum_tensor("e_ps", [P, 8, 512], F32))
        ident = K["ident"][:, :]
        S = 4
        wu = sb("e_wu", [P, WSLOTS, KD, 2 * FE])
        wd = sb("e_wd", [P, WSLOTS, 2, D])
        X = [sb(f"e_x{i}", [P, D]) for i in range(S)]
        xT = [sb(f"e_xT{i}", [P, KD, P]) for i in range(2)]
        sg = sb("e_sg", [P, FE])
        sl = sb("e_sl", [P, FE])
        av = sb("e_av", [P, FE])
        aT = sb("e_aT", [P, 2, P])
        yo = [sb(f"e_yo{i}", [P, D]) for i in range(2)]
        w_in, x_in = [sem(f"e_w_in{i}") for i in range(WSLOTS)], [sem(f"e_x_in{i}") for i in range(S)]
        w_ok = sem("e_w_ok")
        y_st = [sem(f"e_y_st{i}") for i in range(2)]
        xT_ps, xT_ok, up_ps, sg_ok, sl_ok, a_ok, aT_ps, aT_ok, y_ps, y_ok = (sem("e_" + n) for n in (
            "xT_ps", "xT_ok", "up_ps", "sg_ok", "sl_ok", "a_ok", "aT_ps", "aT_ok", "y_ps", "y_ok"))
        TB, UB, AB, YB = (0, 1), (2, 3), 4, (5, 6)

        def blocks(e, step):
            for i in range(S):
                step(i, i, 0, False)
            with e.Fori(1, NB // S) as j:
                for i in range(S):
                    step(j * S + i, i, j, False)
            step(NB - 1, 0, NB // S, True)


        with nc.Block() as block:
            @block.sync
            def _(sp):
                for e in range(NEXP + 1):
                    if e < NEXP:
                        i = e % WSLOTS
                        if e >= WSLOTS:
                            ended = sp.value_load(K["plan"][0:1, 2, e - WSLOTS:e - WSLOTS + 1], min_val=1, max_val=NB + 1)
                            sp.wait_ge(y_ps, ended)
                        sp.dma_start(wu[:, i, :, 0:FE], io["exp_w1"][e].rearrange("(k p) n -> p k n", p=P))\
                            .then_inc(w_in[i], 16)
                        sp.dma_start(wu[:, i, :, FE:2 * FE], io["exp_w3"][e].rearrange("(k p) n -> p k n", p=P))\
                            .then_inc(w_in[i], 16)
                        sp.dma_start(wd[:, i, :, :], io["exp_w2"][e].rearrange("(k p) n -> p k n", p=P))\
                            .then_inc(w_in[i], 16)
                    if e >= 1:
                        sp.wait_ge(w_in[(e - 1) % WSLOTS], 48 * ((e - 1) // WSLOTS + 1))
                        sp.nop().then_inc(w_ok, 1)

            @block.gpsimd
            def _(pool):
                for b in range(NB):
                    if b >= S:
                        pool.wait_ge(xT_ps, b - S + 1)
                    pool.indirect_dma_start(X[b % S][:, :], None, scr["h2"].rearrange("t p n -> (t p) n"),
                                            bass.IndirectOffsetOnAxis(K["src"][:, b:b + 1], 0)).then_inc(x_in[b % S], 16)

            @block.scalar
            def _(act):
                a = nc.scalar.activation

                def rows(b, i):
                    after(act, xT_ps, b)
                    a(xT[i % 2][:, 0:4, :].rearrange("p k n -> p (k n)"), ps[:, TB[0], :], ACT.Copy).then_inc(xT_ok, 1)

                rows(0, 0)

                def finish(b, i, n):
                    after(act, y_ps, b + 1)
                    freed(act, y_st[i % 2], n * 2 + i // 2, 16)
                    a(yo[i % 2][:, 0:512], ps[:, YB[0], :], ACT.Copy).then_inc(y_ok, 1)
                    after(act, y_ok, b, 2)
                    act.dma_start(scr["yr"][bass.ds(b, 1)].rearrange("a p n -> (a p) n"), yo[i % 2][:, :])\
                        .then_inc(y_st[i % 2], 16)

                def step(b, i, n, last):
                    after(act, up_ps, b)
                    freed(act, sl_ok, b)
                    a(sg[:, :], ps[:, UB[i % 2], 0:FE], ACT.Sigmoid).then_inc(sg_ok, 1)
                    if not last:
                        rows(b + 1, i + 1)
                    if not (isinstance(b, int) and b == 0):
                        finish(b - 1, i - 1, n)

                blocks(act, step)
                finish(NB - 1, 0, NB // S)
                act.wait_ge(y_st[0], 16 * 25)
                act.wait_ge(y_st[1], 16 * 24)

            @block.vector
            def _(dve):
                v = nc.vector

                def rows(b, i):
                    after(dve, xT_ps, b)
                    v.tensor_copy(xT[i % 2][:, 4:8, :].rearrange("p k n -> p (k n)"), ps[:, TB[1], :]).then_inc(xT_ok, 1)

                rows(0, 0)

                def activated(b):
                    after(dve, aT_ps, b)
                    freed(dve, y_ps, b + 1)
                    v.tensor_copy(aT[:, :, :].rearrange("p k n -> p (k n)"), ps[:, AB, 0:2 * P]).then_inc(aT_ok, 1)

                def finish(b, i, n):
                    after(dve, y_ps, b + 1)
                    freed(dve, y_st[i % 2], n * 2 + i // 2, 16)
                    v.tensor_copy(yo[i % 2][:, 512:1024], ps[:, YB[1], :]).then_inc(y_ok, 1)

                def step(b, i, n, last):
                    first = isinstance(b, int) and b == 0
                    if not first:
                        activated(b - 1)
                    after(dve, sg_ok, b)
                    v.tensor_tensor(sl[:, :], sg[:, :], ps[:, UB[i % 2], 0:FE], ALU.mult).then_inc(sl_ok, 1)
                    after(dve, sl_ok, b)
                    freed(dve, aT_ps, b)
                    v.tensor_tensor(av[:, :], sl[:, :], ps[:, UB[i % 2], FE:2 * FE], ALU.mult).then_inc(a_ok, 1)
                    if not last:
                        rows(b + 1, i + 1)
                    if not first:
                        finish(b - 1, i - 1, n)

                blocks(dve, step)
                activated(NB - 1)
                finish(NB - 1, 0, NB // S)

            @block.tensor
            def _(pe):
                def mm(out, lhsT, rhs, start, stop):
                    return nc.tensor.matmul(out, lhsT, rhs, start=start, stop=stop)

                def rows(b, i, n):
                    after(pe, x_in[i], n, 16)
                    freed(pe, xT_ok, b, 2)
                    for k in range(KD):
                        ins = nc.tensor.transpose(ps[:, TB[k // 4], (k % 4) * P:(k % 4 + 1) * P],
                                                  X[i][:, k * P:(k + 1) * P], ident)
                    ins.then_inc(xT_ps, 1)

                pe.nop().then_inc(y_ps, 1)
                rows(0, 0, 0)

                def activated(b):
                    after(pe, a_ok, b)
                    freed(pe, aT_ok, b)
                    for k in range(2):
                        ins = nc.tensor.transpose(ps[:, AB, k * P:(k + 1) * P], av[:, k * P:(k + 1) * P], ident)
                    ins.then_inc(aT_ps, 1)

                def down(b, slot):
                    after(pe, aT_ok, b)
                    freed(pe, y_ok, b, 2)
                    for half in range(2):
                        for k in range(2):
                            ins = mm(ps[:, YB[half], :], aT[:, k, :], wd[:, bass.ds(slot, 1), k, half * 512:(half + 1) * 512],
                                     k == 0, k == 1)
                    ins.then_inc(y_ps, 1)

                def slot_of(b):
                    return pe.value_load(K["plan"][0:1, 1, bass.ds(b, 1)], min_val=0, max_val=WSLOTS - 1)

                def step(b, i, n, last):
                    first = isinstance(b, int) and b == 0
                    place = pe.value_load(K["plan"][0:1, 0, bass.ds(b, 1)], min_val=1, max_val=NEXP)
                    slot = slot_of(b)
                    before = None if first else slot_of(b - 1)
                    pe.wait_ge(w_ok, place)
                    after(pe, xT_ok, b, 2)
                    freed(pe, a_ok, b)
                    for k in range(KD):
                        ins = mm(ps[:, UB[i % 2], :], xT[i % 2][:, k, :], wu[:, bass.ds(slot, 1), k, :], k == 0, k == KD - 1)
                    ins.then_inc(up_ps, 1)
                    if not first:
                        activated(b - 1)
                    if not last:
                        rows(b + 1, (i + 1) % S, n if i < S - 1 else n + 1)
                    if not first:
                        down(b - 1, before)

                blocks(pe, step)
                activated(NB - 1)
                down(NB - 1, slot_of(NB - 1))


def stage_combine(nc, io, scr, K):
    with ExitStack() as ctx:
        def sb(name, shape):
            return ctx.enter_context(nc.sbuf_tensor(name, shape, F32))

        sem = Sems(nc, ctx)
        r = [[sb(f"f_r{k}{i}", [P, D]) for i in range(2)] for k in range(2)]
        x = [sb(f"f_x{i}", [P, D]) for i in range(2)]
        g1 = [sb(f"f_g{i}", [P, 2]) for i in range(2)]
        acc, acc2, acc3, x3, sq = (sb("f_" + n, [P, D]) for n in ("acc", "acc2", "acc3", "x3", "sq"))
        yo = [sb(f"f_yo{i}", [P, D]) for i in range(2)]
        ga2 = sb("f_ga2", [P, 2, D])
        fg = sb("f_fg", [P, D])
        ss, ms, sd, rs = (sb("f_" + n, [P, 1]) for n in ("ss", "ms", "sd", "rs"))
        p_in = sem("f_p_in")
        r_in, x_in, y_st = ([sem(f"f_{n}{i}") for i in range(2)] for n in ("r_in", "x_in", "y_st"))
        g_ok, a_ok, b_ok, c_ok, x3_ok, ss_ok, ms_ok, sd_ok, rs_ok, y_ok = (sem("f_" + n) for n in (
            "g_ok", "a_ok", "b_ok", "c_ok", "x3_ok", "ss_ok", "ms_ok", "sd_ok", "rs_ok", "y_ok"))

        def tile_of(ap, t):
            return ap[bass.ds(t, 1)].rearrange("a p n -> (a p) n")

        with nc.Block() as block:
            @block.sync
            def _(sp):
                for v in range(2):
                    sp.dma_start(ga2[:, v, :], scr["mod"][v, 5 * D:6 * D].partition_broadcast(P)).then_inc(p_in, 16)
                sp.dma_start(fg[:, :], io["final_g"].partition_broadcast(P)).then_inc(p_in, 16)
                for b in range(2):
                    sp.dma_start(x[b][:, :], tile_of(scr["x2"], b)).then_inc(x_in[b], 16)

                def step(t, b, n, left):
                    if left >= 2:
                        sp.wait_ge(p_in, 48)
                        after(sp, x3_ok, t)
                        sp.dma_start(x[b][:, :], tile_of(scr["x2"], t + 2)).then_inc(x_in[b], 16)
                    sp.wait_ge(p_in, 48)
                    after(sp, y_ok, t)
                    sp.dma_start(tile_of(io["y_all"], t), yo[b][:, :]).then_inc(y_st[b], 16)

                over_tiles(sp, step)
                sp.wait_ge(y_st[0], 16 * 9)
                sp.wait_ge(y_st[1], 16 * 8)

            @block.gpsimd
            def _(pool):
                rows = scr["yr"].rearrange("b p n -> (b p) n")
                for t in range(NT):
                    if t >= 2:
                        pool.wait_ge(b_ok, t - 1)
                    for k in range(2):
                        pool.indirect_dma_start(r[k][t % 2][:, :], None, rows,
                                                bass.IndirectOffsetOnAxis(K["dest"][:, k, t:t + 1], 0))\
                            .then_inc(r_in[t % 2], 16)

            @block.scalar
            def _(act):
                def step(t, b, n, left):
                    after(act, x3_ok, t)
                    nc.scalar.activation(sq[:, :], x3[:, :], ACT.Square, accum_out=ss[:, :]).then_inc(ss_ok, 1)
                    after(act, ms_ok, t)
                    nc.scalar.activation(sd[:, :], ms[:, :], ACT.Sqrt).then_inc(sd_ok, 1)

                over_tiles(act, step)

            @block.vector
            def _(dve):
                v = nc.vector
                dve.wait_ge(p_in, 48)

                def step(t, b, n, left):
                    v.tensor_copy(g1[b][:, :], K["gate"][:, :, bass.ds(t, 1)].rearrange("p k a -> p (k a)"))\
                        .then_inc(g_ok, 1)
                    after(dve, g_ok, t)
                    after(dve, r_in[b], n, 32)
                    v.tensor_scalar(acc[:, :], r[0][b][:, :], g1[b][:, 0:1], None, ALU.mult).then_inc(a_ok, 1)
                    after(dve, a_ok, t)
                    v.scalar_tensor_tensor(acc2[:, :], r[1][b][:, :], g1[b][:, 1:2], acc[:, :], ALU.mult, ALU.add)\
                        .then_inc(b_ok, 1)
                    after(dve, b_ok, t)
                    v.tensor_tensor(acc3[:, :], acc2[:, :], ga2[:, int(left == 0), :], ALU.mult).then_inc(c_ok, 1)
                    after(dve, c_ok, t)
                    after(dve, x_in[b], n, 16)
                    v.tensor_tensor(x3[:, :], acc3[:, :], x[b][:, :], ALU.add).then_inc(x3_ok, 1)
                    after(dve, ss_ok, t)
                    v.tensor_scalar(ms[:, :], ss[:, :], 1.0 / D, EPS, ALU.mult, ALU.add).then_inc(ms_ok, 1)
                    after(dve, sd_ok, t)
                    v.reciprocal(rs[:, :], sd[:, :]).then_inc(rs_ok, 1)
                    after(dve, rs_ok, t)
                    freed(dve, y_st[b], n, 16)
                    v.scalar_tensor_tensor(yo[b][:, :], x3[:, :], rs[:, :], fg[:, :], ALU.mult, ALU.mult)\
                        .then_inc(y_ok, 1)

                over_tiles(dve, step)


def program(nc, io, scr):
    with ExitStack() as ctx:
        K = {"logits": ctx.enter_context(nc.sbuf_tensor("logits", [P, NT * NEXP], F32)),
             "ident": ctx.enter_context(nc.sbuf_tensor("ident", [P, P], F32)),
             "pt": ctx.enter_context(nc.sbuf_tensor("pt", [P, 118], F32)),
             "gs": ctx.enter_context(nc.sbuf_tensor("gs", [P, 2, 2, KD], F32))}
        stage_modulation(nc, io, scr, K)
        stage_tokens(nc, io, scr, K)
        stage_scan(nc, io, scr, K)
        stage_merge(nc, io, scr, K)
        K["dest"] = ctx.enter_context(nc.sbuf_tensor("dest", [P, 2, NT], U32))
        K["src"] = ctx.enter_context(nc.sbuf_tensor("src", [P, NB], U32))
        K["gate"] = ctx.enter_context(nc.sbuf_tensor("gate", [P, 2, NT], F32))
        K["plan"] = ctx.enter_context(nc.sbuf_tensor("plan", [1, 3, NB], I32))
        stage_route(nc, io, scr, K)
        stage_experts(nc, io, scr, K)
        stage_combine(nc, io, scr, K)


SCRATCH = {"mod": (2, 6 * D), "h": (NT, P, D), "cs": (NT, P, 4 * P), "A": (NT, P, 3 * W), "D0": (NT, P, 3 * W),
           "D1": (NT, P, 3 * W), "O": (NT, P, 2 * W), "Y0": (NT, P, W),
           "Y1": (NT, P, W), "rows": (2, 3, D), "x2": (NT, P, D), "h2": (NT, P, D),
           "src": (NB * P, 1), "yr": (NB, P, D)}
NAMES = ["s_" + n for n in SCRATCH] + ["state_new", "y_all"]


def kernel(**inputs):
    import numpy as _np
    import concourse.bacc as _bacc
    from concourse import mybir as _mybir
    from concourse.bass_utils import run_bass_kernel_spmd as _run

    f = {n: _np.asarray(a) for n, a in inputs.items()}
    a = {
        "x_all": _np.concatenate([f["x_sample"][0], f["x_prompt"][0]]).reshape(NT, P, D),
        "c_all": _np.stack([f["c"][0], f["c_ctx"]]),
        "consts": shape_constants(),
        "route_consts": route_constants(),
        "state_T": f["state_rwkv"][0, 0].reshape(2, 4, 2, N, N).transpose(0, 2, 4, 1, 3).reshape(2, P, 4, N),
        "rwkv_w2": f["rwkv_w2"][0].reshape(P, W),
        "rwkv_a2": f["rwkv_a2"][0].reshape(P, W),
        "rwkv_r_k": f["rwkv_r_k"][0].reshape(W),
        "sgu_wsT": f["sgu_ws"][0].transpose(2, 0, 1),
        "final_g": f["final_g"], "router_w": f["router_w"], "router_b": f["router_b"],
    }
    for n in ("norm1_g", "norm2_g", "ada_w", "ada_b", "w_in", "conv_w", "rwkv_w0", "rwkv_a0", "rwkv_g2", "rwkv_k_k",
              "rwkv_k_a", "rwkv_lnx_w", "rwkv_lnx_b", "sgu_ln_g", "sgu_ln_b", "sgu_bs", "proj_conv", "proj_rwkv",
              "proj_sgu", "w_out", "exp_w1", "exp_w3", "exp_w2"):
        a[n] = f[n][0]
    nc = _bacc.Bacc("TRN2", target_bir_lowering=False, num_devices=1)
    io, arrays = {}, {}
    for n, v in a.items():
        arrays["in_" + n] = _np.ascontiguousarray(v)
        io[n] = nc.dram_tensor("in_" + n, v.shape, _mybir.dt.float32, kind="ExternalInput").ap()
    scr = {n: nc.dram_tensor("s_" + n, shape, _mybir.dt.float32, kind="Internal").ap() for n, shape in SCRATCH.items()}
    for n, shape in (("y_all", (NT, P, D)), ("state_new", (2, P, 4, N))):
        io[n] = nc.dram_tensor(n, shape, _mybir.dt.float32, kind="ExternalOutput").ap()
    program(nc, io, scr)
    r = _run(nc, [arrays], core_ids=[0]).results[0]
    y = r["y_all"].reshape(NT * P, D)
    state = r["state_new"].reshape(2, 2, N, 4, N).transpose(0, 3, 1, 4, 2).reshape(1, 1, 2, H, N, N)
    return y[None, LAT * P:].copy(), y[None, :LAT * P].copy(), _np.ascontiguousarray(state)
```

```python
from contextlib import ExitStack

import numpy as np

import concourse.bass as bass
from concourse import mybir

F32 = mybir.dt.float32
U32, I32 = mybir.dt.uint32, mybir.dt.int32
ALU = mybir.AluOpType
ACT = mybir.ActivationFunctionType
X_AXIS = mybir.AxisListType.X

P = 128
D = 1024
KD = D // P
NT = 17
LAT = 16
H, N = 8, 64
W = H * N
NEXP = 16
FE = 256
EPS = 1e-6
GN_EPS = 64e-5
DECAY = float(np.exp(-0.5))

CB, CC, CX = 0, 256, 512
CR, CK, CV = 768, 1280, 1792
CWLO, CALO, CGLO, CSU, CSV, CGATE = 2304, 2432, 2560, 2688, 2944, 3200

IDENT, LOW, UP, LOWI, UPI = range(5)
CUMI = (5, 6)
LEVEL = [[7 + 7 * d + l for l in range(7)] for d in range(2)]
IND = 21
PAIR = 22
NCONST = 23
NB = (NT * P * 2 + NEXP * (P - 1)) // P
ROUTE_COLS = 20 + NT + NB + NEXP * NEXP + NT
ROUTE_OH = 24
WSLOTS = 4
EARLY = 3


def shape_constants():
    i = np.arange(P)
    r, c = i[:, None], i[None, :]
    m = np.zeros((NCONST, P, P), np.float32)
    m[IDENT] = r == c
    m[LOW], m[UP], m[LOWI], m[UPI] = r > c, r < c, r >= c, r <= c
    half = [(i < 64), (i >= 64)]
    for d in range(2):
        s, t = r, c
        incl = (s <= t) if d == 0 else (s >= t)
        m[CUMI[d]] = -DECAY * (incl.astype(np.float64) - half[d][:, None])
        for l in range(7):
            b = 1 << l
            low = (r // (2 * b) == c // (2 * b)) & ((r // b) % 2 == 1) & ((c // b) % 2 == 0)
            m[LEVEL[d][l]] = low if d == 0 else low.T
        m[IND][:, 2 * d] = -DECAY * half[d]
        m[IND][:, 2 * d + 1] = -DECAY * ~half[d]
    m[PAIR] = r // 64 == c // 64
    return np.ascontiguousarray(m.transpose(1, 0, 2))


def route_constants():
    m = np.zeros((P, ROUTE_COLS), np.float32)
    e = np.arange(NEXP)
    row = np.concatenate([np.arange(4), e, P * np.arange(NT), np.arange(NB),
                          (e[None, :] <= e[:, None]).astype(np.float32).reshape(-1)])
    m[:, :row.size] = row
    m[:, row.size:] = np.arange(P)[:, None] + P * np.arange(NT)
    return m


def after(e, sem, t, per=1):
    e.wait_ge(sem, t * per + per)


def freed(e, sem, t, per=1):
    if not (isinstance(t, int) and t == 0):
        e.wait_ge(sem, t * per)


def over_tiles(e, step):
    for t in range(2):
        step(t, t, 0, 3)
    with e.Fori(1, LAT // 2 - 1) as j:
        step(j * 2, 0, j, 3)
        step(j * 2 + 1, 1, j, 3)
    for t in range(LAT - 2, NT):
        step(t, t % 2, t // 2, LAT - t)


class Sems:

    def __init__(self, nc, ctx):
        self.nc, self.taken = nc, []
        ctx.callback(self.clear)

    def __call__(self, name):
        self.taken.append(self.nc.alloc_semaphore(name=name))
        return self.taken[-1]

    def clear(self):
        self.nc.clear_and_free_semaphores(self.taken)
        self.nc.all_engine_barrier()


def stage_modulation(nc, io, scr, K):
    with ExitStack() as ctx:
        def sb(name, shape):
            return ctx.enter_context(nc.sbuf_tensor(name, shape, F32))

        sem = Sems(nc, ctx)
        NC = 12
        crow = sb("m_crow", [16, P])
        sig = sb("m_sig", [P, 16])
        sil = sb("m_sil", [P, 16])
        cw = [sb(f"m_w{b}", [P, KD, 512]) for b in range(2)]
        brow = sb("m_brow", [2, 6 * D])
        mrow = sb("m_mrow", [2, 6 * D])
        prow = sb("m_prow", [118, P])
        n2row = sb("m_n2row", [2, D])
        rows = sb("m_rows", [2, 3, D])
        ps = ctx.enter_context(nc.psum_tensor("m_ps", [P, 4, 512], F32))
        const_in, c_in, b_in = sem("m_const_in"), sem("m_c_in"), sem("m_b_in")
        w_in = [sem(f"m_w_in{b}") for b in range(2)]
        cT, sig_ok, sil_ok = sem("m_cT"), sem("m_sig_ok"), sem("m_sil_ok")
        out_ps, out_sb, rows_ok = sem("m_out_ps"), sem("m_out_sb"), sem("m_rows_ok")
        stored, rows_in, rowsT, pt_ok, g_ok = (sem("m_stored"), sem("m_rows_in"), sem("m_rowsT"),
                                               sem("m_pt_ok"), sem("m_g_ok"))
        ada = io["ada_w"].rearrange("(k p) n -> p k n", p=P)

        with nc.Block() as block:
            @block.sync
            def _(sp):
                sp.dma_start(K["ident"][:, :], io["consts"][:, IDENT, :]).then_inc(const_in, 16)
                sp.dma_start(crow[:, :], io["c_all"].rearrange("v (k p) -> (v k) p", p=P)).then_inc(c_in, 16)
                for n in range(NC):
                    if n >= 2:
                        sp.wait_ge(out_ps, n - 1)
                    sp.dma_start(cw[n % 2][:, :, :], ada[:, :, n * 512:(n + 1) * 512]).then_inc(w_in[n % 2], 16)
                sp.wait_ge(out_sb, NC)
                sp.dma_start(scr["mod"], mrow[:, :]).then_inc(stored, 16)
                sp.wait_ge(stored, 16)
                sp.dma_start(prow[0:96, :], scr["mod"].rearrange("v (s k p) -> (v s k) p", k=KD, p=P))\
                    .then_inc(rows_in, 16)
                sp.wait_ge(rows_in, 64)
                sp.wait_ge(rows_ok, 3)
                sp.dma_start(scr["rows"], rows[:, :, :]).then_inc(stored, 16)
                sp.wait_ge(stored, 32)

            @block.scalar
            def _(act):
                act.dma_start(brow[:, :], io["ada_b"].partition_broadcast(2)).then_inc(b_in, 16)
                act.dma_start(n2row[:, :], io["norm2_g"].partition_broadcast(2)).then_inc(b_in, 16)
                act.dma_start(prow[96:104, :], io["norm1_g"].rearrange("(k p) -> k p", p=P)).then_inc(rows_in, 16)
                act.dma_start(prow[104:112, :], io["norm2_g"].rearrange("(k p) -> k p", p=P)).then_inc(rows_in, 16)
                act.dma_start(prow[112:118, :], io["conv_w"].rearrange("c (k p) -> (c k) p", p=P))\
                    .then_inc(rows_in, 16)
                act.wait_ge(cT, 1)
                nc.scalar.activation(sig[:, :], ps[:, 0, 0:16], ACT.Sigmoid).then_inc(sig_ok, 1)

            @block.vector
            def _(dve):
                dve.wait_ge(sig_ok, 1)
                nc.vector.tensor_tensor(sil[:, :], ps[:, 0, 0:16], sig[:, :], ALU.mult).then_inc(sil_ok, 1)
                dve.wait_ge(b_in, 32)
                for n in range(NC):
                    dve.wait_ge(out_ps, n + 1)
                    nc.vector.tensor_tensor(mrow[:, n * 512:(n + 1) * 512], ps[0:2, 1 + n % 2, :],
                                            brow[:, n * 512:(n + 1) * 512], ALU.add).then_inc(out_sb, 1)
                dve.wait_ge(out_sb, NC)
                nc.vector.tensor_copy(rows[:, 0, :], mrow[:, 2 * D:3 * D]).then_inc(rows_ok, 1)
                nc.vector.scalar_tensor_tensor(rows[:, 1, :], mrow[:, 4 * D:5 * D], 1.0, n2row[:, :], ALU.add, ALU.mult)\
                    .then_inc(rows_ok, 1)
                nc.vector.tensor_copy(rows[:, 2, :], mrow[:, 3 * D:4 * D]).then_inc(rows_ok, 1)
                dve.wait_ge(rowsT, 1)
                nc.vector.tensor_copy(K["pt"][:, :], ps[:, 3, 0:118]).then_inc(pt_ok, 1)
                dve.wait_ge(pt_ok, 1)
                for norm, sc_at in ((0, 1), (1, 4)):
                    for v in range(2):
                        at = (v * 6 + sc_at) * KD
                        g = 96 + 8 * norm
                        nc.vector.scalar_tensor_tensor(K["gs"][:, norm, v, :], K["pt"][:, at:at + KD], 1.0,
                                                       K["pt"][:, g:g + KD], ALU.add, ALU.mult).then_inc(g_ok, 1)
                dve.wait_ge(g_ok, 4)

            @block.tensor
            def _(pe):
                pe.wait_ge(const_in, 16)
                pe.wait_ge(c_in, 16)
                nc.tensor.transpose(ps[:, 0, 0:16], crow[:, :], K["ident"][0:16, 0:16]).then_inc(cT, 1)
                pe.wait_ge(sil_ok, 1)
                both = sil[:, :].rearrange("p (v k) -> p k v", v=2)
                for n in range(NC):
                    pe.wait_ge(w_in[n % 2], 16 * (n // 2 + 1))
                    if n >= 2:
                        pe.wait_ge(out_sb, n - 1)
                    for k in range(KD):
                        last = nc.tensor.matmul(ps[0:2, 1 + n % 2, :], both[:, k, :], cw[n % 2][:, k, :],
                                                start=k == 0, stop=k == KD - 1)
                    last.then_inc(out_ps, 1)
                pe.wait_ge(rows_in, 64)
                nc.tensor.transpose(ps[:, 3, 0:118], prow[:, :], K["ident"][0:118, 0:118]).then_inc(rowsT, 1)


def stage_tokens(nc, io, scr, K):
    with ExitStack() as ctx:
        def sb(name, shape):
            return ctx.enter_context(nc.sbuf_tensor(name, shape, F32))

        sem = Sems(nc, ctx)
        ps = ctx.enter_context(nc.psum_tensor("a_ps", [P, 8, 512], F32))
        ident = K["ident"][:, :]
        win = sb("a_win", [P, KD, CGATE])
        lw = sb("a_lora_w", [P, W])
        la = sb("a_lora_a", [P, W])
        lg = sb("a_lora_g", [P, W])
        prm = sb("a_prm", [P, 7, W])
        w0b, a0b, kkb, kab, rkb = [0, 1], [2, 3], 4, 5, 6
        lng = sb("a_lng", [P, 256])
        lnb = sb("a_lnb", [P, 256])
        bsb = sb("a_bsb", [P, 2, P])
        wsT = sb("a_wsT", [P, 4, P])
        X = [sb(f"a_x{b}", [P, D]) for b in range(2)]
        Xn = sb("a_xn", [P, D])
        hT = [sb(f"a_hT{b}", [P, KD, P]) for b in range(2)]
        junk = Xn
        sqi = sb("a_sqi", [P, 10])
        sqs = sb("a_sqs", [P, 10])
        sqm = sb("a_sqm", [P, 10])
        rc = sb("a_rc", [P, 10])
        ssx = sb("a_ssx", [P, 1])
        WLO, ALO, GLO = sb("a_wlo", [P, P]), sb("a_alo", [P, P]), sb("a_glo", [P, P])
        CCs = sb("a_cc", [P, 2, P])
        Pc = sb("a_pc", [P, 2, P])
        Yc = sb("a_yc", [P, 2, P])
        CBSU = sb("a_cbsu", [P, 4, P])
        Ks = sb("a_k", [P, W])
        kk0 = sb("a_kk0", [P, W])
        ksq = sb("a_ksq", [P, W])
        m1 = sb("a_m1", [P, W])
        SV = sb("a_sv", [P, 256])
        st = sb("a_st", [P, 6])
        mv = sb("a_mv", [P, 2])
        gap = sb("a_gap", [P, 1])
        vn = sb("a_vn", [P, 256])
        vg = sb("a_vg", [P, 256])
        vb = sb("a_vb", [P, 256])
        mixs = sb("a_mix", [P, 2, P])
        ag = [sb(f"a_ag{d}", [P, W]) for d in range(2)]
        am = sb("a_am", [P, W])
        rsum = sb("a_rsum", [P, W])
        rk8 = sb("a_rk8", [P, H])
        lxb = sb("a_lxb", [P, W])
        oA = sb("a_oA", [P, 3, W])
        oD = [sb(f"a_oD{d}", [P, 3, W]) for d in range(2)]
        oO = sb("a_oO", [P, 2, W])
        tw = [oD[d][:, 2, :] for d in range(2)]
        ta = ag
        oC = sb("a_oC", [P, 4, P])

        B_T, B_F1, B_F2, B_F3, B5, B6, B7 = 0, 2, 3, 4, 5, 6, 7
        s = {n: sem("a_" + n) for n in (
            "prm_in", "ssx_ok", "ms_ok", "xrt_ok", "rc_ok", "xm_ok", "xn_ok", "hT_ps", "hT_ok",
            "F1", "F2", "F3", "lo_ok", "cc_ok", "cbsu_ok", "pc_ok", "yc_ok", "conv_ok",
            "K", "R", "V", "SV", "WL0", "AL0", "WL1", "AL1", "G", "MIX",
            "k_ok", "r_ok", "v_ok", "sv_ok", "kk0_ok", "ksq_ok", "n2_ok", "st_ok", "mv_ok", "var_ok", "sq_ok",
            "sqm_ok", "kk_ok", "vn_ok", "vg_ok", "vb_ok", "m1_ok", "tw0", "ta0", "tw1", "ta1",
            "sg0", "sg1", "ag0", "ag1", "ka0", "ka1", "am0", "am1", "kd0", "kd1",
            "s1", "s2", "s3", "rk_ok", "bm_ok", "bonus_ok", "g_ok", "mix_ok", "sgu_ok",
            "stA", "stD0", "stD1", "stO", "stC")}
        GROUPS = {"F1": ((CWLO, CSU),), "K": ((CK, CV),), "SV": ((CSV, CGATE),), "F2": ((CC, CR),),
                  "F3": ((CB, CC), (CSU, CSV)), "R": ((CR, CK),), "V": ((CV, CWLO),)}
        win_in = {name: sem("a_win_in_" + name) for name in GROUPS}
        x_in = [sem(f"a_x_in{b}") for b in range(2)]
        st_h = [sem(f"a_st_h{b}") for b in range(2)]

        def tile_of(ap, t):
            return ap[bass.ds(t, 1)].rearrange("a p n -> (a p) n")

        with nc.Block() as block:
            @block.sync
            def _(sp):
                def load_x(t, b):
                    sp.dma_start(X[b][:, :], tile_of(io["x_all"], t)).then_inc(x_in[b], 16)

                load_x(0, 0)
                load_x(1, 1)
                w_v = io["w_in"].rearrange("(k p) n -> p k n", p=P)
                for name, spans in GROUPS.items():
                    if name == "SV":
                        sp.wait_ge(s["prm_in"], 16 * 18)
                    for lo, hi in spans:
                        sp.dma_start(win[:, :, lo:hi], w_v[:, :, lo:hi]).then_inc(win_in[name], 16)

                def step(t, b, n, left):
                    last = left == 0
                    if left >= 2:
                        after(sp, s["xn_ok"], t)
                        load_x(t + 2, b)
                    after(sp, s["hT_ok"], t, 2)
                    sp.dma_start(tile_of(scr["h"], t), hT[b][:, :, :].rearrange("p k n -> p (k n)"))\
                        .then_inc(st_h[b], 16)
                    after(sp, s["conv_ok"], t)
                    after(sp, s["sgu_ok"], t)
                    sp.dma_start(tile_of(scr["cs"], t), oC[:, :, :].rearrange("p k n -> p (k n)")).then_inc(s["stC"], 16)
                    after(sp, s["r_ok"], t)
                    after(sp, s["v_ok"], t)
                    after(sp, s["kk_ok"], t)
                    sp.dma_start(tile_of(scr["A"], t), oA[:, :, :].rearrange("p k n -> p (k n)")).then_inc(s["stA"], 16)
                    for d in range(2):
                        after(sp, s[f"sg{d}"], t)
                        after(sp, s[f"ka{d}"], t)
                        after(sp, s[f"kd{d}"], t)
                        sp.dma_start(tile_of(scr[f"D{d}"], t), oD[d][:, :, :].rearrange("p k n -> p (k n)"))\
                            .then_inc(s[f"stD{d}"], 16)
                    after(sp, s["g_ok"], t)
                    after(sp, s["bonus_ok"], t)
                    sp.dma_start(tile_of(scr["O"], t), oO[:, :, :].rearrange("p k n -> p (k n)")).then_inc(s["stO"], 16)

                over_tiles(sp, step)
                for name in ("stC", "stA", "stD0", "stD1", "stO"):
                    sp.wait_ge(s[name], 16 * NT)
                sp.wait_ge(st_h[0], 16 * 9)
                sp.wait_ge(st_h[1], 16 * 8)

            @block.scalar
            def _(act):
                loads = [(lw[:, :], io["rwkv_w2"]), (la[:, :], io["rwkv_a2"]), (lg[:, :], io["rwkv_g2"]),
                         (prm[:, 0, :], io["rwkv_w0"][0].partition_broadcast(P)),
                         (prm[:, 1, :], io["rwkv_w0"][1].partition_broadcast(P)),
                         (prm[:, 2, :], io["rwkv_a0"][0].partition_broadcast(P)),
                         (prm[:, 3, :], io["rwkv_a0"][1].partition_broadcast(P)),
                         (prm[:, 4, :], io["rwkv_k_k"].partition_broadcast(P)),
                         (prm[:, 5, :], io["rwkv_k_a"].partition_broadcast(P)),
                         (prm[:, 6, :], io["rwkv_r_k"].partition_broadcast(P)),
                         (lng[:, :], io["sgu_ln_g"].partition_broadcast(P)),
                         (lnb[:, :], io["sgu_ln_b"].partition_broadcast(P)),
                         (lxb[:, :], io["rwkv_lnx_b"].partition_broadcast(P)),
                         (wsT[:, :, :], io["sgu_wsT"])]
                for g in range(4):
                    loads.append((bsb[64 * (g % 2):64 * (g % 2) + 64, g // 2, :],
                                  io["sgu_bs"][g].partition_broadcast(64)))
                for dst, src in loads:
                    act.dma_start(dst, src).then_inc(s["prm_in"], 16)

                def sum_squares(t, b, n):
                    after(act, x_in[b], n, 16)
                    freed(act, s["hT_ps"], t)
                    nc.scalar.activation(junk[:, :], X[b][:, :], ACT.Square, accum_out=ssx[:, :])\
                        .then_inc(s["ssx_ok"], 1)

                def evacuate_h(t, b, v):
                    after(act, s["hT_ps"], t)
                    for k in range(4):
                        ins = nc.scalar.activation(hT[b][:, k, :], ps[:, B_T, k * P:(k + 1) * P], ACT.Identity,
                                                   bias=K["pt"][:, v * 48 + k:v * 48 + k + 1],
                                                   scale=K["gs"][:, 0, v, k:k + 1])
                    ins.then_inc(s["hT_ok"], 1)

                sum_squares(0, 0, 0)
                act.wait_ge(s["ms_ok"], 1)
                nc.scalar.activation(sqs[:, 9:10], sqi[:, 9:10], ACT.Sqrt).then_inc(s["xrt_ok"], 1)
                evacuate_h(0, 0, 0)

                def step(t, b, n, left):
                    last = left == 0
                    if not last:
                        sum_squares(t + 1, 1 - b, n + b)
                    after(act, s["F1"], t)
                    nc.scalar.activation(WLO[:, :], ps[:, B_F1, 0:P], ACT.Tanh)
                    nc.scalar.activation(ALO[:, :], ps[:, B_F1, P:2 * P], ACT.Copy)
                    nc.scalar.activation(GLO[:, :], ps[:, B_F1, 2 * P:3 * P], ACT.Sigmoid).then_inc(s["lo_ok"], 1)
                    after(act, s["F2"], t)
                    freed(act, s["pc_ok"], t)
                    nc.scalar.activation(CCs[:, :, :].rearrange("p a n -> p (a n)"), ps[:, B_F2, 0:256], ACT.Copy)\
                        .then_inc(s["cc_ok"], 1)
                    after(act, s["F3"], t)
                    freed(act, s["conv_ok"], t)
                    freed(act, s["sgu_ok"], t)
                    nc.scalar.activation(CBSU[:, :, :].rearrange("p a n -> p (a n)"), ps[:, B_F3, :], ACT.Copy)\
                        .then_inc(s["cbsu_ok"], 1)
                    after(act, s["K"], t)
                    freed(act, s["kd1"], t)
                    nc.scalar.activation(Ks[:, :], ps[:, B5, :], ACT.Copy).then_inc(s["k_ok"], 1)
                    after(act, s["R"], t)
                    freed(act, s["stA"], t, 16)
                    freed(act, s["s2"], t)
                    nc.scalar.activation(oA[:, 0, :], ps[:, B7, :], ACT.Copy).then_inc(s["r_ok"], 1)
                    after(act, s["kk0_ok"], t)
                    freed(act, s["n2_ok"], t)
                    nc.scalar.activation(ksq[:, :], kk0[:, :], ACT.Square).then_inc(s["ksq_ok"], 1)
                    after(act, s["n2_ok"], t)
                    after(act, s["var_ok"], t)
                    if last:
                        nc.scalar.activation(sqs[:, 0:9], sqi[:, 0:9], ACT.Sqrt).then_inc(s["sq_ok"], 1)
                    else:
                        after(act, s["ms_ok"], t + 1)
                        nc.scalar.activation(sqs[:, :], sqi[:, :], ACT.Sqrt).then_inc(s["sq_ok"], 1)
                    if not last:
                        freed(act, s["V"], t)
                        freed(act, st_h[1 - b], n + b, 16)
                        evacuate_h(t + 1, 1 - b, int(left == 1))
                    for d in range(2):
                        after(act, s[f"tw{d}"], t)
                        nc.scalar.activation(oD[d][:, 2, :], tw[d], ACT.Sigmoid).then_inc(s[f"sg{d}"], 1)
                        after(act, s[f"ta{d}"], t)
                        nc.scalar.activation(ag[d][:, :], ta[d][:, :], ACT.Sigmoid).then_inc(s[f"ag{d}"], 1)
                    after(act, s["G"], t)
                    freed(act, s["stO"], t, 16)
                    nc.scalar.activation(oO[:, 1, :], ps[:, B7, :], ACT.Copy).then_inc(s["g_ok"], 1)

                over_tiles(act, step)

            @block.vector
            def _(dve):
                def mean_square(t):
                    after(dve, s["ssx_ok"], t)
                    nc.vector.tensor_scalar(sqi[:, 9:10], ssx[:, :], 1.0 / D, EPS, ALU.mult, ALU.add)\
                        .then_inc(s["ms_ok"], 1)

                def evacuate_h(t, b, v):
                    after(dve, s["hT_ps"], t)
                    for k in range(4, KD):
                        ins = nc.vector.tensor_scalar(hT[b][:, k, :], ps[:, B_T + 1, (k - 4) * P:(k - 3) * P],
                                                      K["gs"][:, 0, v, k:k + 1],
                                                      K["pt"][:, v * 48 + k:v * 48 + k + 1], ALU.mult, ALU.add)
                    ins.then_inc(s["hT_ok"], 1)

                mean_square(0)
                dve.wait_ge(s["xrt_ok"], 1)
                nc.vector.reciprocal(rc[:, 9:10], sqs[:, 9:10]).then_inc(s["xm_ok"], 1)
                dve.wait_ge(s["xm_ok"], 1)
                nc.vector.tensor_scalar(Xn[:, :], X[0][:, :], rc[:, 9:10], None, ALU.mult).then_inc(s["xn_ok"], 1)
                evacuate_h(0, 0, 0)
                dve.wait_ge(s["prm_in"], 16 * 18)

                def step(t, b, n, left):
                    last = left == 0
                    if not last:
                        mean_square(t + 1)
                    after(dve, s["cc_ok"], t)
                    freed(dve, s["conv_ok"], t)
                    nc.vector.tensor_tensor(Pc[:, :, :].rearrange("p a n -> p (a n)"),
                                            CCs[:, :, :].rearrange("p a n -> p (a n)"), ps[:, B_F2, 256:512],
                                            ALU.mult).then_inc(s["pc_ok"], 1)
                    after(dve, s["pc_ok"], t)
                    rows, cols = (1, P) if last else (2, 64)
                    for m in range(2):
                        nc.vector.tensor_scalar(Yc[:, m, :], Pc[:, m, :], K["pt"][:, 114 + m:115 + m], None, ALU.mult)\
                            .then_inc(s["yc_ok"], 1)
                    for m in range(2):
                        pv = Pc[:, m, :].rearrange("p (r c) -> p r c", r=rows)
                        yv = Yc[:, m, :].rearrange("p (r c) -> p r c", r=rows)
                        dve.wait_ge(s["yc_ok"], t * 6 + 1 + m)
                        nc.vector.scalar_tensor_tensor(yv[:, :, 1:cols], pv[:, :, 0:cols - 1], K["pt"][:, 112 + m:113 + m],
                                                       yv[:, :, 1:cols], ALU.mult, ALU.add).then_inc(s["yc_ok"], 1)
                    for m in range(2):
                        pv = Pc[:, m, :].rearrange("p (r c) -> p r c", r=rows)
                        yv = Yc[:, m, :].rearrange("p (r c) -> p r c", r=rows)
                        dve.wait_ge(s["yc_ok"], t * 6 + 3 + m)
                        nc.vector.scalar_tensor_tensor(yv[:, :, 0:cols - 1], pv[:, :, 1:cols], K["pt"][:, 116 + m:117 + m],
                                                       yv[:, :, 0:cols - 1], ALU.mult, ALU.add).then_inc(s["yc_ok"], 1)
                    after(dve, s["SV"], t)
                    freed(dve, s["vn_ok"], t)
                    nc.vector.tensor_copy(SV[:, :], ps[:, B6, 0:256]).then_inc(s["sv_ok"], 1)
                    after(dve, s["sv_ok"], t)
                    nc.vector.bn_stats(st[:, :], SV[:, :]).then_inc(s["st_ok"], 1)
                    after(dve, s["st_ok"], t)
                    nc.vector.memset(gap[:, :], 0.0)
                    nc.vector.bn_aggr(mv[:, :], st[:, :]).then_inc(s["mv_ok"], 1)
                    after(dve, s["mv_ok"], t)
                    nc.vector.tensor_scalar(sqi[:, 8:9], mv[:, 1:2], EPS, None, ALU.add).then_inc(s["var_ok"], 1)
                    after(dve, s["ksq_ok"], t)
                    nc.vector.reduce_sum(sqi[:, 0:8], ksq[:, :].rearrange("p (h n) -> p h n", h=H), axis=X_AXIS)\
                        .then_inc(s["n2_ok"], 1)
                    after(dve, s["sq_ok"], t)
                    cols = 9 if last else 10
                    nc.vector.tensor_scalar(sqm[:, 0:cols], sqs[:, 0:cols], 1e-12, None, ALU.max).then_inc(s["sqm_ok"], 1)
                    after(dve, s["sqm_ok"], t)
                    nc.vector.reciprocal(rc[:, 0:cols], sqm[:, 0:cols]).then_inc(s["rc_ok"], 1)
                    after(dve, s["rc_ok"], t)
                    if not last:
                        nc.vector.tensor_scalar(Xn[:, :], X[1 - b][:, :], rc[:, 9:10], None, ALU.mult)\
                            .then_inc(s["xn_ok"], 1)
                    after(dve, s["V"], t)
                    freed(dve, s["stA"], t, 16)
                    freed(dve, s["bonus_ok"], t)
                    nc.vector.tensor_copy(oA[:, 1, :], ps[:, B5, :]).then_inc(s["v_ok"], 1)
                    freed(dve, s["vg_ok"], t)
                    nc.vector.tensor_scalar(vn[:, :], SV[:, :], mv[:, 0:1], rc[:, 8:9], ALU.subtract, ALU.mult)\
                        .then_inc(s["vn_ok"], 1)
                    freed(dve, s["ka1"], t)
                    nc.vector.tensor_tensor(oA[:, 2, :].rearrange("p (h n) -> p h n", h=H),
                                            kk0[:, :].rearrange("p (h n) -> p h n", h=H),
                                            rc[:, 0:8].unsqueeze(2).broadcast_to([P, H, N]), ALU.mult)\
                        .then_inc(s["kk_ok"], 1)
                    for d, bw, ba in ((0, B6, B7), (1, B5, B6)):
                        after(dve, s[f"WL{d}"], t)
                        freed(dve, s[f"stD{d}"], t, 16)
                        nc.vector.tensor_tensor(tw[d], ps[:, bw, :], prm[:, w0b[d], :], ALU.add)\
                            .then_inc(s[f"tw{d}"], 1)
                        after(dve, s[f"AL{d}"], t)
                        freed(dve, s[f"ka{d}"], t)
                        nc.vector.tensor_tensor(ta[d][:, :], ps[:, ba, :], prm[:, a0b[d], :], ALU.add)\
                            .then_inc(s[f"ta{d}"], 1)
                        if d == 0 and not last:
                            freed(dve, s["V"], t)
                            freed(dve, st_h[1 - b], n + b, 16)
                            evacuate_h(t + 1, 1 - b, int(left == 1))
                    for d in range(2):
                        after(dve, s[f"ag{d}"], t)
                        after(dve, s["m1_ok"], t)
                        if d == 0:
                            freed(dve, s["kd1"], t)
                        else:
                            after(dve, s["kd0"], t)
                        nc.vector.scalar_tensor_tensor(am[:, :], ag[d][:, :], -1.0, m1[:, :], ALU.add, ALU.mult)\
                            .then_inc(s[f"am{d}"], 1)
                    after(dve, s["MIX"], t)
                    freed(dve, s["sgu_ok"], t)
                    nc.vector.tensor_tensor(mixs[:, :, :].rearrange("p a n -> p (a n)"), ps[:, B5, 0:256],
                                            bsb[:, :, :].rearrange("p a n -> p (a n)"), ALU.add).then_inc(s["mix_ok"], 1)
                    after(dve, s["s3"], t)
                    nc.vector.reduce_sum(rk8[:, :], rsum[:, :].rearrange("p (h n) -> p h n", h=H), axis=X_AXIS)\
                        .then_inc(s["rk_ok"], 1)

                over_tiles(dve, step)

            @block.gpsimd
            def _(pool):
                pool.wait_ge(s["prm_in"], 16 * 18)

                def step(t, b, n, left):
                    last = left == 0
                    g = nc.gpsimd
                    after(pool, s["k_ok"], t)
                    freed(pool, s["kk_ok"], t)
                    g.tensor_tensor(kk0[:, :], Ks[:, :], prm[:, kkb, :], ALU.mult).then_inc(s["kk0_ok"], 1)
                    freed(pool, s["am1"], t)
                    g.tensor_tensor(m1[:, :], Ks[:, :], prm[:, kab, :], ALU.mult).then_inc(s["m1_ok"], 1)
                    after(pool, s["cbsu_ok"], t)
                    pool.wait_ge(s["yc_ok"], t * 6 + 6)
                    freed(pool, s["stC"], t, 16)
                    g.tensor_tensor(oC[:, 0:2, :], CBSU[:, 0:2, :], Yc[:, :, :], ALU.mult).then_inc(s["conv_ok"], 1)
                    after(pool, s["vn_ok"], t)
                    g.tensor_tensor(vg[:, :], vn[:, :], lng[:, :], ALU.mult).then_inc(s["vg_ok"], 1)
                    after(pool, s["vg_ok"], t)
                    freed(pool, s["MIX"], t)
                    g.tensor_tensor(vb[:, :], vg[:, :], lnb[:, :], ALU.add).then_inc(s["vb_ok"], 1)
                    after(pool, s["kk_ok"], t)
                    for d in range(2):
                        after(pool, s[f"ag{d}"], t)
                        freed(pool, s[f"stD{d}"], t, 16)
                        g.tensor_tensor(oD[d][:, 1, :], oA[:, 2, :], ag[d][:, :], ALU.mult).then_inc(s[f"ka{d}"], 1)
                        after(pool, s[f"am{d}"], t)
                        g.tensor_tensor(oD[d][:, 0, :], am[:, :], Ks[:, :], ALU.add).then_inc(s[f"kd{d}"], 1)
                    after(pool, s["kd1"], t)
                    freed(pool, s["rk_ok"], t)
                    g.tensor_tensor(rsum[:, :], oD[0][:, 0, :], oD[1][:, 0, :], ALU.add).then_inc(s["s1"], 1)
                    after(pool, s["s1"], t)
                    after(pool, s["r_ok"], t)
                    g.tensor_tensor(rsum[:, :], rsum[:, :], oA[:, 0, :], ALU.mult).then_inc(s["s2"], 1)
                    after(pool, s["s2"], t)
                    g.tensor_tensor(rsum[:, :], rsum[:, :], prm[:, rkb, :], ALU.mult).then_inc(s["s3"], 1)
                    after(pool, s["rk_ok"], t)
                    after(pool, s["v_ok"], t)
                    freed(pool, s["stO"], t, 16)
                    g.tensor_tensor(oO[:, 0, :].rearrange("p (h n) -> p h n", h=H),
                                    oA[:, 1, :].rearrange("p (h n) -> p h n", h=H),
                                    rk8[:, :].unsqueeze(2).broadcast_to([P, H, N]), ALU.mult).then_inc(s["bm_ok"], 1)
                    after(pool, s["bm_ok"], t)
                    g.tensor_tensor(oO[:, 0, :], oO[:, 0, :], lxb[:, :], ALU.add).then_inc(s["bonus_ok"], 1)
                    after(pool, s["mix_ok"], t)
                    g.tensor_tensor(oC[:, 2:4, :], CBSU[:, 2:4, :], mixs[:, :, :], ALU.mult).then_inc(s["sgu_ok"], 1)

                over_tiles(pool, step)

            @block.tensor
            def _(pe):
                def transposes(t):
                    after(pe, s["xn_ok"], t)
                    freed(pe, s["hT_ok"], t, 2)
                    for k in range(KD):
                        ins = nc.tensor.transpose(ps[:, B_T + k // 4, (k % 4) * P:(k % 4 + 1) * P],
                                                  Xn[:, k * P:(k + 1) * P], ident)
                    ins.then_inc(s["hT_ps"], 1)

                def by_feature(bank, cols, b):
                    for j, c in enumerate(cols):
                        for k in range(KD):
                            ins = nc.tensor.matmul(ps[:, bank, j * P:(j + 1) * P], win[:, k, c:c + P], hT[b][:, k, :],
                                                   start=k == 0, stop=k == KD - 1)
                    return ins

                def by_token(bank, c, width, b):
                    for k in range(KD):
                        ins = nc.tensor.matmul(ps[:, bank, 0:width], hT[b][:, k, :], win[:, k, c:c + width],
                                               start=k == 0, stop=k == KD - 1)
                    return ins

                transposes(0)

                def step(t, b, n, left):
                    last = left == 0

                    def weights(name):
                        if isinstance(t, int) and t == 0:
                            pe.wait_ge(win_in[name], 16 * len(GROUPS[name]))

                    after(pe, s["hT_ok"], t, 2)
                    freed(pe, s["lo_ok"], t)
                    weights("F1")
                    by_feature(B_F1, (CWLO, CALO, CGLO), b).then_inc(s["F1"], 1)
                    freed(pe, s["mix_ok"], t)
                    weights("K")
                    by_token(B5, CK, W, b).then_inc(s["K"], 1)
                    freed(pe, s["ta1"], t)
                    weights("SV")
                    by_token(B6, CSV, 256, b).then_inc(s["SV"], 1)
                    freed(pe, s["pc_ok"], t)
                    weights("F2")
                    by_feature(B_F2, (CC, CC + P, CX, CX + P), b).then_inc(s["F2"], 1)
                    freed(pe, s["cbsu_ok"], t)
                    weights("F3")
                    by_feature(B_F3, (CB, CB + P, CSU, CSU + P), b).then_inc(s["F3"], 1)
                    freed(pe, s["g_ok"], t)
                    weights("R")
                    by_token(B7, CR, W, b).then_inc(s["R"], 1)
                    after(pe, s["k_ok"], t)
                    weights("V")
                    by_token(B5, CV, W, b).then_inc(s["V"], 1)
                    if isinstance(t, int) and t == 0:
                        pe.wait_ge(s["prm_in"], 16 * 18)
                    after(pe, s["lo_ok"], t)
                    after(pe, s["sv_ok"], t)
                    nc.tensor.matmul(ps[:, B6, :], WLO[0:64, :], lw[0:64, :], start=True, stop=True).then_inc(s["WL0"], 1)
                    after(pe, s["r_ok"], t)
                    nc.tensor.matmul(ps[:, B7, :], ALO[0:64, :], la[0:64, :], start=True, stop=True).then_inc(s["AL0"], 1)
                    if not last:
                        transposes(t + 1)
                    after(pe, s["v_ok"], t)
                    nc.tensor.matmul(ps[:, B5, :], WLO[64:128, :], lw[64:128, :], start=True, stop=True)\
                        .then_inc(s["WL1"], 1)
                    after(pe, s["tw0"], t)
                    nc.tensor.matmul(ps[:, B6, :], ALO[64:128, :], la[64:128, :], start=True, stop=True)\
                        .then_inc(s["AL1"], 1)
                    after(pe, s["ta0"], t)
                    nc.tensor.matmul(ps[:, B7, :], GLO[:, :], lg[:, :], start=True, stop=True).then_inc(s["G"], 1)
                    after(pe, s["vb_ok"], t)
                    after(pe, s["tw1"], t)
                    for g in range(4):
                        q = 64 * (g % 2)
                        ins = nc.tensor.matmul(ps[q:q + 64, B5, (g // 2) * P:(g // 2 + 1) * P],
                                               vb[:, g * 64:(g + 1) * 64], wsT[:, g, :], start=True, stop=True)
                    ins.then_inc(s["MIX"], 1)

                over_tiles(pe, step)


def stage_scan(nc, io, scr, K):
    with ExitStack() as ctx:
        def sb(name, shape):
            return ctx.enter_context(nc.sbuf_tensor(name, shape, F32))

        def each(name, shape):
            return [sb(f"b_{name}{d}", shape) for d in range(2)]

        sem = Sems(nc, ctx)
        ps = ctx.enter_context(nc.psum_tensor("b_ps", [P, 8, 512], F32))
        const = sb("b_const", [P, NCONST, P])
        ident = K["ident"][:, :]
        inA = [[sb(f"b_inA{d}{b}", [P, 3, W]) for b in range(2)] for d in range(2)]
        inD = [[sb(f"b_inD{d}{b}", [P, 3, W]) for b in range(2)] for d in range(2)]
        EI, EN, EX = each("ei", [P, W]), each("en", [P, W]), each("ex", [P, W])
        PM = each("pm", [P, 4, 2])
        QH = each("qh", [P, 2, W])
        Rt = [[sb(f"b_r{d}{b}", [P, W]) for b in range(2)] for d in range(2)]
        Bt, Kt = each("b", [P, W]), each("k", [P, W])
        QT, RT, BT, KT = each("qT", [P, 4, P]), each("rT", [P, 4, P]), each("bT", [P, 4, P]), each("kT", [P, 4, P])
        Am, ArbT, AqkT, ArkT = (each(n, [P, H, P]) for n in ("am", "arbT", "aqkT", "arkT"))
        TI, TIT, U, AL = (each(n, [P, H, P]) for n in ("ti", "tiT", "u", "al"))
        GH = each("gh", [P, 2, W])
        E, ET, YH = each("e", [P, W]), QT, each("yh", [P, W])
        MT, Shd = each("mt", [P, 4, P]), each("shd", [P, 4, P])
        S, Sh, SN = each("s", [P, 4, N]), each("sh", [P, 4, N]), each("sn", [P, 4, N])
        Yo = YH
        LV, LD = 6, 4
        XB = (2, 1)

        def per_dir(name):
            return [sem(f"b_{name}{d}") for d in range(2)]

        def per_group(name):
            return [[sem(f"b_{name}{d}{g}") for g in range(2)] for d in range(2)]

        const_in, cum_in = sem("b_const_in"), sem("b_cum_in")
        s0_in, s_out = sem("b_s0_in"), sem("b_s_out")
        a_in = [[sem(f"b_a_in{d}{b}") for b in range(2)] for d in range(2)]
        cum_ps, pm_ps, e_ok, pm_ok = per_dir("cum_ps"), per_dir("pm_ps"), per_dir("e_ok"), per_dir("pm_ok")
        x_ok, kx_ok = per_dir("x_ok"), per_dir("kx_ok")
        q_ok, r_ok, b_ok, k_ok = per_dir("q_ok"), per_dir("r_ok"), per_dir("b_ok"), per_dir("k_ok")
        qT_ps, rT_ps, bT_ps, kT_ps = per_dir("qT_ps"), per_dir("rT_ps"), per_dir("bT_ps"), per_dir("kT_ps")
        qT_ok, rT_ok, bT_ok, kT_ok = per_dir("qT_ok"), per_dir("rT_ok"), per_dir("bT_ok"), per_dir("kT_ok")
        prod_ps, prod_ok = per_group("prod_ps"), per_group("prod_ok")
        h0_ps, h0_ok = per_dir("h0_ps"), per_dir("h0_ok")
        a0_ok, t0_ok, r0_ok = per_group("a0_ok"), per_group("t0_ok"), per_group("r0_ok")
        al_ok, u_ps, u_ok, w_ps, tr_ok = (per_group(n) for n in ("al_ok", "u_ps", "u_ok", "w_ps", "tr_ok"))
        t_ok, tl_ps, tl_ok, gh_ps, gh_ok = (per_group(n) for n in ("t_ok", "tl_ps", "tl_ok", "gh_ps", "gh_ok"))
        x_ps, eg_ok, yh_ok = per_group("x_ps"), per_group("eg_ok"), per_group("yh_ok")
        et_ps, et_ok, m_ps, mt_ok, n_ps = (per_dir(n) for n in ("et_ps", "et_ok", "m_ps", "mt_ok", "n_ps"))
        sh_ok, sn_ok, st_ps, sp_ok, s_ok = (per_dir(n) for n in ("sh_ok", "sn_ok", "st_ps", "sp_ok", "s_ok"))
        y_ps, y_ok, y_st = per_dir("y_ps"), per_dir("y_ok"), per_dir("y_st")
        zero_ok, shd_ok, clear_ok = per_dir("zero_ok"), per_dir("shd_ok"), sem("b_clear_ok")
        GROUPS = [(d, g) for g in range(2) for d in range(2)]
        PAIRS = [((0, 0), (1, 1)), ((1, 0), (0, 1))]

        def tile_of(ap, t):
            return ap[bass.ds(t, 1)].rearrange("a p n -> (a p) n")

        def tile_at(d, q):
            if isinstance(q, int) and q == LAT:
                return LAT
            return q if d == 0 else 15 - q

        def of_group(ap, g):
            return ap.rearrange("p (i g n) -> p g i n", g=2, n=N)[:, g]

        def heads(g):
            return slice(4 * g, 4 * g + 4)

        def over_group(c):
            return const[:, c, :].unsqueeze(1).broadcast_to([P, 4, P])

        with nc.Block() as block:
            @block.sync
            def _(sp):
                def load(t, b, d):
                    sp.dma_start(inA[d][b][:, :, :].rearrange("p k n -> p (k n)"), tile_of(scr["A"], t))\
                        .then_inc(a_in[d][b], 16)
                    sp.dma_start(inD[d][b][:, :, :].rearrange("p k n -> p (k n)"), tile_of(scr[f"D{d}"], t))\
                        .then_inc(a_in[d][b], 16)

                sp.dma_start(const[:, CUMI[0]:CUMI[1] + 1, :], io["consts"][:, CUMI[0]:CUMI[1] + 1, :])\
                    .then_inc(cum_in, 16)
                for d in range(2):
                    load(tile_at(d, 0), 0, d)
                sp.dma_start(const[:, 0:CUMI[0], :], io["consts"][:, 0:CUMI[0], :]).then_inc(const_in, 16)
                sp.dma_start(const[:, CUMI[1] + 1:, :], io["consts"][:, CUMI[1] + 1:, :]).then_inc(const_in, 16)
                for d in range(2):
                    load(tile_at(d, 1), 1, d)
                    sp.dma_start(S[d][:, :, :], io["state_T"][d]).then_inc(s0_in, 16)

                def step(q, b, n, left):
                    now = [tile_at(d, q) for d in range(2)]
                    nxt = [tile_at(d, q + 2 if left > 2 else LAT) for d in range(2)]
                    if left > 2:
                        now, nxt = [sp.snap(t) for t in now], [sp.snap(t) for t in nxt]
                    for d in range(2):
                        sp.wait_ge(const_in, 32)
                        after(sp, y_ps[d], q)
                        if left >= 2:
                            after(sp, a_in[d][b], n, 32)
                            load(nxt[d], b, d)
                        sp.wait_ge(const_in, 32)
                        after(sp, y_ok[d], q)
                        sp.dma_start(tile_of(scr[f"Y{d}"], now[d]), Yo[d][:, :]).then_inc(y_st[d], 16)

                over_tiles(sp, step)
                for d in range(2):
                    sp.wait_ge(s_ok[d], NT)
                    sp.dma_start(io["state_new"][d], S[d][:, :, :]).then_inc(s_out, 16)
                    sp.wait_ge(y_st[d], 16 * NT)
                sp.wait_ge(s_out, 32)

            @block.scalar
            def _(act):
                def flat(ap):
                    return ap.rearrange("p a n -> p (a n)")

                act.wait_ge(clear_ok, 2)
                a = nc.scalar.activation

                def own_decay(q, b, n, d):
                    after(act, a_in[d][b], n, 32)
                    a(EX[d][:, :], inD[d][b][:, 2, :], ACT.Exp, scale=DECAY).then_inc(x_ok[d], 1)

                def decays(q, d):
                    after(act, cum_ps[d], q)
                    a(EI[d][:, :], ps[:, 4 * d + 1, :], ACT.Exp)
                    a(EN[d][:, :], ps[:, 4 * d + 1, :], ACT.Exp, scale=-1.0).then_inc(e_ok[d], 1)

                for d in range(2):
                    own_decay(0, 0, 0, d)
                for d in range(2):
                    decays(0, d)

                def step(q, b, n, left):
                    for d in range(2):
                        after(act, qT_ps[d], q)
                        a(flat(QT[d][:, :, :]), ps[:, 4 * d, :], ACT.Copy).then_inc(qT_ok[d], 1)
                    for d in range(2):
                        after(act, bT_ps[d], q)
                        a(flat(BT[d][:, :, :]), ps[:, 4 * d + 2, :], ACT.Copy).then_inc(bT_ok[d], 1)
                    for d in range(2):
                        after(act, pm_ps[d], q)
                        freed(act, s_ok[d], q)
                        sums = ps[:, 4 * d + 1, 0:4 * N].rearrange("p (j n) -> p j n", j=4)
                        a(PM[d][:, :, :], sums[:, :, 0:2], ACT.Exp).then_inc(pm_ok[d], 1)
                    for l in range(LV):
                        for d, g in GROUPS:
                            after(act, u_ps[d][g], q * LV + l)
                            a(flat(U[d][:, heads(g), :]), ps[:, 4 * d + 2 * g, :], ACT.Copy).then_inc(u_ok[d][g], 1)
                        if l == LD:
                            for d, g in GROUPS:
                                after(act, tl_ps[d][g], q)
                                a(flat(TI[d][:, heads(g), :]), ps[:, 4 * d + 2 * g, :], ACT.Copy)\
                                    .then_inc(tl_ok[d][g], 1)
                    if left > 0:
                        for d in range(2):
                            own_decay(q + 1, 1 - b, n + b, d)
                    for d, g in GROUPS:
                        after(act, gh_ps[d][g], q)
                        a(GH[d][:, :, :].rearrange("p a (i g n) -> p g i a n", g=2, n=N)[:, g],
                          ps[:, 4 * d + 2 * g, :].rearrange("p (i a n) -> p i a n", a=2, n=N), ACT.Copy)\
                            .then_inc(gh_ok[d][g], 1)
                    for d in range(2):
                        if left > 0:
                            decays(q + 1, d)
                        after(act, m_ps[d], q)
                        both = ps[:, 4 * d + 3, :].rearrange("p (j n) -> p j n", j=4)
                        for u in range(2):
                            own = slice(64 * u, 64 * u + 64)
                            ins = a(MT[d][own, :, own], both[own, :, own], ACT.Copy)
                        ins.then_inc(mt_ok[d], 1)
                    for d in range(2):
                        for g in range(2):
                            after(act, eg_ok[d][g], q)
                            freed(act, y_st[d], q, 16)
                            both = ps[:, 4 * d + XB[g], :].rearrange("p (i a n) -> p a i n", a=2, n=N)
                            a(of_group(YH[d][:, :], g), both[:, 1], ACT.Copy).then_inc(yh_ok[d][g], 1)
                    for d in range(2):
                        after(act, et_ps[d], q)
                        a(flat(ET[d][:, :, :]), ps[:, 4 * d, :], ACT.Copy).then_inc(et_ok[d], 1)

                over_tiles(act, step)

            @block.gpsimd
            def _(pool):
                pool.wait_ge(const_in, 32)
                g_ = nc.gpsimd
                for d in range(2):
                    g_.memset(MT[d][:, :, :], 0.0).then_inc(clear_ok, 1)

                def scaled(q, b, n, d):
                    after(pool, e_ok[d], q)
                    after(pool, a_in[d][b], n, 32)
                    g_.tensor_tensor(Rt[d][b][:, :], inA[d][b][:, 0, :], EI[d][:, :], ALU.mult).then_inc(r_ok[d], 1)
                    freed(pool, n_ps[d], q)
                    g_.tensor_tensor(Kt[d][:, :], inD[d][b][:, 0, :], EN[d][:, :], ALU.mult).then_inc(k_ok[d], 1)

                for d in range(2):
                    scaled(0, 0, 0, d)

                def step(q, b, n, left):
                    for d, g in PAIRS[0] + PAIRS[1]:
                        hs = heads(g)
                        pool.wait_ge(prod_ok[d][g], q * 4 + 1)
                        freed(pool, u_ps[d][g], q, LV)
                        freed(pool, gh_ps[d][g], q)
                        g_.tensor_tensor(AL[d][:, hs, :], Am[d][:, hs, :], over_group(LEVEL[d][0]), ALU.mult)\
                            .then_inc(a0_ok[d][g], 1)
                        after(pool, a0_ok[d][g], q)
                        g_.tensor_tensor(TI[d][:, hs, :], AL[d][:, hs, :], over_group(IDENT), ALU.add)\
                            .then_inc(t0_ok[d][g], 1)
                        after(pool, t0_ok[d][g], q)
                        g_.tensor_tensor(AL[d][:, hs, :], Am[d][:, hs, :], over_group(LEVEL[d][1]), ALU.mult)\
                            .then_inc(al_ok[d][g], 1)
                    for l in range(1, LV):
                        for d, g in GROUPS:
                            hs = heads(g)
                            after(pool, u_ps[d][g], q * LV + l - 1)
                            g_.tensor_tensor(AL[d][:, hs, :], Am[d][:, hs, :], over_group(LEVEL[d][l + 1]), ALU.mult)\
                                .then_inc(al_ok[d][g], 1)

                    for d in range(2):
                        after(pool, sh_ok[d], q)
                        freed(pool, y_ps[d], q)
                        pair = const[:, PAIR, :].rearrange("p (u n) -> p u n", u=2).unsqueeze(1)
                        g_.tensor_tensor(Shd[d][:, :, :].rearrange("p j (u n) -> p j u n", u=2),
                                         Sh[d][:, :, :].unsqueeze(2).broadcast_to([P, 4, 2, N]),
                                         pair.broadcast_to([P, 4, 2, N]), ALU.mult).then_inc(shd_ok[d], 1)
                    if left > 0:
                        for d in range(2):
                            scaled(q + 1, 1 - b, n + b, d)

                over_tiles(pool, step)

            @block.vector
            def _(dve):
                dve.wait_ge(const_in, 32)
                dve.wait_ge(s0_in, 32)
                v_ = nc.vector

                def bank(d, i):
                    return ps[:, 4 * d + i, :].rearrange("p (h n) -> p h n", h=4)

                def turn(out, src, d, g):
                    return v_.transpose(out[d][:, heads(g), :].rearrange("p a n -> p (a n)"),
                                        src[d][:, heads(g), :].rearrange("p a n -> p (a n)"))

                def before_token(q, b, n, d):
                    after(dve, a_in[d][b], n, 32)
                    after(dve, x_ok[d], q)
                    v_.tensor_tensor(EX[d][:, :], inA[d][b][:, 2, :], EX[d][:, :], ALU.mult).then_inc(kx_ok[d], 1)

                def scaled_q(q, d):
                    after(dve, e_ok[d], q)
                    after(dve, kx_ok[d], q)
                    for g in range(2):
                        freed(dve, gh_ps[d][g], q)
                    v_.tensor_tensor(QH[d][:, 0, :], EX[d][:, :], EI[d][:, :], ALU.mult).then_inc(q_ok[d], 1)

                def scaled_b(q, b, d):
                    freed(dve, n_ps[d], q)
                    after(dve, e_ok[d], q)
                    v_.scalar_tensor_tensor(Bt[d][:, :], inD[d][b][:, 1, :], -1.0, EN[d][:, :], ALU.mult, ALU.mult)\
                        .then_inc(b_ok[d], 1)

                for d in range(2):
                    before_token(0, 0, 0, d)
                for d in range(2):
                    scaled_q(0, d)
                    scaled_b(0, 0, d)

                def step(q, b, n, left):
                    for d in range(2):
                        after(dve, rT_ps[d], q)
                        v_.tensor_copy(RT[d][:, :, :], bank(d, 1)).then_inc(rT_ok[d], 1)
                    for d in range(2):
                        after(dve, kT_ps[d], q)
                        v_.tensor_copy(KT[d][:, :, :], bank(d, 3)).then_inc(kT_ok[d], 1)
                    for pair in PAIRS:
                        for i, out in enumerate((Am, ArbT, AqkT, ArkT)):
                            for d, g in pair:
                                strict, strictT, inclT = (LOW, UP, UPI) if d == 0 else (UP, LOW, LOWI)
                                mask = (strict, inclT, strictT, inclT)[i]
                                dve.wait_ge(prod_ps[d][g], q * 4 + i + 1)
                                v_.tensor_tensor(out[d][:, heads(g), :], bank(d, i), over_group(mask), ALU.mult)\
                                    .then_inc(prod_ok[d][g], 1)

                    def first_turn(d, g):
                        after(dve, t0_ok[d][g], q)
                        turn(TIT, TI, d, g).then_inc(r0_ok[d][g], 1)

                    for d, g in PAIRS[0]:
                        first_turn(d, g)
                    for d, g in PAIRS[1]:
                        after(dve, h0_ps[1 - d], q)
                        v_.tensor_copy(QH[1 - d][:, 1, :], ps[:, 4 * (1 - d), :]).then_inc(h0_ok[1 - d], 1)
                        first_turn(d, g)
                    for d in range(2):
                        after(dve, pm_ok[d], q)
                        if left == 0:
                            v_.memset(S[d][:, :, :], 0.0).then_inc(zero_ok[d], 1)
                            dve.wait_ge(zero_ok[d], 1)
                        else:
                            freed(dve, s_ok[d], q)
                        v_.tensor_tensor(Sh[d][:, :, :], S[d][:, :, :], PM[d][:, :, 0:1].broadcast_to([P, 4, N]),
                                         ALU.mult).then_inc(sh_ok[d], 1)
                    for l in range(LV):
                        def level_turn(d, g):
                            if l < LD:
                                after(dve, tr_ok[d][g], q * LV + l)
                                turn(TI, TIT, d, g).then_inc(t_ok[d][g], 1)

                        for i, (d, g) in enumerate(GROUPS):
                            after(dve, w_ps[d][g], q * LV + l)
                            v_.tensor_tensor(TIT[d][:, heads(g), :], TIT[d][:, heads(g), :], bank(d, 2 * g + 1), ALU.add)\
                                .then_inc(tr_ok[d][g], 1)
                            if i > 0:
                                level_turn(*GROUPS[i - 1])
                        level_turn(*GROUPS[-1])
                    if left > 0:
                        for d in range(2):
                            before_token(q + 1, 1 - b, n + b, d)
                    for d in range(2):
                        after(dve, n_ps[d], q)
                        new = ps[:, 4 * d, :].rearrange("p (j n) -> p j n", j=4)
                        for u in range(2):
                            own = slice(64 * u, 64 * u + 64)
                            ins = v_.tensor_tensor(SN[d][own, :, :], Sh[d][own, :, :], new[own, :, own], ALU.add)
                        ins.then_inc(sn_ok[d], 1)
                    if left > 0:
                        for d in range(2):
                            scaled_q(q + 1, d)
                    for d in range(2):
                        for g in range(2):
                            after(dve, x_ps[d][g], q)
                            both = ps[:, 4 * d + XB[g], :].rearrange("p (i a n) -> p a i n", a=2, n=N)
                            v_.tensor_tensor(of_group(E[d][:, :], g), of_group(Rt[d][b][:, :], g), both[:, 0], ALU.add)\
                                .then_inc(eg_ok[d][g], 1)
                    if left > 0:
                        for d in range(2):
                            scaled_b(q + 1, 1 - b, d)
                    for d in range(2):
                        after(dve, st_ps[d], q)
                        after(dve, sn_ok[d], q)
                        v_.tensor_tensor(SN[d][:, :, :], SN[d][:, :, :],
                                         ps[:, 4 * d + 3, 0:4 * N].rearrange("p (h n) -> p h n", h=4), ALU.add)\
                            .then_inc(sp_ok[d], 1)
                        after(dve, sp_ok[d], q)
                        v_.tensor_tensor(S[d][:, :, :], SN[d][:, :, :], PM[d][:, :, 1:2].broadcast_to([P, 4, N]),
                                         ALU.mult).then_inc(s_ok[d], 1)
                    for d in range(2):
                        after(dve, y_ps[d], q)
                        v_.tensor_tensor(Yo[d][:, :], YH[d][:, :], ps[:, 4 * d + 2, :], ALU.add).then_inc(y_ok[d], 1)

                over_tiles(dve, step)

            @block.tensor
            def _(pe):
                pe.wait_ge(cum_in, 16)

                def mm(out, lhsT, rhs, start=True, stop=True):
                    return nc.tensor.matmul(out, lhsT, rhs, start=start, stop=stop)

                def head(h):
                    return h // 2, 64 * (h % 2)

                def slot(h):
                    return 4 * (h % 2) + h // 2

                def cumulate(q, b, n, d):
                    after(pe, a_in[d][b], n, 32)
                    mm(ps[:, 4 * d + 1, :], const[:, CUMI[d], :], inD[d][b][:, 2, :]).then_inc(cum_ps[d], 1)

                for d in range(2):
                    cumulate(0, 0, 0, d)
                pe.wait_ge(const_in, 32)

                def by_feature(bank, src, done):
                    for j in range(4):
                        ins = nc.tensor.transpose(ps[:, bank, j * P:(j + 1) * P], src[:, j * P:(j + 1) * P], ident)
                    ins.then_inc(done, 1)

                def step(q, b, n, left):
                    for d in range(2):
                        freed(pe, et_ok[d], q)
                        after(pe, q_ok[d], q)
                        by_feature(4 * d, QH[d][:, 0, :], qT_ps[d])
                    for d in range(2):
                        after(pe, e_ok[d], q)
                        freed(pe, yh_ok[d][1], q)
                        after(pe, r_ok[d], q)
                        by_feature(4 * d + 1, Rt[d][b], rT_ps[d])
                    for d in range(2):
                        freed(pe, sp_ok[d], q)
                        after(pe, k_ok[d], q)
                        by_feature(4 * d + 3, Kt[d], kT_ps[d])
                    for d in range(2):
                        freed(pe, y_ok[d], q)
                        after(pe, b_ok[d], q)
                        by_feature(4 * d + 2, Bt[d], bT_ps[d])
                    for d in range(2):
                        after(pe, rT_ok[d], q)
                        for j in range(4):
                            ins = mm(ps[:, 4 * d + 1, j * N:(j + 1) * N], inD[d][b][:, 2, j * P:(j + 1) * P],
                                     const[:, IND, 2 * d:2 * d + N])
                        ins.then_inc(pm_ps[d], 1)
                    for p, pair in enumerate(PAIRS):
                        for i, (left_, right, ready) in enumerate(((QT, BT, (qT_ok, bT_ok)), (BT, RT, (rT_ok, pm_ok)),
                                                                   (KT, QT, (kT_ok,)), (KT, RT, ()))):
                            for d, g in pair:
                                if p == 0:
                                    for ok in ready:
                                        after(pe, ok[d], q)
                                else:
                                    pe.wait_ge(prod_ok[d][1 - g], q * 4 + i + 1)
                            for j in range(4):
                                for d, g in pair:
                                    u = 64 * g
                                    ins = mm(ps[:, 4 * d + i, j * P:(j + 1) * P], left_[d][u:u + 64, j, :],
                                             right[d][u:u + 64, j, :])
                                    if j == 3:
                                        ins.then_inc(prod_ps[d][g], 1)
                    for d in range(2):
                        for g in range(2):
                            pe.wait_ge(prod_ok[d][g], q * 4 + 3)
                        for h in range(H):
                            ins = mm(ps[:, 4 * d, h * N:(h + 1) * N], AqkT[d][:, slot(h), :], inA[d][b][:, 1, h * N:(h + 1) * N])
                        ins.then_inc(h0_ps[d], 1)
                    for l in range(LV):
                        for d, g in GROUPS:
                            after(pe, al_ok[d][g], q * LV + l)
                            if l == 0:
                                after(pe, h0_ok[d], q)
                                after(pe, r0_ok[d][g], q)
                            else:
                                after(pe, tr_ok[d][g], q * LV + l - 1)
                            if l == LD + 1:
                                after(pe, tl_ok[d][g], q)
                            for i in range(4):
                                k = 4 * g + i
                                ins = mm(ps[:, 4 * d + 2 * g, i * P:(i + 1) * P], AL[d][:, k, :], TIT[d][:, k, :])
                            ins.then_inc(u_ps[d][g], 1)
                        for d, g in GROUPS:
                            if 1 <= l <= LD:
                                after(pe, t_ok[d][g], q * LD + l - 1)
                            after(pe, u_ok[d][g], q * LV + l)
                            for i in range(4):
                                k = 4 * g + i
                                ins = mm(ps[:, 4 * d + 2 * g + 1, i * P:(i + 1) * P], TI[d][:, k, :], U[d][:, k, :])
                            ins.then_inc(w_ps[d][g], 1)
                        if l == LD:
                            for d, g in GROUPS:
                                after(pe, tr_ok[d][g], q * LV + l)
                                for i in range(4):
                                    ins = nc.tensor.transpose(ps[:, 4 * d + 2 * g, i * P:(i + 1) * P],
                                                              TIT[d][:, 4 * g + i, :], ident)
                                ins.then_inc(tl_ps[d][g], 1)
                    for d, g in GROUPS:
                        after(pe, tr_ok[d][g], q * LV + LV - 1)
                        for i in range(4):
                            h = 2 * i + g
                            ins = mm(ps[:, 4 * d + 2 * g, i * P:(i + 1) * P], TIT[d][:, slot(h), :],
                                     QH[d][:, :, h * N:(h + 1) * N])
                        ins.then_inc(gh_ps[d][g], 1)
                    if left > 0:
                        for d in range(2):
                            cumulate(q + 1, 1 - b, n + b, d)
                    for d in range(2):
                        after(pe, gh_ok[d][0], q)
                        after(pe, gh_ok[d][1], q)
                        for j in range(4):
                            two = slice(j * P, (j + 1) * P)
                            ins = mm(ps[:, 4 * d + 3, two], GH[d][:, 0, two], Bt[d][:, two])
                        ins.then_inc(m_ps[d], 1)
                        for j in range(4):
                            two = slice(j * P, (j + 1) * P)
                            mm(ps[:, 4 * d, two], Kt[d][:, two], inA[d][b][:, 1, two], stop=False)
                            ins = mm(ps[:, 4 * d, two], Bt[d][:, two], GH[d][:, 1, two], start=False)
                        ins.then_inc(n_ps[d], 1)
                    for d in range(2):
                        for g in range(2):
                            if left > 0 and g == 1:
                                after(pe, e_ok[d], q + 1)
                            for i in range(4):
                                h = 2 * i + g
                                ins = mm(ps[:, 4 * d + XB[g], i * P:(i + 1) * P], ArbT[d][:, slot(h), :],
                                         GH[d][:, :, h * N:(h + 1) * N])
                            ins.then_inc(x_ps[d][g], 1)
                    for d in range(2):
                        after(pe, mt_ok[d], q)
                        after(pe, sh_ok[d], q)
                        for j in range(4):
                            ins = mm(ps[:, 4 * d + 3, j * N:(j + 1) * N], MT[d][:, j, :], Sh[d][:, j, :])
                        ins.then_inc(st_ps[d], 1)
                    for d in range(2):
                        after(pe, sn_ok[d], q)
                        for g in range(2):
                            after(pe, eg_ok[d][g], q)
                        by_feature(4 * d, E[d], et_ps[d])
                    for d in range(2):
                        after(pe, yh_ok[d][0], q)
                        after(pe, et_ok[d], q)
                        after(pe, shd_ok[d], q)
                        for j in range(4):
                            mm(ps[:, 4 * d + 2, j * P:(j + 1) * P], ET[d][:, j, :], Shd[d][:, j, :], stop=False)
                            for h in (2 * j, 2 * j + 1):
                                ins = mm(ps[:, 4 * d + 2, h * N:(h + 1) * N], ArkT[d][:, slot(h), :],
                                         inA[d][b][:, 1, h * N:(h + 1) * N], start=False, stop=h % 2 == 1)
                        ins.then_inc(y_ps[d], 1)

                over_tiles(pe, step)


def stage_merge(nc, io, scr, K):
    with ExitStack() as ctx:
        def sb(name, shape):
            return ctx.enter_context(nc.sbuf_tensor(name, shape, F32))

        sem = Sems(nc, ctx)
        ps = ctx.enter_context(nc.psum_tensor("c_ps", [P, 8, 512], F32))
        ident = K["ident"][:, :]
        wg = sb("c_wg", [P, KD, 3 * D])
        wp = sb("c_wp", [P, KD, D])
        wo = sb("c_wo", [P, KD, D])
        RCOLS = 4 * NEXP
        rw = sb("c_rw", [P, KD * NEXP + RCOLS - NEXP])
        rowp = sb("c_rowp", [P, 3, D])
        ga1, g2, sh2 = (rowp[:, i, :] for i in range(3))
        lnx = sb("c_lnx", [P, W])
        hT = sb("c_hT", [P, KD, P])
        cs = sb("c_cs", [P, 4, P])
        ya, yb = sb("c_ya", [P, W]), sb("c_yb", [P, W])
        ob = sb("c_ob", [P, 2, W])
        s8 = [K["pt"][:, 4 + H * i:4 + H * (i + 1)] for i in range(6)]
        yT = sb("c_yT", [P, 4, P])
        Gs = [sb(f"c_gs{b}", [P, 3 * P]) for b in range(2)]
        Ms = Gs
        mT = sb("c_mT", [P, KD, P])
        h2T = mT
        xx = sb("c_xx", [P, D])
        h2 = sb("c_h2", [P, D])
        s1 = [K["pt"][:, i:i + 1] for i in range(4)]
        GB, PB, WB, TB = (0, 1, 2), (3, 4), (5, 6), 7
        HB = (TB, WB[0])

        s = {n: sem("c_" + n) for n in (
            "w_in", "wp_in", "wo_in", "pad_ok", "rp_in", "h_in", "cs_in", "y_in", "x_in", "ysum", "m_ok", "mean_ok", "yc_ok", "sq_ok",
            "v_ok", "ve_ok", "sd_ok", "rs_ok", "yn_ok", "yw_ok", "yo_ok", "yf_ok", "yT_ps", "yT_ok",
            "G_ps", "G_ok", "P_ps", "M_ok", "mg_ok", "W_ps", "mix_ok", "x2_ok", "ss_ok", "ms_ok", "sx_ok", "rx_ok",
            "hm_ok", "h2_ok", "hT_ps", "hT_ok", "lg_ps", "lg_ok", "st_x", "st_h")}

        wg_in = [sem(f"c_wg_in{i}") for i in range(4)]

        def tile_of(ap, t):
            return ap[bass.ds(t, 1)].rearrange("a p n -> (a p) n")

        def tiles(e, step):
            step(0, 0, 0, 3)
            with e.Fori(0, LAT // 2 - 1) as j:
                step(j * 2 + 1, 1, j, 3)
                step(j * 2 + 2, 0, j + 1, 3)
            step(LAT - 1, 1, LAT // 2 - 1, 1)
            step(LAT, 0, LAT // 2, 0)

        def first(t):
            return isinstance(t, int) and t == 0

        with nc.Block() as block:
            @block.sync
            def _(sp):
                def load_h(t):
                    sp.dma_start(hT[:, :, :].rearrange("p k n -> p (k n)"), tile_of(scr["h"], t)).then_inc(s["h_in"], 16)

                def load_y(t):
                    sp.dma_start(ya[:, :], tile_of(scr["Y0"], t)).then_inc(s["y_in"], 16)
                    sp.dma_start(yb[:, :], tile_of(scr["Y1"], t)).then_inc(s["y_in"], 16)
                    sp.dma_start(ob[:, :, :].rearrange("p k n -> p (k n)"), tile_of(scr["O"], t)).then_inc(s["y_in"], 16)

                def load_rows(v):
                    sp.dma_start(ga1, scr["rows"][v, 0].partition_broadcast(P)).then_inc(s["rp_in"], 16)
                    sp.dma_start(g2, scr["rows"][v, 1].partition_broadcast(P)).then_inc(s["rp_in"], 16)
                    sp.dma_start(sh2, scr["rows"][v, 2].partition_broadcast(P)).then_inc(s["rp_in"], 16)

                def load_cs(t):
                    sp.dma_start(cs[:, :, :].rearrange("p k n -> p (k n)"), tile_of(scr["cs"], t)).then_inc(s["cs_in"], 16)

                def load_x(t):
                    sp.dma_start(xx[:, :], tile_of(io["x_all"], t)).then_inc(s["x_in"], 16)

                def load_gate_weights(i):
                    for br in range(3):
                        c = br * D + i * 2 * P
                        sp.dma_start(wg[:, :, c:c + 2 * P], w_v[:, :, CGATE + c:CGATE + c + 2 * P]).then_inc(wg_in[i], 16)

                load_y(0)
                load_h(0)
                w_v = io["w_in"].rearrange("(k p) n -> p k n", p=P)
                load_gate_weights(0)
                sp.dma_start(lnx[:, :], io["rwkv_lnx_w"].partition_broadcast(P)).then_inc(s["w_in"], 16)
                load_cs(0)
                load_gate_weights(1)
                sp.dma_start(wp[:, 0:2, :], io["proj_conv"].rearrange("(k p) n -> p k n", p=P)).then_inc(s["wp_in"], 16)
                sp.dma_start(wp[:, 2:6, :], io["proj_rwkv"].rearrange("(k p) n -> p k n", p=P)).then_inc(s["wp_in"], 16)
                sp.dma_start(wp[:, 6:8, :], io["proj_sgu"].rearrange("(k p) n -> p k n", p=P)).then_inc(s["wp_in"], 16)
                load_gate_weights(2)
                load_gate_weights(3)
                load_x(0)
                load_rows(0)
                sp.dma_start(wo[:, :, :], io["w_out"].rearrange("(k p) n -> p k n", p=P)).then_inc(s["wo_in"], 16)
                sp.dma_start(rw[:, 0:KD * NEXP].rearrange("p (k n) -> p k n", k=KD), io["router_w"].rearrange("(k p) n -> p k n", p=P)).then_inc(s["wo_in"], 16)

                def step(t, b, n, left):
                    freed(sp, s["P_ps"], t, KD)
                    if not first(t):
                        load_cs(t)
                    sp.wait_ge(s["w_in"], 16)
                    freed(sp, s["st_x"], t, 16)
                    sp.wait_ge(s["w_in"], 16)
                    freed(sp, s["h2_ok"], t)
                    if left == 0:
                        load_rows(1)
                    if not first(t):
                        load_x(t)
                    if left > 0:
                        sp.wait_ge(s["w_in"], 16)
                        after(sp, s["yT_ps"], t)
                        load_y(t + 1)
                        sp.wait_ge(s["w_in"], 16)
                        after(sp, s["G_ps"], t, KD)
                        load_h(t + 1)
                    after(sp, s["x2_ok"], t)
                    sp.dma_start(tile_of(scr["x2"], t), xx[:, :]).then_inc(s["st_x"], 16)
                    sp.wait_ge(s["w_in"], 16)
                    after(sp, s["h2_ok"], t)
                    sp.dma_start(tile_of(scr["h2"], t), h2[:, :]).then_inc(s["st_h"], 16)

                tiles(sp, step)
                sp.wait_ge(s["st_x"], 16 * NT)
                sp.wait_ge(s["st_h"], 16 * NT)

            @block.scalar
            def _(act):
                a = nc.scalar.activation

                def scan_norm(t, part):
                    if part == 0:
                        after(act, s["yc_ok"], t)
                        a(ya[:, :], yb[:, :], ACT.Square).then_inc(s["sq_ok"], 1)
                    else:
                        after(act, s["ve_ok"], t)
                        a(s8[3][:, :], s8[2][:, :], ACT.Sqrt).then_inc(s["sd_ok"], 1)

                scan_norm(0, 0)
                scan_norm(0, 1)

                def step(t, b, n, left):
                    for j in range(KD):
                        if j == 2:
                            after(act, s["yT_ps"], t)
                            freed(act, s["P_ps"], t, KD)
                            a(yT[:, :, :].rearrange("p k n -> p (k n)"), ps[:, WB[1], :], ACT.Copy).then_inc(s["yT_ok"], 1)
                        after(act, s["G_ps"], t * KD + j)
                        if j >= 2:
                            act.wait_ge(s["mg_ok"], t * KD + j - 1)
                        else:
                            freed(act, s["mg_ok"], t, KD)
                        a(Gs[j % 2][:, :], ps[:, GB[j % 3], 0:3 * P], ACT.Sigmoid).then_inc(s["G_ok"], 1)
                        if left > 0 and j == 4:
                            scan_norm(t + 1, 0)
                    if left > 0:
                        scan_norm(t + 1, 1)
                    after(act, s["x2_ok"], t)
                    after(act, s["mix_ok"], t, 2)
                    a(h2[:, :], xx[:, :], ACT.Square, accum_out=s1[0]).then_inc(s["ss_ok"], 1)
                    after(act, s["ms_ok"], t)
                    a(s1[2], s1[1], ACT.Sqrt).then_inc(s["sx_ok"], 1)

                tiles(act, step)

            @block.gpsimd
            def _(pool):
                g = nc.gpsimd
                pool.wait_ge(s["w_in"], 16)

                def scan_sum(t):
                    after(pool, s["y_in"], t, 48)
                    g.tensor_tensor(ya[:, :], ya[:, :], yb[:, :], ALU.add).then_inc(s["ysum"], 1)

                def scan_out(t):
                    after(pool, s["yn_ok"], t)
                    g.tensor_tensor(yb[:, :], yb[:, :], lnx[:, :], ALU.mult).then_inc(s["yw_ok"], 1)
                    after(pool, s["yw_ok"], t)
                    g.tensor_tensor(yb[:, :], yb[:, :], ob[:, 0, :], ALU.add).then_inc(s["yo_ok"], 1)
                    after(pool, s["yo_ok"], t)
                    g.tensor_tensor(ya[:, :], yb[:, :], ob[:, 1, :], ALU.mult).then_inc(s["yf_ok"], 1)

                scan_sum(0)
                scan_out(0)

                def step(t, b, n, left):
                    if left > 0:
                        scan_sum(t + 1)
                        scan_out(t + 1)
                    after(pool, s["x_in"], t, 16)
                    after(pool, s["mix_ok"], t, 2)
                    g.tensor_tensor(xx[:, :], xx[:, :], h2[:, :], ALU.add).then_inc(s["x2_ok"], 1)
                    after(pool, s["hm_ok"], t)
                    g.tensor_tensor(h2[:, :], h2[:, :], sh2, ALU.add).then_inc(s["h2_ok"], 1)

                tiles(pool, step)

            @block.vector
            def _(dve):
                v = nc.vector
                dve.wait_ge(s["w_in"], 16)
                v.memset(rw[:, KD * NEXP:], 0.0).then_inc(s["pad_ok"], 1)

                def by_head(ap):
                    return ap.rearrange("p (h n) -> p h n", h=H)

                def wide(ap):
                    return ap.unsqueeze(2).broadcast_to([P, H, N])

                def scan_center(t):
                    after(dve, s["ysum"], t)
                    v.reduce_sum(s8[0][:, :], by_head(ya[:, :]), axis=X_AXIS).then_inc(s["m_ok"], 1)
                    after(dve, s["m_ok"], t)
                    v.tensor_scalar(s8[5][:, :], s8[0][:, :], 1.0 / N, None, ALU.mult).then_inc(s["mean_ok"], 1)
                    after(dve, s["mean_ok"], t)
                    v.tensor_tensor(by_head(yb[:, :]), by_head(ya[:, :]), wide(s8[5][:, :]), ALU.subtract)\
                        .then_inc(s["yc_ok"], 1)

                def scan_variance(t):
                    after(dve, s["sq_ok"], t)
                    v.reduce_sum(s8[1][:, :], by_head(ya[:, :]), axis=X_AXIS).then_inc(s["v_ok"], 1)
                    after(dve, s["v_ok"], t)
                    v.tensor_scalar(s8[2][:, :], s8[1][:, :], 1.0 / N, GN_EPS, ALU.mult, ALU.add).then_inc(s["ve_ok"], 1)

                def scan_scale(t):
                    after(dve, s["sd_ok"], t)
                    v.reciprocal(s8[4][:, :], s8[3][:, :]).then_inc(s["rs_ok"], 1)
                    after(dve, s["rs_ok"], t)
                    v.tensor_tensor(by_head(yb[:, :]), by_head(yb[:, :]), wide(s8[4][:, :]), ALU.mult)\
                        .then_inc(s["yn_ok"], 1)

                def tail(t):
                    for half in range(2):
                        after(dve, s["hT_ps"], t * 2 + half)
                        v.tensor_copy(h2T[:, 4 * half:4 * half + 4, :].rearrange("p k n -> p (k n)"), ps[:, HB[half], :])\
                            .then_inc(s["hT_ok"], 1)
                    after(dve, s["lg_ps"], t)
                    v.tensor_copy(K["logits"][:, bass.ds(t * NEXP, NEXP)], ps[:, TB, 0:NEXP]).then_inc(s["lg_ok"], 1)

                scan_center(0)
                scan_variance(0)
                scan_scale(0)

                def step(t, b, n, left):
                    if not first(t):
                        tail(t - 1)
                    for j in range(KD):
                        after(dve, s["P_ps"], t * KD + j)
                        after(dve, s["G_ok"], t * KD + j)
                        v.tensor_tensor(Ms[j % 2][:, :], Gs[j % 2][:, :], ps[:, PB[j % 2], 0:3 * P], ALU.mult)\
                            .then_inc(s["M_ok"], 1)
                        after(dve, s["M_ok"], t * KD + j)
                        v.reduce_sum(mT[:, j, :], Ms[j % 2][:, :].rearrange("p (b n) -> p n b", b=3), axis=X_AXIS)\
                            .then_inc(s["mg_ok"], 1)
                        if left > 0 and j in (3, 5):
                            (scan_center if j == 3 else scan_variance)(t + 1)
                    if left > 0:
                        scan_scale(t + 1)
                    freed(dve, s["st_h"], t, 16)
                    dve.wait_ge(s["rp_in"], 96 if left == 0 else 48)
                    for i in range(2):
                        after(dve, s["W_ps"], t * 2 + i)
                        if not first(t) and i == 0:
                            freed(dve, s["hT_ps"], t, 2)
                        v.tensor_tensor(h2[:, i * 512:(i + 1) * 512], ga1[:, i * 512:(i + 1) * 512], ps[:, WB[i], :],
                                        ALU.mult).then_inc(s["mix_ok"], 1)
                    after(dve, s["ss_ok"], t)
                    v.tensor_scalar(s1[1], s1[0], 1.0 / D, EPS, ALU.mult, ALU.add).then_inc(s["ms_ok"], 1)
                    after(dve, s["sx_ok"], t)
                    v.reciprocal(s1[3], s1[2]).then_inc(s["rx_ok"], 1)
                    after(dve, s["rx_ok"], t)
                    after(dve, s["x2_ok"], t)
                    v.scalar_tensor_tensor(h2[:, :], xx[:, :], s1[3], g2, ALU.mult, ALU.mult)\
                        .then_inc(s["hm_ok"], 1)
                    if left == 0:
                        tail(t)

                tiles(dve, step)
                dve.wait_ge(s["lg_ok"], NT)

            @block.tensor
            def _(pe):
                def mm(out, lhsT, rhs, start, stop):
                    return nc.tensor.matmul(out, lhsT, rhs, start=start, stop=stop)

                def turn_h2(t):
                    after(pe, s["h2_ok"], t)
                    freed(pe, s["lg_ok"], t)
                    for half in range(2):
                        for k in range(4):
                            c = (4 * half + k) * P
                            ins = nc.tensor.transpose(ps[:, HB[half], k * P:(k + 1) * P], h2[:, c:c + P], ident)
                        ins.then_inc(s["hT_ps"], 1)

                def logits(t):
                    after(pe, s["hT_ok"], t, 2)
                    for k in range(KD):
                        ins = mm(ps[:, TB, 0:RCOLS], h2T[:, k, :], rw[:, k * NEXP:k * NEXP + RCOLS], k == 0, k == KD - 1)
                    ins.then_inc(s["lg_ps"], 1)

                def step(t, b, n, left):
                    def gates(j):
                        if first(t) and j % 2 == 0:
                            pe.wait_ge(wg_in[j // 2], 48)
                        if j >= 3:
                            pe.wait_ge(s["G_ok"], t * KD + j - 2)
                        else:
                            freed(pe, s["G_ok"], t, KD)
                        for br in range(3):
                            c = br * D + j * P
                            for k in range(KD):
                                ins = mm(ps[:, GB[j % 3], br * P:(br + 1) * P], wg[:, k, c:c + P], hT[:, k, :],
                                         k == 0, k == KD - 1)
                        ins.then_inc(s["G_ps"], 1)

                    def project(j):
                        if j >= 2:
                            pe.wait_ge(s["M_ok"], t * KD + j - 1)
                        else:
                            freed(pe, s["M_ok"], t, KD)
                        parts = [(0, [(0, cs[:, 0, :]), (1, cs[:, 1, :])]),
                                 (1, [(2 + i, yT[:, i, :]) for i in range(4)]),
                                 (2, [(6, cs[:, 2, :]), (7, cs[:, 3, :])])]
                        for br, terms in parts:
                            for i, (k, rhs) in enumerate(terms):
                                ins = mm(ps[:, PB[j % 2], br * P:(br + 1) * P], wp[:, k, j * P:(j + 1) * P], rhs,
                                         i == 0, i == len(terms) - 1)
                        ins.then_inc(s["P_ps"], 1)

                    after(pe, s["h_in"], t, 16)
                    gates(0)
                    gates(1)
                    after(pe, s["yf_ok"], t)
                    freed(pe, s["mix_ok"], t, 2)
                    for k in range(4):
                        ins = nc.tensor.transpose(ps[:, WB[1], k * P:(k + 1) * P], ya[:, k * P:(k + 1) * P], ident)
                    ins.then_inc(s["yT_ps"], 1)
                    gates(2)
                    if not first(t):
                        turn_h2(t - 1)
                    gates(3)
                    if not first(t):
                        logits(t - 1)
                    after(pe, s["yT_ok"], t)
                    after(pe, s["cs_in"], t, 16)
                    if first(t):
                        pe.wait_ge(s["wp_in"], 48)
                    for j in range(KD):
                        project(j)
                        if j + 4 < KD:
                            gates(j + 4)
                    if first(t):
                        pe.wait_ge(s["wo_in"], 32)
                        pe.wait_ge(s["pad_ok"], 1)
                    for i in range(2):
                        freed(pe, s["mix_ok"], t, 2)
                        for k in range(KD):
                            if i == 0 and k >= KD - 2:
                                pe.wait_ge(s["mg_ok"], t * KD + k + 1)
                            elif i == 0 and k == 0:
                                pe.wait_ge(s["mg_ok"], t * KD + KD - 2)
                            ins = mm(ps[:, WB[i], :], mT[:, k, :], wo[:, k, i * 512:(i + 1) * 512], k == 0, k == KD - 1)
                        ins.then_inc(s["W_ps"], 1)
                    if left == 0:
                        turn_h2(t)
                        logits(t)

                tiles(pe, step)


def load_expert(e, io, K, x, done):
    i = x % WSLOTS
    e.dma_start(K["wu"][:, i, :, 0:FE], io["exp_w1"][x].rearrange("(k p) n -> p k n", p=P)).then_inc(done, 16)
    e.dma_start(K["wu"][:, i, :, FE:2 * FE], io["exp_w3"][x].rearrange("(k p) n -> p k n", p=P)).then_inc(done, 16)
    e.dma_start(K["wd"][:, i, :, :], io["exp_w2"][x].rearrange("(k p) n -> p k n", p=P)).then_inc(done, 16)


def stage_route(nc, io, scr, K):
    with ExitStack() as ctx:
        def sb(name, shape, dt=F32):
            return ctx.enter_context(nc.sbuf_tensor(name, shape, dt))

        sem = Sems(nc, ctx)
        ps = ctx.enter_context(nc.psum_tensor("r_ps", [P, 3, 512], F32))
        BIG = 1e30
        E, G, M = NEXP, 4, 4
        rc = sb("r_const", [P, ROUTE_COLS])
        cmask = sb("r_up", [P, P])
        ones = sb("r_ones", [P, P])
        zero = sb("r_zero", [NB, P])
        rb = sb("r_rb", [P, E])
        sc, bi, mb, mb2, key, eq, oh, tmp, base = (sb("r_" + n, [P, NT, E]) for n in (
            "sc", "bi", "mb", "mb2", "key", "eq", "oh", "tmp", "base"))
        ohk = [sb(f"r_oh{k}", [P, NT, E]) for k in range(2)]
        pr = sb("r_pr", [P, NT * G, 6])
        gs, gk, gq = (sb("r_" + n, [P, NT, G]) for n in ("gs", "gk", "gq"))
        mx = sb("r_mx", [P, NT])
        g12 = sb("r_g12", [P, 2, NT])
        gsum, grec = sb("r_gsum", [P, NT]), sb("r_grec", [P, NT])
        carry = sb("r_carry", [P, NT + 1, E])
        cmp_ = sb("r_cmp", [P, E, NT])
        nb, ends, pst = sb("r_nb", [P, E]), sb("r_ends", [P, E]), sb("r_pst", [P, E])
        tri = sb("r_tri", [P, E, E])
        bc = sb("r_bc", [1, NB, E])
        be = sb("r_be", [1, NB])
        dst = sb("r_dst", [P, 2, NT])
        srow = sb("r_srow", [NB, P])
        iota4, iota16 = rc[:, 0:4], rc[:, 4:20]
        j128, iotab = rc[:, 20:20 + NT], rc[:, 20 + NT:20 + NT + NB]
        incl = rc[:, 20 + NT + NB:20 + NT + NB + E * E]
        tok = rc[:, 20 + NT + NB + E * E:ROUTE_COLS]

        c_in, sig_ok, step_ok, cnt_ps, ones_ok, zeroed = (sem("r_" + n) for n in (
            "c_in", "sig_ok", "step_ok", "cnt_ps", "ones_ok", "zeroed"))
        w_in = sem("r_w_in")
        scat, s_in, sT, plan_ok, zstored = (sem("r_" + n) for n in ("scat", "s_in", "sT", "plan_ok", "zstored"))

        def wide(ap, n):
            return ap.unsqueeze(2).broadcast_to([P, ap.shape[1], n])

        def over(ap, m):
            return ap.unsqueeze(1).broadcast_to([P, m, ap.shape[1]])

        with nc.Block() as block:
            @block.sync
            def _(sp):
                sp.dma_start(rc[:, :], io["route_consts"]).then_inc(c_in, 16)
                sp.dma_start(cmask[:, :], io["consts"][:, UP, :]).then_inc(c_in, 16)
                sp.dma_start(rb[:, :], io["router_b"].partition_broadcast(P)).then_inc(c_in, 16)
                for e in range(EARLY):
                    load_expert(sp, io, K, e, w_in)
                sp.wait_ge(zeroed, 1)
                sp.dma_start(scr["src"].rearrange("(b p) a -> b (p a)", p=P), zero[:, :]).then_inc(zstored, 16)
                sp.wait_ge(scat, 16 * 2 * NT)
                sp.dma_start(srow[:, :], scr["src"].rearrange("(b p) a -> b (p a)", p=P)).then_inc(s_in, 16)
                sp.wait_ge(s_in, 16)
                sp.wait_ge(w_in, 48 * EARLY)

            @block.scalar
            def _(act):
                nc.scalar.activation(sc[:, :, :].rearrange("p t e -> p (t e)"), K["logits"][:, :], ACT.Sigmoid)\
                    .then_inc(sig_ok, 1)

            @block.gpsimd
            def _(pool):
                nc.gpsimd.memset(zero[:, :], 0.0).then_inc(zeroed, 1)
                nc.gpsimd.memset(ones[:, :], 1.0).then_inc(ones_ok, 1)
                pool.wait_ge(zstored, 16)
                pool.wait_ge(plan_ok, 1)
                for t in range(NT):
                    for k in range(2):
                        pool.indirect_dma_start(scr["src"], bass.IndirectOffsetOnAxis(K["dest"][:, k, t:t + 1], 0),
                                                tok[:, t:t + 1], None).then_inc(scat, 16)
                pool.wait_ge(scat, 16 * 2 * NT)

            @block.tensor
            def _(pe):
                pe.wait_ge(step_ok, ROUTE_OH)
                pe.wait_ge(ones_ok, 1)
                pe.wait_ge(c_in, 48)
                ohv = oh[:, :, :].rearrange("p t e -> p (t e)")
                nc.tensor.matmul(ps[:, 0, 0:NT * E], cmask[:, :], ohv, start=True, stop=True)
                nc.tensor.matmul(ps[:, 1, 0:NT * E], ones[:, :], ohv, start=True, stop=True).then_inc(cnt_ps, 1)
                pe.wait_ge(s_in, 16)
                nc.tensor.transpose(ps[:, 2, 0:NB], srow[:, :], K["ident"][0:NB, 0:NB]).then_inc(sT, 1)

            @block.vector
            def _(dve):
                v = nc.vector
                count = [0]

                def then(ins):
                    count[0] += 1
                    ins.then_inc(step_ok, 1)
                    dve.wait_ge(step_ok, count[0])

                dve.wait_ge(c_in, 48)
                dve.wait_ge(sig_ok, 1)
                then(v.tensor_tensor(bi[:, :, :], sc[:, :, :], over(rb[:, :], NT), ALU.add))
                b4 = bi[:, :, :].rearrange("p t (g m) -> p (t g) m", m=M)
                then(v.tensor_tensor(pr[:, :, 0:3], b4[:, :, 0:3], b4[:, :, 1:4], ALU.add))
                then(v.tensor_tensor(pr[:, :, 3:5], b4[:, :, 0:2], b4[:, :, 2:4], ALU.add))
                then(v.tensor_tensor(pr[:, :, 5:6], b4[:, :, 0:1], b4[:, :, 3:4], ALU.add))
                then(v.reduce_max(gs[:, :, :].rearrange("p t g -> p (t g)"), pr[:, :, :], axis=X_AXIS))

                def first_max(values, iota, scale, eq_, key_, out):
                    n = values.shape[2]
                    then(v.reduce_max(mx[:, :], values, axis=X_AXIS))
                    then(v.tensor_tensor(eq_, values, wide(mx[:, :], n), ALU.is_equal))
                    then(v.scalar_tensor_tensor(key_, eq_, scale, over(iota, NT), ALU.mult, ALU.subtract))
                    then(v.reduce_max(mx[:, :], key_, axis=X_AXIS))
                    then(v.tensor_tensor(out, key_, wide(mx[:, :], n), ALU.is_equal))

                first_max(gs[:, :, :], iota4, 8.0, gq[:, :, :], gk[:, :, :], gs[:, :, :])
                then(v.tensor_scalar(gq[:, :, :], gs[:, :, :], BIG, -BIG, ALU.mult, ALU.add))
                then(v.tensor_tensor(mb[:, :, :].rearrange("p t (g m) -> p (t g) m", m=M), b4,
                                     wide(gq[:, :, :].rearrange("p t g -> p (t g)"), M), ALU.add))
                first_max(mb[:, :, :], iota16, 32.0, eq[:, :, :], key[:, :, :], ohk[0][:, :, :])
                then(v.scalar_tensor_tensor(mb2[:, :, :], ohk[0][:, :, :], -2 * BIG, mb[:, :, :], ALU.mult, ALU.add))
                first_max(mb2[:, :, :], iota16, 32.0, eq[:, :, :], key[:, :, :], ohk[1][:, :, :])
                then(v.tensor_tensor(oh[:, :, :], ohk[0][:, :, :], ohk[1][:, :, :], ALU.add))
                assert count[0] == ROUTE_OH
                then(v.memset(carry[:, 0, :], 0.0))
                dve.wait_ge(cnt_ps, 1)
                for t in range(NT):
                    then(v.tensor_tensor(carry[:, t + 1, :], carry[:, t, :], ps[:, 1, t * E:(t + 1) * E], ALU.add))
                then(v.tensor_tensor(cmp_[:, :, :], wide(carry[:, NT, :], NT), over(j128, E), ALU.is_gt))
                then(v.reduce_sum(nb[:, :], cmp_[:, :, :], axis=X_AXIS))
                then(v.tensor_tensor(tri[:, :, :], over(nb[:, :], E), incl.rearrange("p (a b) -> p a b", a=E), ALU.mult))
                then(v.reduce_sum(ends[:, :], tri[:, :, :], axis=X_AXIS))
                then(v.tensor_tensor(pst[:, :], ends[:, :], nb[:, :], ALU.subtract))
                then(v.tensor_scalar(pst[:, :], pst[:, :], float(P), None, ALU.mult))
                then(v.tensor_tensor(base[:, :, :], carry[:, 0:NT, :],
                                     ps[:, 0, 0:NT * E].rearrange("p (t e) -> p t e", t=NT), ALU.add))
                then(v.tensor_tensor(base[:, :, :], base[:, :, :], over(pst[:, :], NT), ALU.add))
                for k in range(2):
                    then(v.tensor_tensor(tmp[:, :, :], base[:, :, :], ohk[k][:, :, :], ALU.mult))
                    then(v.reduce_sum(dst[:, k, :], tmp[:, :, :], axis=X_AXIS))
                v.tensor_copy(K["dest"][:, :, :], dst[:, :, :]).then_inc(plan_ok, 1)
                for k in range(2):
                    then(v.tensor_tensor(tmp[:, :, :], sc[:, :, :], ohk[k][:, :, :], ALU.mult))
                    then(v.reduce_sum(g12[:, k, :], tmp[:, :, :], axis=X_AXIS))
                then(v.tensor_tensor(gsum[:, :], g12[:, 0, :], g12[:, 1, :], ALU.add))
                then(v.reciprocal(grec[:, :], gsum[:, :]))
                then(v.tensor_tensor(K["gate"][:, :, :], g12[:, :, :], over(grec[:, :], 2), ALU.mult))
                then(v.tensor_tensor(bc[:, :, :], iotab[0:1, :].unsqueeze(2).broadcast_to([1, NB, E]),
                                     ends[0:1, :].unsqueeze(1).broadcast_to([1, NB, E]), ALU.is_ge))
                then(v.reduce_sum(be[:, :], bc[:, :, :], axis=X_AXIS))
                then(v.tensor_scalar(be[:, :], be[:, :], float(E - 1), None, ALU.min))
                then(v.tensor_scalar(K["plan"][:, 0, 0:NB], be[:, :], 1.0, None, ALU.add))
                then(v.tensor_scalar(bc[:, :, 0], be[:, :], float(E // 4), None, ALU.is_ge))
                for i in (2, 3):
                    then(v.tensor_scalar(bc[:, :, 1], be[:, :], float(i * E // 4), None, ALU.is_ge))
                    then(v.tensor_tensor(bc[:, :, 0], bc[:, :, 0], bc[:, :, 1], ALU.add))
                then(v.scalar_tensor_tensor(K["plan"][:, 1, 0:NB], bc[:, :, 0], -float(WSLOTS), be[:, :], ALU.mult, ALU.add))
                then(v.tensor_scalar(K["plan"][:, 2, 0:E], ends[0:1, :], 1.0, None, ALU.add))
                dve.wait_ge(sT, 1)
                v.tensor_copy(K["src"][:, :], ps[:, 2, 0:NB]).then_inc(plan_ok, 1)
                dve.wait_ge(plan_ok, 2)


def stage_experts(nc, io, scr, K):
    with ExitStack() as ctx:
        def sb(name, shape):
            return ctx.enter_context(nc.sbuf_tensor(name, shape, F32))

        sem = Sems(nc, ctx)
        ps = ctx.enter_context(nc.psum_tensor("e_ps", [P, 8, 512], F32))
        ident = K["ident"][:, :]
        S = 4
        wu, wd = K["wu"], K["wd"]
        X = [sb(f"e_x{i}", [P, D]) for i in range(S)]
        xT = [sb(f"e_xT{i}", [P, KD, P]) for i in range(2)]
        sg = sb("e_sg", [P, FE])
        sl = sb("e_sl", [P, FE])
        av = sb("e_av", [P, FE])
        aT = sb("e_aT", [P, 2, P])
        yo = [sb(f"e_yo{i}", [P, D]) for i in range(2)]
        w_in, x_in = [sem(f"e_w_in{i}") for i in range(WSLOTS)], [sem(f"e_x_in{i}") for i in range(S)]
        w_ok = sem("e_w_ok")
        y_st = [sem(f"e_y_st{i}") for i in range(2)]
        x2_in = sem("e_x2_in")
        xT_ps, xT_ok, up_ps, sg_ok, sl_ok, a_ok, aT_ps, aT_ok, y_ps, y_ok = (sem("e_" + n) for n in (
            "xT_ps", "xT_ok", "up_ps", "sg_ok", "sl_ok", "a_ok", "aT_ps", "aT_ok", "y_ps", "y_ok"))
        TB, UB, AB, YB = (0, 1), (2, 3), 4, (5, 6)

        def blocks(e, step):
            for i in range(S):
                step(i, i, 0, False)
            with e.Fori(1, NB // S) as j:
                for i in range(S):
                    step(j * S + i, i, j, False)
            step(NB - 1, 0, NB // S, True)


        with nc.Block() as block:
            @block.sync
            def _(sp):
                for e in range(NEXP + 1):
                    if e < NEXP:
                        i = e % WSLOTS
                        if e >= WSLOTS:
                            ended = sp.value_load(K["plan"][0:1, 2, e - WSLOTS:e - WSLOTS + 1], min_val=1, max_val=NB + 1)
                            sp.wait_ge(y_ps, ended)
                        if e >= EARLY:
                            load_expert(sp, io, K, e, w_in[i])
                    if e >= 1:
                        if e - 1 >= EARLY:
                            uses = (e - 1) // WSLOTS + int((e - 1) % WSLOTS >= EARLY)
                            sp.wait_ge(w_in[(e - 1) % WSLOTS], 48 * uses)
                        sp.nop().then_inc(w_ok, 1)
                    if e == WSLOTS:
                        sp.dma_start(K["fg"][:, :], io["final_g"].partition_broadcast(P)).then_inc(x2_in, 16)
                    elif e > WSLOTS:
                        for t in range(2 * (e - WSLOTS - 1), min(2 * (e - WSLOTS), NT)):
                            sp.dma_start(K["x2"][:, t, :], scr["x2"][t]).then_inc(x2_in, 16)
                sp.wait_ge(x2_in, 16 * (NT + 1))

            @block.gpsimd
            def _(pool):
                for b in range(NB):
                    if b >= S:
                        pool.wait_ge(xT_ps, b - S + 1)
                    pool.indirect_dma_start(X[b % S][:, :], None, scr["h2"].rearrange("t p n -> (t p) n"),
                                            bass.IndirectOffsetOnAxis(K["src"][:, b:b + 1], 0)).then_inc(x_in[b % S], 16)

            @block.scalar
            def _(act):
                a = nc.scalar.activation

                def rows(b, i):
                    after(act, xT_ps, b)
                    a(xT[i % 2][:, 0:4, :].rearrange("p k n -> p (k n)"), ps[:, TB[0], :], ACT.Copy).then_inc(xT_ok, 1)

                rows(0, 0)

                def finish(b, i, n):
                    after(act, y_ps, b + 1)
                    freed(act, y_st[i % 2], n * 2 + i // 2, 16)
                    a(yo[i % 2][:, 0:512], ps[:, YB[0], :], ACT.Copy).then_inc(y_ok, 1)
                    after(act, y_ok, b, 2)
                    act.dma_start(scr["yr"][bass.ds(b, 1)].rearrange("a p n -> (a p) n"), yo[i % 2][:, :])\
                        .then_inc(y_st[i % 2], 16)

                def step(b, i, n, last):
                    after(act, up_ps, b)
                    freed(act, sl_ok, b)
                    a(sg[:, :], ps[:, UB[i % 2], 0:FE], ACT.Sigmoid).then_inc(sg_ok, 1)
                    if not last:
                        rows(b + 1, i + 1)
                    if not (isinstance(b, int) and b == 0):
                        finish(b - 1, i - 1, n)

                blocks(act, step)
                finish(NB - 1, 0, NB // S)
                act.wait_ge(y_st[0], 16 * 25)
                act.wait_ge(y_st[1], 16 * 24)

            @block.vector
            def _(dve):
                v = nc.vector

                def rows(b, i):
                    after(dve, xT_ps, b)
                    v.tensor_copy(xT[i % 2][:, 4:8, :].rearrange("p k n -> p (k n)"), ps[:, TB[1], :]).then_inc(xT_ok, 1)

                rows(0, 0)

                def activated(b):
                    after(dve, aT_ps, b)
                    freed(dve, y_ps, b + 1)
                    v.tensor_copy(aT[:, :, :].rearrange("p k n -> p (k n)"), ps[:, AB, 0:2 * P]).then_inc(aT_ok, 1)

                def finish(b, i, n):
                    after(dve, y_ps, b + 1)
                    freed(dve, y_st[i % 2], n * 2 + i // 2, 16)
                    v.tensor_copy(yo[i % 2][:, 512:1024], ps[:, YB[1], :]).then_inc(y_ok, 1)

                def step(b, i, n, last):
                    first = isinstance(b, int) and b == 0
                    if not first:
                        activated(b - 1)
                    after(dve, sg_ok, b)
                    v.tensor_tensor(sl[:, :], sg[:, :], ps[:, UB[i % 2], 0:FE], ALU.mult).then_inc(sl_ok, 1)
                    after(dve, sl_ok, b)
                    freed(dve, aT_ps, b)
                    v.tensor_tensor(av[:, :], sl[:, :], ps[:, UB[i % 2], FE:2 * FE], ALU.mult).then_inc(a_ok, 1)
                    if not last:
                        rows(b + 1, i + 1)
                    if not first:
                        finish(b - 1, i - 1, n)

                blocks(dve, step)
                activated(NB - 1)
                finish(NB - 1, 0, NB // S)

            @block.tensor
            def _(pe):
                def mm(out, lhsT, rhs, start, stop):
                    return nc.tensor.matmul(out, lhsT, rhs, start=start, stop=stop)

                def rows(b, i, n):
                    after(pe, x_in[i], n, 16)
                    freed(pe, xT_ok, b, 2)
                    for k in range(KD):
                        ins = nc.tensor.transpose(ps[:, TB[k // 4], (k % 4) * P:(k % 4 + 1) * P],
                                                  X[i][:, k * P:(k + 1) * P], ident)
                    ins.then_inc(xT_ps, 1)

                pe.nop().then_inc(y_ps, 1)
                rows(0, 0, 0)

                def activated(b):
                    after(pe, a_ok, b)
                    freed(pe, aT_ok, b)
                    for k in range(2):
                        ins = nc.tensor.transpose(ps[:, AB, k * P:(k + 1) * P], av[:, k * P:(k + 1) * P], ident)
                    ins.then_inc(aT_ps, 1)

                def down(b, slot):
                    after(pe, aT_ok, b)
                    freed(pe, y_ok, b, 2)
                    for half in range(2):
                        for k in range(2):
                            ins = mm(ps[:, YB[half], :], aT[:, k, :], wd[:, bass.ds(slot, 1), k, half * 512:(half + 1) * 512],
                                     k == 0, k == 1)
                    ins.then_inc(y_ps, 1)

                def slot_of(b):
                    return pe.value_load(K["plan"][0:1, 1, bass.ds(b, 1)], min_val=0, max_val=WSLOTS - 1)

                def step(b, i, n, last):
                    first = isinstance(b, int) and b == 0
                    place = pe.value_load(K["plan"][0:1, 0, bass.ds(b, 1)], min_val=1, max_val=NEXP)
                    slot = slot_of(b)
                    before = None if first else slot_of(b - 1)
                    pe.wait_ge(w_ok, place)
                    after(pe, xT_ok, b, 2)
                    freed(pe, a_ok, b)
                    for k in range(KD):
                        ins = mm(ps[:, UB[i % 2], :], xT[i % 2][:, k, :], wu[:, bass.ds(slot, 1), k, :], k == 0, k == KD - 1)
                    ins.then_inc(up_ps, 1)
                    if not first:
                        activated(b - 1)
                    if not last:
                        rows(b + 1, (i + 1) % S, n if i < S - 1 else n + 1)
                    if not first:
                        down(b - 1, before)

                blocks(pe, step)
                activated(NB - 1)
                down(NB - 1, slot_of(NB - 1))


def stage_combine(nc, io, scr, K):
    with ExitStack() as ctx:
        def sb(name, shape):
            return ctx.enter_context(nc.sbuf_tensor(name, shape, F32))

        sem = Sems(nc, ctx)
        r = [[sb(f"f_r{k}{i}", [P, D]) for i in range(2)] for k in range(2)]
        x, fg = K["x2"], K["fg"]
        ga2 = sb("f_ga2", [P, 2, D])
        p_in = sem("f_p_in")
        g1 = [sb(f"f_g{i}", [P, 2]) for i in range(2)]
        acc, x3 = ([sb(f"f_{n}{i}", [P, D]) for i in range(2)] for n in ("acc", "x3"))
        acc2, acc3, sq = (sb("f_" + n, [P, D]) for n in ("acc2", "acc3", "sq"))
        yo = [sb(f"f_yo{i}", [P, D]) for i in range(2)]
        ss, ms, sd, rs = (sb("f_" + n, [P, 1]) for n in ("ss", "ms", "sd", "rs"))
        r_in, y_st = ([sem(f"f_{n}{i}") for i in range(2)] for n in ("r_in", "y_st"))
        g_ok, a_ok, b_ok, c_ok, x3_ok, ss_ok, ms_ok, sd_ok, rs_ok, y_ok = (sem("f_" + n) for n in (
            "g_ok", "a_ok", "b_ok", "c_ok", "x3_ok", "ss_ok", "ms_ok", "sd_ok", "rs_ok", "y_ok"))

        def tile_of(ap, t):
            return ap[bass.ds(t, 1)].rearrange("a p n -> (a p) n")

        def tile_rows(sbuf, t):
            return sbuf[:, bass.ds(t, 1), :].rearrange("p a n -> p (a n)")

        with nc.Block() as block:
            @block.sync
            def _(sp):
                for i in range(2):
                    sp.nop().then_inc(y_st[i], 16)
                for v in range(2):
                    sp.dma_start(ga2[:, v, :], scr["mod"][v, 5 * D:6 * D].partition_broadcast(P)).then_inc(p_in, 16)

                def step(t, b, n, left):
                    after(sp, y_ok, t)
                    sp.dma_start(tile_of(io["y_all"], t), yo[b][:, :]).then_inc(y_st[b], 16)

                over_tiles(sp, step)
                sp.wait_ge(y_st[0], 16 * 10)
                sp.wait_ge(y_st[1], 16 * 9)

            @block.gpsimd
            def _(pool):
                rows = scr["yr"].rearrange("b p n -> (b p) n")
                for t in range(NT):
                    if t >= 2:
                        pool.wait_ge(b_ok, t - 1)
                    for k in range(2):
                        pool.indirect_dma_start(r[k][t % 2][:, :], None, rows,
                                                bass.IndirectOffsetOnAxis(K["dest"][:, k, t:t + 1], 0))\
                            .then_inc(r_in[t % 2], 16)

            @block.scalar
            def _(act):
                def first_row(t, b, n):
                    after(act, r_in[b], n, 32)
                    after(act, g_ok, t)
                    if not (isinstance(t, int) and t < 2):
                        act.wait_ge(b_ok, t - 1)
                    nc.scalar.activation(acc[b][:, :], r[0][b][:, :], ACT.Copy, scale=g1[b][:, 0:1]).then_inc(a_ok, 1)

                def root(t):
                    after(act, ms_ok, t)
                    nc.scalar.activation(sd[:, :], ms[:, :], ACT.Sqrt).then_inc(sd_ok, 1)

                first_row(0, 0, 0)

                def step(t, b, n, left):
                    if left > 0:
                        first_row(t + 1, 1 - b, n + b)
                    if not (isinstance(t, int) and t == 0):
                        root(t - 1)
                    after(act, x3_ok, t)
                    nc.scalar.activation(sq[:, :], x3[b][:, :], ACT.Square, accum_out=ss[:, :]).then_inc(ss_ok, 1)

                over_tiles(act, step)
                root(NT - 1)

            @block.vector
            def _(dve):
                v = nc.vector
                dve.wait_ge(p_in, 32)

                def gates(t, b):
                    if not (isinstance(t, int) and t < 2):
                        dve.wait_ge(a_ok, t - 1)
                        dve.wait_ge(b_ok, t - 1)
                    v.tensor_copy(g1[b][:, :], K["gate"][:, :, bass.ds(t, 1)].rearrange("p k a -> p (k a)"))\
                        .then_inc(g_ok, 1)

                def mean_square(t):
                    after(dve, ss_ok, t)
                    v.tensor_scalar(ms[:, :], ss[:, :], 1.0 / D, EPS, ALU.mult, ALU.add).then_inc(ms_ok, 1)

                def normalise(t, b, n):
                    after(dve, sd_ok, t)
                    v.reciprocal(rs[:, :], sd[:, :]).then_inc(rs_ok, 1)
                    after(dve, rs_ok, t)
                    after(dve, y_st[b], n, 16)
                    v.scalar_tensor_tensor(yo[b][:, :], x3[b][:, :], rs[:, :], fg[:, :], ALU.mult, ALU.mult)\
                        .then_inc(y_ok, 1)

                gates(0, 0)

                def step(t, b, n, left):
                    first = isinstance(t, int) and t == 0
                    if left > 0:
                        gates(t + 1, 1 - b)
                    if not first:
                        mean_square(t - 1)
                    after(dve, g_ok, t)
                    after(dve, a_ok, t)
                    v.scalar_tensor_tensor(acc2[:, :], r[1][b][:, :], g1[b][:, 1:2], acc[b][:, :], ALU.mult, ALU.add)\
                        .then_inc(b_ok, 1)
                    after(dve, b_ok, t)
                    v.tensor_tensor(acc3[:, :], acc2[:, :], ga2[:, int(left == 0), :], ALU.mult).then_inc(c_ok, 1)
                    after(dve, c_ok, t)
                    v.tensor_tensor(x3[b][:, :], acc3[:, :], tile_rows(x, t), ALU.add).then_inc(x3_ok, 1)
                    if not first:
                        normalise(t - 1, 1 - b, n - 1 + b)

                over_tiles(dve, step)
                mean_square(NT - 1)
                normalise(NT - 1, 0, NT // 2)


def program(nc, io, scr):
    with ExitStack() as ctx:
        K = {"logits": ctx.enter_context(nc.sbuf_tensor("logits", [P, NT * NEXP], F32)),
             "ident": ctx.enter_context(nc.sbuf_tensor("ident", [P, P], F32)),
             "pt": ctx.enter_context(nc.sbuf_tensor("pt", [P, 118], F32)),
             "gs": ctx.enter_context(nc.sbuf_tensor("gs", [P, 2, 2, KD], F32))}
        stage_modulation(nc, io, scr, K)
        stage_tokens(nc, io, scr, K)
        stage_scan(nc, io, scr, K)
        stage_merge(nc, io, scr, K)
        K["dest"] = ctx.enter_context(nc.sbuf_tensor("dest", [P, 2, NT], U32))
        K["src"] = ctx.enter_context(nc.sbuf_tensor("src", [P, NB], U32))
        K["gate"] = ctx.enter_context(nc.sbuf_tensor("gate", [P, 2, NT], F32))
        K["plan"] = ctx.enter_context(nc.sbuf_tensor("plan", [1, 3, NB], I32))
        K["x2"] = ctx.enter_context(nc.sbuf_tensor("x2_all", [P, NT, D], F32))
        K["fg"] = ctx.enter_context(nc.sbuf_tensor("final_rows", [P, D], F32))
        with ExitStack() as weights:
            K["wu"] = weights.enter_context(nc.sbuf_tensor("expert_up", [P, WSLOTS, KD, 2 * FE], F32))
            K["wd"] = weights.enter_context(nc.sbuf_tensor("expert_down", [P, WSLOTS, 2, D], F32))
            stage_route(nc, io, scr, K)
            stage_experts(nc, io, scr, K)
        stage_combine(nc, io, scr, K)


SCRATCH = {"mod": (2, 6 * D), "h": (NT, P, D), "cs": (NT, P, 4 * P), "A": (NT, P, 3 * W), "D0": (NT, P, 3 * W),
           "D1": (NT, P, 3 * W), "O": (NT, P, 2 * W), "Y0": (NT, P, W),
           "Y1": (NT, P, W), "rows": (2, 3, D), "x2": (NT, P, D), "h2": (NT, P, D),
           "src": (NB * P, 1), "yr": (NB, P, D)}
NAMES = ["s_" + n for n in SCRATCH] + ["state_new", "y_all"]


def kernel(**inputs):
    import numpy as _np
    import concourse.bacc as _bacc
    from concourse import mybir as _mybir
    from concourse.bass_utils import run_bass_kernel_spmd as _run

    f = {n: _np.asarray(a) for n, a in inputs.items()}
    a = {
        "x_all": _np.concatenate([f["x_sample"][0], f["x_prompt"][0]]).reshape(NT, P, D),
        "c_all": _np.stack([f["c"][0], f["c_ctx"]]),
        "consts": shape_constants(),
        "route_consts": route_constants(),
        "state_T": f["state_rwkv"][0, 0].reshape(2, 4, 2, N, N).transpose(0, 2, 4, 1, 3).reshape(2, P, 4, N),
        "rwkv_w2": f["rwkv_w2"][0].reshape(P, W),
        "rwkv_a2": f["rwkv_a2"][0].reshape(P, W),
        "rwkv_r_k": f["rwkv_r_k"][0].reshape(W),
        "sgu_wsT": f["sgu_ws"][0].transpose(2, 0, 1),
        "final_g": f["final_g"], "router_w": f["router_w"], "router_b": f["router_b"],
    }
    for n in ("norm1_g", "norm2_g", "ada_w", "ada_b", "w_in", "conv_w", "rwkv_w0", "rwkv_a0", "rwkv_g2", "rwkv_k_k",
              "rwkv_k_a", "rwkv_lnx_w", "rwkv_lnx_b", "sgu_ln_g", "sgu_ln_b", "sgu_bs", "proj_conv", "proj_rwkv",
              "proj_sgu", "w_out", "exp_w1", "exp_w3", "exp_w2"):
        a[n] = f[n][0]
    nc = _bacc.Bacc("TRN2", target_bir_lowering=False, num_devices=1)
    io, arrays = {}, {}
    for n, v in a.items():
        arrays["in_" + n] = _np.ascontiguousarray(v)
        io[n] = nc.dram_tensor("in_" + n, v.shape, _mybir.dt.float32, kind="ExternalInput").ap()
    scr = {n: nc.dram_tensor("s_" + n, shape, _mybir.dt.float32, kind="Internal").ap() for n, shape in SCRATCH.items()}
    for n, shape in (("y_all", (NT, P, D)), ("state_new", (2, P, 4, N))):
        io[n] = nc.dram_tensor(n, shape, _mybir.dt.float32, kind="ExternalOutput").ap()
    program(nc, io, scr)
    r = _run(nc, [arrays], core_ids=[0]).results[0]
    y = r["y_all"].reshape(NT * P, D)
    state = r["state_new"].reshape(2, 2, N, 4, N).transpose(0, 3, 1, 4, 2).reshape(1, 1, 2, H, N, N)
    return y[None, LAT * P:].copy(), y[None, :LAT * P].copy(), _np.ascontiguousarray(state)
```
